# Optimizing a Trainium2 kernel written in Bass

```python
import jax, jax.numpy as jnp
from jax import lax
import numpy as np

D_MODEL = 1024
BATCH = 1
SEQ = 256
DEPTH = 2

CHUNK = 64
Q_BLOCK = 128
N_A_LAYERS = DEPTH // 2
N_B_LAYERS = DEPTH - N_A_LAYERS
CONV_WIDTH = 31
D_FF = 4 * D_MODEL
N_HEADS = 8
QK_NOPE_DIM = 128
QK_ROPE_DIM = 64
QK_HEAD_DIM = QK_NOPE_DIM + QK_ROPE_DIM
V_HEAD_DIM = 128
Q_LORA_RANK = 384
KV_LORA_RANK = 256
ROPE_BASE = 10000.0
RMS_EPS = 1e-6
LN_EPS = 1e-5


def rms_norm(x, g):
    xf = x.astype(jnp.float32)
    y = xf * lax.rsqrt(jnp.mean(xf * xf, axis=-1, keepdims=True) + RMS_EPS)
    return (y * g.astype(jnp.float32)).astype(x.dtype)

def layer_norm(x, g, b):
    xf = x.astype(jnp.float32)
    mu = jnp.mean(xf, axis=-1, keepdims=True)
    xc = xf - mu
    var = jnp.mean(xc * xc, axis=-1, keepdims=True)
    y = xc * lax.rsqrt(var + LN_EPS) * g.astype(jnp.float32) + b.astype(jnp.float32)
    return y.astype(x.dtype)

def rope_tables(seq):
    inv = 1.0 / (ROPE_BASE ** (jnp.arange(0, QK_ROPE_DIM, 2, dtype=jnp.float32) / QK_ROPE_DIM))
    pos = jnp.arange(seq, dtype=jnp.float32)
    ang = pos[:, None] * inv[None, :]
    return jnp.cos(ang), jnp.sin(ang)

def apply_rope(x, cos, sin):
    xf = x.astype(jnp.float32)
    half = QK_ROPE_DIM // 2
    x1, x2 = xf[..., :half], xf[..., half:]
    out = jnp.concatenate([x1 * cos - x2 * sin, x1 * sin + x2 * cos], axis=-1)
    return out.astype(x.dtype)

def conformer_conv(h, w_pw1, b_pw1, w_dw, b_dw, ln_g, ln_b, w_pw2, b_pw2):
    u = h @ w_pw1 + b_pw1
    a, gate = jnp.split(u, 2, axis=-1)
    u = a * jax.nn.sigmoid(gate)
    u = jnp.pad(u, ((0, 0), (CONV_WIDTH - 1, 0), (0, 0)))
    u = lax.conv_general_dilated(u, w_dw[:, None, :], window_strides=(1,), padding='VALID',
                                 dimension_numbers=('NWC', 'WIO', 'NWC'),
                                 feature_group_count=D_MODEL) + b_dw
    u = jax.nn.silu(layer_norm(u, ln_g, ln_b))
    return u @ w_pw2 + b_pw2

def squared_relu_mlp(h, w1, w2):
    return jnp.square(jax.nn.relu(h @ w1)) @ w2

def mla_shared_kv(h, kv_in_g, w_dkv, kv_norm_g, w_kr, w_uk, w_uv, cos, sin):
    b, s, _ = h.shape
    hn = rms_norm(h, kv_in_g)
    c_kv = rms_norm(hn @ w_dkv, kv_norm_g)
    k_rope = apply_rope(hn @ w_kr, cos, sin)
    k_nope = (c_kv @ w_uk).reshape(b, s, N_HEADS, QK_NOPE_DIM)
    v = (c_kv @ w_uv).reshape(b, s, N_HEADS, V_HEAD_DIM)
    return k_nope, k_rope, v

def mla_attention(hn, w_dq, q_norm_g, w_uq, w_o, k_nope, k_rope, v, cos, sin):
    b, s, _ = hn.shape
    q = (rms_norm(hn @ w_dq, q_norm_g) @ w_uq).reshape(b, s, N_HEADS, QK_HEAD_DIM)
    q_nope = q[..., :QK_NOPE_DIM]
    q_rope = apply_rope(q[..., QK_NOPE_DIM:], cos[:, None, :], sin[:, None, :])
    scale = QK_HEAD_DIM ** -0.5
    key_chunk = jnp.arange(s) // CHUNK

    def block(i):
        start = i * Q_BLOCK
        qn = lax.dynamic_slice_in_dim(q_nope, start, Q_BLOCK, axis=1)
        qr = lax.dynamic_slice_in_dim(q_rope, start, Q_BLOCK, axis=1)
        sc = (jnp.einsum('bqhd,bkhd->bhqk', qn, k_nope, preferred_element_type=jnp.float32)
              + jnp.einsum('bqhr,bkr->bhqk', qr, k_rope, preferred_element_type=jnp.float32)) * scale
        q_chunk = (start + jnp.arange(Q_BLOCK)) // CHUNK
        mask = key_chunk[None, :] <= q_chunk[:, None]
        sc = jnp.where(mask[None, None], sc, -jnp.inf)
        p = jax.nn.softmax(sc, axis=-1).astype(v.dtype)
        return jnp.einsum('bhqk,bkhd->bqhd', p, v)

    o = lax.map(block, jnp.arange(s // Q_BLOCK))
    o = jnp.transpose(o, (1, 0, 2, 3, 4)).reshape(b, s, N_HEADS * V_HEAD_DIM)
    return o @ w_o

def first_inputs(seed: int = 0) -> dict:
    key = jax.random.key(seed)
    ks = jax.random.split(key, 40)
    f32 = jnp.float32

    def nrm(k, shape, fan_in):
        return jax.random.normal(k, shape, f32) * (fan_in ** -0.5)

    def gain(k, shape):
        return 1.0 + 0.1 * jax.random.normal(k, shape, f32)

    def bias(k, shape):
        return 0.02 * jax.random.normal(k, shape, f32)

    D = D_MODEL
    return {
        "x": jax.random.normal(ks[0], (BATCH, SEQ, D), f32),
        "mix_pre_g": gain(ks[1], (DEPTH, D)),
        "mix_post_g": gain(ks[2], (DEPTH, D)),
        "ffn_pre_g": gain(ks[3], (DEPTH, D)),
        "ffn_post_g": gain(ks[4], (DEPTH, D)),
        "w_ff1": nrm(ks[5], (DEPTH, D, D_FF), D),
        "w_ff2": nrm(ks[6], (DEPTH, D_FF, D), D_FF),
        "conv_w_pw1": nrm(ks[7], (N_A_LAYERS, D, 2 * D), D),
        "conv_b_pw1": bias(ks[8], (N_A_LAYERS, 2 * D)),
        "conv_w_dw": nrm(ks[9], (N_A_LAYERS, CONV_WIDTH, D), CONV_WIDTH),
        "conv_b_dw": bias(ks[10], (N_A_LAYERS, D)),
        "conv_ln_g": gain(ks[11], (N_A_LAYERS, D)),
        "conv_ln_b": bias(ks[12], (N_A_LAYERS, D)),
        "conv_w_pw2": nrm(ks[13], (N_A_LAYERS, D, D), D),
        "conv_b_pw2": bias(ks[14], (N_A_LAYERS, D)),
        "mla_w_dq": nrm(ks[15], (N_B_LAYERS, D, Q_LORA_RANK), D),
        "mla_q_norm_g": gain(ks[16], (N_B_LAYERS, Q_LORA_RANK)),
        "mla_w_uq": nrm(ks[17], (N_B_LAYERS, Q_LORA_RANK, N_HEADS * QK_HEAD_DIM), Q_LORA_RANK),
        "mla_w_o": nrm(ks[18], (N_B_LAYERS, N_HEADS * V_HEAD_DIM, D), N_HEADS * V_HEAD_DIM),
        "kv_in_g": gain(ks[19], (D,)),
        "kv_w_dkv": nrm(ks[20], (D, KV_LORA_RANK), D),
        "kv_norm_g": gain(ks[21], (KV_LORA_RANK,)),
        "kv_w_kr": nrm(ks[22], (D, QK_ROPE_DIM), D),
        "kv_w_uk": nrm(ks[23], (KV_LORA_RANK, N_HEADS * QK_NOPE_DIM), KV_LORA_RANK),
        "kv_w_uv": nrm(ks[24], (KV_LORA_RANK, N_HEADS * V_HEAD_DIM), KV_LORA_RANK),
    }

def first_block(x, mix_pre_g, mix_post_g, ffn_pre_g, ffn_post_g, w_ff1, w_ff2,
              conv_w_pw1, conv_b_pw1, conv_w_dw, conv_b_dw, conv_ln_g, conv_ln_b,
              conv_w_pw2, conv_b_pw2, mla_w_dq, mla_q_norm_g, mla_w_uq, mla_w_o,
              kv_in_g, kv_w_dkv, kv_norm_g, kv_w_kr, kv_w_uk, kv_w_uv):
    cos, sin = rope_tables(x.shape[1])
    h = x
    k_nope = k_rope = v = None
    for layer in range(DEPTH):
        if layer == N_A_LAYERS:
            k_nope, k_rope, v = mla_shared_kv(h, kv_in_g, kv_w_dkv, kv_norm_g, kv_w_kr,
                                              kv_w_uk, kv_w_uv, cos, sin)
        hn = rms_norm(h, mix_pre_g[layer])
        if layer < N_A_LAYERS:
            a = layer
            m = conformer_conv(hn, conv_w_pw1[a], conv_b_pw1[a], conv_w_dw[a], conv_b_dw[a],
                               conv_ln_g[a], conv_ln_b[a], conv_w_pw2[a], conv_b_pw2[a])
        else:
            bl = layer - N_A_LAYERS
            m = mla_attention(hn, mla_w_dq[bl], mla_q_norm_g[bl], mla_w_uq[bl], mla_w_o[bl],
                              k_nope, k_rope, v, cos, sin)
        h = h + rms_norm(m, mix_post_g[layer])
        f = squared_relu_mlp(rms_norm(h, ffn_pre_g[layer]), w_ff1[layer], w_ff2[layer])
        h = h + rms_norm(f, ffn_post_g[layer])
    return h


HEAD_DIM = 64
ROPE_DIM = HEAD_DIM // 4
ROPE_THETA = 500000.0
N_FOX_HEADS = 8
N_DSA_HEADS = 8
N_MOBA_HEADS = D_MODEL // HEAD_DIM
DSA_KV_RANK = 128
DSA_NOPE_DIM = HEAD_DIM - ROPE_DIM
DSA_V_DIM = HEAD_DIM
N_IDX_HEADS = 4
IDX_DIM = 64
DSA_TOPK_MAX = 256
MOBA_BLOCK = 256
MOBA_TOPB_MAX = 3
D_FF_2 = 2816
CONV_WIDTH_2 = 3
MOBA_Q_CHUNK = 16
EPS = 1e-6
N_EVEN = (DEPTH + 1) // 2
N_ODD = DEPTH // 2
FOX_WIDTH = N_FOX_HEADS * HEAD_DIM
DSA_WIDTH = N_DSA_HEADS * HEAD_DIM
EVEN_SIZES = (FOX_WIDTH, FOX_WIDTH, FOX_WIDTH, N_FOX_HEADS, DSA_WIDTH, DSA_KV_RANK, ROPE_DIM,
              N_IDX_HEADS * IDX_DIM, IDX_DIM, N_IDX_HEADS)
EVEN_IN_DIM = sum(EVEN_SIZES)
ODD_IN_DIM = 3 * N_MOBA_HEADS * HEAD_DIM


def rmsnorm(x, g):
    xf = x.astype(jnp.float32)
    y = xf * lax.rsqrt(jnp.mean(xf * xf, axis=-1, keepdims=True) + EPS) * g.astype(jnp.float32)
    return y.astype(x.dtype)

def rope_tables_2(positions):
    inv_freq = ROPE_THETA ** (-jnp.arange(0, ROPE_DIM, 2, dtype=jnp.float32) / ROPE_DIM)
    ang = positions.astype(jnp.float32)[..., None] * inv_freq
    return jnp.cos(ang), jnp.sin(ang)

def apply_partial_rope(t, cos, sin):
    half = ROPE_DIM // 2
    tf = t[..., :ROPE_DIM].astype(jnp.float32)
    t1, t2 = tf[..., :half], tf[..., half:]
    c, s = cos[:, :, None, :], sin[:, :, None, :]
    rot = jnp.concatenate([t1 * c - t2 * s, t2 * c + t1 * s], axis=-1).astype(t.dtype)
    return jnp.concatenate([rot, t[..., ROPE_DIM:]], axis=-1)

def to_blocks(a, nb, blk):
    return jnp.swapaxes(a.reshape(a.shape[0], nb, blk, *a.shape[2:]), 0, 1)

def from_blocks(a):
    a = jnp.swapaxes(a, 0, 1)
    return a.reshape(a.shape[0], a.shape[1] * a.shape[2], *a.shape[3:])

def fox_attention(q, k, v, log_f):
    B, S, H, D = q.shape
    nqb = S // Q_BLOCK
    c = jnp.cumsum(log_f, axis=1)
    c_k = jnp.swapaxes(c, 1, 2)
    key_pos = jnp.arange(S)
    scale = D ** -0.5

    def block(args):
        i, q_i, c_i = args
        q_pos = i * Q_BLOCK + jnp.arange(Q_BLOCK)
        s = jnp.einsum('bqhd,bkhd->bhqk', q_i, k, preferred_element_type=jnp.float32) * scale
        s = s + jnp.swapaxes(c_i, 1, 2)[..., None] - c_k[:, :, None, :]
        s = jnp.where(key_pos[None, :] <= q_pos[:, None], s, -jnp.inf)
        p = jax.nn.softmax(s, axis=-1)
        return jnp.einsum('bhqk,bkhd->bqhd', p.astype(v.dtype), v)

    out = lax.map(block, (jnp.arange(nqb), to_blocks(q, nqb, Q_BLOCK), to_blocks(c, nqb, Q_BLOCK)))
    return from_blocks(out)

def dsa_attention(q_lat, q_rope, c_kv, k_rope, iq, ik, iw, topk):
    B, S, H, R = q_lat.shape
    nqb = S // Q_BLOCK
    key_pos = jnp.arange(S)
    bidx = jnp.arange(B)[:, None, None]
    scale = HEAD_DIM ** -0.5
    idx_scale = (IDX_DIM ** -0.5) * (N_IDX_HEADS ** -0.5)

    def block(args):
        i, ql_i, qr_i, iq_i, iw_i = args
        q_pos = i * Q_BLOCK + jnp.arange(Q_BLOCK)
        causal = key_pos[None, :] <= q_pos[:, None]
        dots = jnp.einsum('bqhd,bkd->bqhk', iq_i, ik, preferred_element_type=jnp.float32)
        score = jnp.einsum('bqh,bqhk->bqk', iw_i.astype(jnp.float32), jax.nn.relu(dots)) * idx_scale
        score = jnp.where(causal[None], score, -jnp.inf)
        _, sel = lax.top_k(score, topk)
        valid = sel <= q_pos[None, :, None]
        c_sel = c_kv[bidx, sel]
        kr_sel = k_rope[bidx, sel]
        logits = (jnp.einsum('bqhr,bqkr->bqhk', ql_i, c_sel, preferred_element_type=jnp.float32)
                  + jnp.einsum('bqhd,bqkd->bqhk', qr_i, kr_sel, preferred_element_type=jnp.float32)) * scale
        logits = jnp.where(valid[:, :, None, :], logits, -jnp.inf)
        p = jax.nn.softmax(logits, axis=-1)
        return jnp.einsum('bqhk,bqkr->bqhr', p.astype(c_kv.dtype), c_sel)

    out = lax.map(block, (jnp.arange(nqb), to_blocks(q_lat, nqb, Q_BLOCK), to_blocks(q_rope, nqb, Q_BLOCK),
                          to_blocks(iq, nqb, Q_BLOCK), to_blocks(iw, nqb, Q_BLOCK)))
    return from_blocks(out)

def moba_attention(q, k, v):
    B, S, H, D = q.shape
    nb = -(-S // MOBA_BLOCK)
    topb = min(MOBA_TOPB_MAX, nb - 1)
    pad = nb * MOBA_BLOCK - S
    qh = jnp.swapaxes(q, 1, 2)
    k_pad = jnp.pad(jnp.swapaxes(k, 1, 2), ((0, 0), (0, 0), (0, pad), (0, 0)))
    v_pad = jnp.pad(jnp.swapaxes(v, 1, 2), ((0, 0), (0, 0), (0, pad), (0, 0)))
    kb = k_pad.reshape(B, H, nb, MOBA_BLOCK, D)
    vb = v_pad.reshape(B, H, nb, MOBA_BLOCK, D)
    k_mean = jnp.mean(kb.astype(jnp.float32), axis=3)
    bi = jnp.arange(B)[:, None, None, None]
    hi = jnp.arange(H)[None, :, None, None]
    scale = D ** -0.5
    n_chunks = S // MOBA_Q_CHUNK
    q_chunks = jnp.transpose(qh.reshape(B, H, n_chunks, MOBA_Q_CHUNK, D), (2, 0, 1, 3, 4))

    def chunk(args):
        i, q_i = args
        q_pos = i * MOBA_Q_CHUNK + jnp.arange(MOBA_Q_CHUNK)
        own = (i * MOBA_Q_CHUNK) // MOBA_BLOCK
        k_own = lax.dynamic_slice_in_dim(k_pad, own * MOBA_BLOCK, MOBA_BLOCK, axis=2)
        v_own = lax.dynamic_slice_in_dim(v_pad, own * MOBA_BLOCK, MOBA_BLOCK, axis=2)
        own_pos = own * MOBA_BLOCK + jnp.arange(MOBA_BLOCK)
        s_own = jnp.einsum('bhqd,bhkd->bhqk', q_i, k_own, preferred_element_type=jnp.float32) * scale
        s_own = jnp.where(own_pos[None, :] <= q_pos[:, None], s_own, -jnp.inf)
        if topb == 0:
            p = jax.nn.softmax(s_own, axis=-1)
            return jnp.einsum('bhqk,bhkd->bhqd', p.astype(v.dtype), v_own)
        gate = jnp.einsum('bhqd,bhnd->bhqn', q_i.astype(jnp.float32), k_mean)
        gate = jnp.where(jnp.arange(nb) < own, gate, -jnp.inf)
        _, sel = lax.top_k(gate, topb)
        valid = sel < own
        k_sel = kb[bi, hi, sel]
        v_sel = vb[bi, hi, sel]
        s_sel = jnp.einsum('bhqd,bhqnkd->bhqnk', q_i, k_sel, preferred_element_type=jnp.float32) * scale
        s_sel = jnp.where(valid[..., None], s_sel, -jnp.inf).reshape(B, H, MOBA_Q_CHUNK, topb * MOBA_BLOCK)
        p = jax.nn.softmax(jnp.concatenate([s_sel, s_own], axis=-1), axis=-1).astype(v.dtype)
        p_sel = p[..., :topb * MOBA_BLOCK].reshape(B, H, MOBA_Q_CHUNK, topb, MOBA_BLOCK)
        p_own = p[..., topb * MOBA_BLOCK:]
        return (jnp.einsum('bhqnk,bhqnkd->bhqd', p_sel, v_sel)
                + jnp.einsum('bhqk,bhkd->bhqd', p_own, v_own))

    out = lax.map(chunk, (jnp.arange(n_chunks), q_chunks))
    return jnp.transpose(out, (1, 0, 3, 2, 4)).reshape(B, S, H, D)

def conv_glu_ffn(x, w_up, conv_w, conv_b, w_down):
    h = x @ w_up
    g, u = h[..., :D_FF_2], h[..., D_FF_2:]
    g = lax.conv_general_dilated(g, conv_w[:, None, :].astype(g.dtype), window_strides=(1,),
                                 padding=[(CONV_WIDTH_2 - 1, 0)], dimension_numbers=('NWC', 'WIO', 'NWC'),
                                 feature_group_count=D_FF_2) + conv_b
    return (jax.nn.silu(g) * u) @ w_down

def second_inputs(seed: int = 0) -> dict:
    key = jax.random.key(seed)
    ks = jax.random.split(key, 20)
    f32 = jnp.float32
    nrm = lambda k, shape, s: jax.random.normal(k, shape, f32) * s
    res_scale = (2 * DEPTH) ** -0.5
    x = jax.random.normal(ks[0], (BATCH, SEQ, D_MODEL), f32)
    positions = jnp.broadcast_to(jnp.arange(SEQ, dtype=jnp.int32)[None, :], (BATCH, SEQ))
    return {
        'x': x,
        'positions': positions,
        'attn_norm': 1.0 + nrm(ks[1], (DEPTH, D_MODEL), 0.02),
        'ffn_norm': 1.0 + nrm(ks[2], (DEPTH, D_MODEL), 0.02),
        'final_norm': 1.0 + nrm(ks[3], (D_MODEL,), 0.02),
        'w_in_even': nrm(ks[4], (N_EVEN, D_MODEL, EVEN_IN_DIM), D_MODEL ** -0.5),
        'b_fox_f': 3.0 + nrm(ks[5], (N_EVEN, N_FOX_HEADS), 0.5),
        'g_ckv': 1.0 + nrm(ks[6], (N_EVEN, DSA_KV_RANK), 0.02),
        'w_uk': nrm(ks[7], (N_EVEN, DSA_KV_RANK, N_DSA_HEADS, DSA_NOPE_DIM), DSA_KV_RANK ** -0.5),
        'w_uv': nrm(ks[8], (N_EVEN, DSA_KV_RANK, N_DSA_HEADS, DSA_V_DIM), DSA_KV_RANK ** -0.5),
        'w_out_even': nrm(ks[9], (N_EVEN, FOX_WIDTH + DSA_WIDTH, D_MODEL), (FOX_WIDTH + DSA_WIDTH) ** -0.5 * res_scale),
        'w_in_odd': nrm(ks[10], (N_ODD, D_MODEL, ODD_IN_DIM), D_MODEL ** -0.5),
        'w_out_odd': nrm(ks[11], (N_ODD, N_MOBA_HEADS * HEAD_DIM, D_MODEL), (N_MOBA_HEADS * HEAD_DIM) ** -0.5 * res_scale),
        'w_up': nrm(ks[12], (DEPTH, D_MODEL, 2 * D_FF_2), D_MODEL ** -0.5),
        'conv_w': nrm(ks[13], (DEPTH, CONV_WIDTH_2, D_FF_2), CONV_WIDTH_2 ** -0.5),
        'conv_b': nrm(ks[14], (DEPTH, D_FF_2), 0.01),
        'w_down': nrm(ks[15], (DEPTH, D_FF_2, D_MODEL), D_FF_2 ** -0.5 * res_scale),
    }

def second_block(x, positions, attn_norm, ffn_norm, final_norm, w_in_even, b_fox_f, g_ckv, w_uk, w_uv,
              w_out_even, w_in_odd, w_out_odd, w_up, conv_w, conv_b, w_down):
    B, S, _ = x.shape
    cos, sin = rope_tables_2(positions)
    dsa_topk = min(DSA_TOPK_MAX, S // 4)
    split_points = [sum(EVEN_SIZES[:j + 1]) for j in range(len(EVEN_SIZES) - 1)]
    for layer in range(DEPTH):
        h = rmsnorm(x, attn_norm[layer])
        if layer % 2 == 0:
            i = layer // 2
            proj = h @ w_in_even[i]
            fq, fk, fv, ff, dq, ckv, dkr, iq, ik, iw = jnp.split(proj, split_points, axis=-1)
            log_f = jax.nn.log_sigmoid(ff.astype(jnp.float32) + b_fox_f[i].astype(jnp.float32))
            fox_out = fox_attention(fq.reshape(B, S, N_FOX_HEADS, HEAD_DIM),
                                    fk.reshape(B, S, N_FOX_HEADS, HEAD_DIM),
                                    fv.reshape(B, S, N_FOX_HEADS, HEAD_DIM), log_f)
            dq = apply_partial_rope(dq.reshape(B, S, N_DSA_HEADS, HEAD_DIM), cos, sin)
            q_rope, q_nope = dq[..., :ROPE_DIM], dq[..., ROPE_DIM:]
            c_kv = rmsnorm(ckv, g_ckv[i])
            k_rope = apply_partial_rope(dkr[:, :, None, :], cos, sin)[:, :, 0, :]
            iq = apply_partial_rope(iq.reshape(B, S, N_IDX_HEADS, IDX_DIM), cos, sin)
            ik = apply_partial_rope(ik[:, :, None, :], cos, sin)[:, :, 0, :]
            q_lat = jnp.einsum('bshn,rhn->bshr', q_nope, w_uk[i])
            o_lat = dsa_attention(q_lat, q_rope, c_kv, k_rope, iq, ik, iw, dsa_topk)
            dsa_out = jnp.einsum('bshr,rhv->bshv', o_lat, w_uv[i])
            mixed = jnp.concatenate([fox_out.reshape(B, S, FOX_WIDTH), dsa_out.reshape(B, S, DSA_WIDTH)], axis=-1)
            x = x + mixed @ w_out_even[i]
        else:
            i = layer // 2
            proj = h @ w_in_odd[i]
            mq, mk, mv = jnp.split(proj, 3, axis=-1)
            mq = apply_partial_rope(mq.reshape(B, S, N_MOBA_HEADS, HEAD_DIM), cos, sin)
            mk = apply_partial_rope(mk.reshape(B, S, N_MOBA_HEADS, HEAD_DIM), cos, sin)
            mv = mv.reshape(B, S, N_MOBA_HEADS, HEAD_DIM)
            moba_out = moba_attention(mq, mk, mv)
            x = x + moba_out.reshape(B, S, N_MOBA_HEADS * HEAD_DIM) @ w_out_odd[i]
        x = x + conv_glu_ffn(rmsnorm(x, ffn_norm[layer]), w_up[layer], conv_w[layer], conv_b[layer], w_down[layer])
    return rmsnorm(x, final_norm)


def setup_inputs(seed=0):
    out = dict(first_inputs(seed))
    for name, value in second_inputs(seed + 1).items():
        if name != "x":
            out[name + "_2"] = value
    return out


def reference(
    x, mix_pre_g, mix_post_g, ffn_pre_g, ffn_post_g, w_ff1, w_ff2, conv_w_pw1, conv_b_pw1,
    conv_w_dw, conv_b_dw, conv_ln_g, conv_ln_b, conv_w_pw2, conv_b_pw2, mla_w_dq, mla_q_norm_g,
    mla_w_uq, mla_w_o, kv_in_g, kv_w_dkv, kv_norm_g, kv_w_kr, kv_w_uk, kv_w_uv, positions_2,
    attn_norm_2, ffn_norm_2, final_norm_2, w_in_even_2, b_fox_f_2, g_ckv_2, w_uk_2, w_uv_2,
    w_out_even_2, w_in_odd_2, w_out_odd_2, w_up_2, conv_w_2, conv_b_2, w_down_2,
):
    x = first_block(
        x, mix_pre_g, mix_post_g, ffn_pre_g, ffn_post_g, w_ff1, w_ff2, conv_w_pw1, conv_b_pw1,
        conv_w_dw, conv_b_dw, conv_ln_g, conv_ln_b, conv_w_pw2, conv_b_pw2, mla_w_dq,
        mla_q_norm_g, mla_w_uq, mla_w_o, kv_in_g, kv_w_dkv, kv_norm_g, kv_w_kr, kv_w_uk,
        kv_w_uv,
    )
    return second_block(
        x, positions_2, attn_norm_2, ffn_norm_2, final_norm_2, w_in_even_2, b_fox_f_2, g_ckv_2,
        w_uk_2, w_uv_2, w_out_even_2, w_in_odd_2, w_out_odd_2, w_up_2, conv_w_2, conv_b_2,
        w_down_2,
    )


_drawn_inputs = setup_inputs


def setup_inputs(seed=0):
    import zlib

    import numpy as np

    out = dict(_drawn_inputs(seed))
    spreads = {}
    factors = {'conv_b_pw1': 2.865,
     'conv_ln_b': 2.749,
     'mla_q_norm_g': 3.315,
     'attn_norm_2': 8.0,
     'ffn_norm_2': 8.0,
     'final_norm_2': 2.91,
     'b_fox_f_2': 5.232,
     'g_ckv_2': 8.0,
     'w_uk_2': 2.951,
     'conv_b_2': 8.0}
    for name, (base, spread) in spreads.items():
        noise = np.random.default_rng([zlib.crc32(name.encode()), seed]).standard_normal(out[name].shape)
        drawn = base * np.exp(spread * noise) if base else spread * noise
        out[name] = __import__('jax').numpy.asarray(drawn.astype(out[name].dtype))
    for name, factor in factors.items():
        out[name] = (out[name] * factor).astype(out[name].dtype)
    return out
```

```python
from contextlib import ExitStack

import numpy as np

import concourse.bass as bass
from concourse import mybir

P = 128
D = 1024
T = 256
DC = D // P
TT = T // P
D_FF = 4096
FC = D_FF // P
D_FF2 = 2816
GC = D_FF2 // P
TAPS = 31
TAPS2 = 3
HEADS = 8
NOPE, ROPE = 128, 64
Q_RANK, KV_RANK = 384, 256
MOBA_HEADS = 16
HD = 64
ROPE2 = 16
IDX_HEADS = 4
TOPK = T // 4
CHUNK = 64
UNIT = 4096
HALF = UNIT // 2
SW = 256.0
SX = 4.0
SF = 1.0
INV = 1.0 / (SW * SX)
INVF = 1.0 / (SW * SF)
RMS_EPS = 1e-6
LN_EPS = 1e-5
MASKED = -1e30
TAKEN = -3e38
RING = 4
SPAN = P + T

F32 = mybir.dt.float32
F16 = mybir.dt.float16
I32 = mybir.dt.int32
ALU = mybir.AluOpType
ACT = mybir.ActivationFunctionType
AXX = mybir.AxisListType.X

STREAM = [("pw1", 4), ("pw2", 2), ("ff1_0", 8), ("ff2_0", 8), ("kv", 1), ("dq", 1), ("ukv", 1), ("uq", 2),
          ("wo", 2), ("ff1_1", 8), ("ff2_1", 8), ("even", 6), ("oute", 2), ("up_0", 11), ("down_0", 8),
          ("odd", 6), ("outo", 2), ("up_1", 11), ("down_1", 8)]
FIRST = {}
UNITS = 0
for _name, _n in STREAM:
    FIRST[_name] = UNITS
    UNITS += _n
HALVES = 2 * UNITS

VECTORS = [("mix_pre_0", DC), ("mix_pre_1", DC), ("mix_post_0", DC), ("mix_post_1", DC), ("ffn_pre_0", DC),
           ("ffn_pre_1", DC), ("ffn_post_0", DC), ("ffn_post_1", DC), ("b_pw1", 2 * DC), ("taps", TAPS * DC),
           ("b_dw", DC), ("ln_g", DC), ("ln_b", DC), ("b_pw2", DC), ("q_norm", Q_RANK // P), ("kv_in", DC),
           ("kv_norm", KV_RANK // P), ("attn_0", DC), ("attn_1", DC), ("ffn2_0", DC), ("ffn2_1", DC),
           ("final", DC), ("g_ckv", 1), ("taps2_0", TAPS2 * GC), ("taps2_1", TAPS2 * GC), ("b_cv_0", GC),
           ("b_cv_1", GC), ("b_fox", HEADS), ("w_uk2", 4 * P), ("w_uv2", HEADS * HD)]
VCOL = {}
VCOLS = 0
for _name, _n in VECTORS:
    VCOL[_name] = VCOLS
    VCOLS += _n

CONSTANTS = [("ident", P), ("ones", P), ("mla_mask", SPAN), ("causal", SPAN), ("swap", P), ("swap2", P),
             ("cos", T), ("sin", T), ("upto", TT * T), ("pick", HEADS), ("freq2", 1), ("sign2", 1)]
CCOL = {}
CCOLS = 0
for _name, _n in CONSTANTS:
    CCOL[_name] = CCOLS
    CCOLS += _n

NORMS = [("mix_pre_0", DC), ("mix_post_0", DC), ("ffn_pre_0", DC), ("ffn_post_0", DC), ("mix_pre_1", DC),
         ("kv_norm", KV_RANK // P), ("q_norm", Q_RANK // P), ("mix_post_1", DC), ("ffn_pre_1", DC),
         ("ffn_post_1", DC), ("attn_0", DC), ("g_ckv", 1), ("ffn2_0", DC), ("attn_1", DC), ("ffn2_1", DC),
         ("final", DC)]
NORM_AT = {}
NORM_CHUNKS = dict(NORMS)
_at = 0
for _i, (_name, _n) in enumerate(NORMS):
    NORM_AT[_name] = (_i, _at)
    _at += _n


def _starts(names):
    at, found = 0, {}
    for name in names:
        found[name] = at
        at += NORM_CHUNKS.get(name, DC)
    return found


SCALE_AT = _starts(["mix_pre_0", "ffn_pre_0", "mix_pre_1", "kv_norm", "q_norm", "ffn_pre_1", "attn_0", "g_ckv",
                    "ffn2_0", "attn_1", "ffn2_1"])
SPLIT_AT = _starts(["mix_pre_0", "layer_norm", "ffn_pre_0", "mix_pre_1", "kv_norm", "q_norm", "ffn_pre_1", "attn_0",
                    "ffn2_0", "attn_1", "ffn2_1"])


def constants():
    c = np.zeros((P, CCOLS), np.float32)

    def put(name, value):
        value = np.asarray(value, np.float32)
        c[:value.shape[0], CCOL[name]:CCOL[name] + value.shape[1]] = value

    put("ident", np.eye(P))
    put("ones", np.ones((P, P)))
    q, k = np.arange(T)[:, None], np.arange(T)[None, :]

    def spans(allowed):
        m = np.where(allowed, 0.0, MASKED)
        return np.concatenate([m[:P, :P], m[P:, :]], axis=1)

    put("mla_mask", spans(k // CHUNK <= q // CHUNK))
    put("causal", spans(k <= q))
    d = np.arange(P)
    half = ROPE // 2
    swap = np.zeros((P, P))
    swap[np.where(d % ROPE < half, d + half, d - half), d] = 1.0
    put("swap", swap)
    half2 = ROPE2 // 2
    swap2 = np.zeros((P, P))
    turned = d % HD < ROPE2
    swap2[np.where(d % HD < half2, d + half2, d - half2)[turned], d[turned]] = 1.0
    put("swap2", swap2)
    inv = (1.0 / (10000.0 ** (np.arange(0, ROPE, 2, dtype=np.float32) / np.float32(ROPE)))).astype(np.float32)
    ang = np.arange(T, dtype=np.float32)[None, :] * inv[d % half][:, None]
    put("cos", np.cos(ang))
    put("sin", np.sin(ang) * np.where(d % ROPE < half, -1.0, 1.0)[:, None])
    put("upto", np.concatenate([(np.arange(P)[:, None] + t * P <= k) for t in range(TT)], axis=1))
    put("pick", np.eye(HEADS) * HD ** 0.5)
    freq = np.float32(500000.0) ** (-np.arange(0, ROPE2, 2, dtype=np.float32) / np.float32(ROPE2))
    put("freq2", np.where(turned, freq[d % half2], 0.0)[:, None])
    put("sign2", np.where(turned, np.where(d % HD < half2, -1.0, 1.0), 0.0)[:, None])
    return c


def conformer_mla_fox_dsa_moba_kernel(nc, w_stream, vec_dram, const_dram, x_dram, pos_dram, out_dram):
    with ExitStack() as ctx:
        def sb(name, shape, dt=F32):
            return ctx.enter_context(nc.sbuf_tensor(name, shape, dt))

        def sem(name):
            return ctx.enter_context(nc.semaphore(name))

        staged = sb("staged", [P, 2, UNIT])
        w_hi = sb("w_hi", [P, 2, UNIT], F16)
        w_lo = sb("w_lo", [P, 2, UNIT], F16)
        vec = sb("vec", [P, VCOLS])
        cst = sb("cst", [P, CCOLS])
        h = sb("h", [P, DC, T])
        m = sb("m", [P, DC, T])
        sq = sb("sq", [P, DC, T])
        xn = sb("xn", [P, DC, T])
        x_hi = sb("x_hi", [P, DC, T], F16)
        x_lo = sb("x_lo", [P, DC, T], F16)
        f_hi = sb("f_hi", [P, FC, T], F16)
        f_lo = sb("f_lo", [P, FC, T], F16)
        qT = sb("qT", [P, 12, T])
        kT = sb("kT", [P, 9, T])
        val = f_lo[:, FC // 2:, :].rearrange("p c t -> p (c t)").bitcast(F32).rearrange("p (t d) -> p t d", t=TT)
        stat = sb("stat", [P, 3, T])
        tmp = sb("tmp", [P, 4, T])
        pad = sb("pad", [P, 2, TAPS2 - 1 + T])
        cos2 = sb("cos2", [P, T])
        sin2 = sb("sin2", [P, T])
        posi = sb("posi", [P, T], I32)
        scores = sb("scores", [P, 2, SPAN])
        probs = sb("probs", [P, 2, SPAN])
        probsT = sb("probsT", [P, 2, SPAN])
        peak = sb("peak", [P, 2, 8])
        idx = sb("idx", [P, 2, SPAN])
        sel = sb("sel", [P, SPAN])
        top8 = sb("top8", [P, 2, 8])
        gates = sb("gates", [P, TT, 12])
        logf = sb("logf", [P, 5, TT * HEADS])
        cumT = sb("cumT", [HEADS, T])
        ckvt = sb("ckvt", [P, TT, P])
        u_pad = f_hi[:].rearrange("p c t -> p (c t)").bitcast(F32)[:, 0:DC * (TAPS - 1 + T)].rearrange(
            "p (c t) -> p c t", c=DC)
        conv = xn
        ps = ctx.enter_context(nc.psum_tensor("ps", [P, 8, 512], F32))
        STAT = ps[:, 7, 0:T]

        def v(name, i=0, n=1):
            return vec[:, VCOL[name] + i:VCOL[name] + i + n]

        def k(name, n=None):
            n = n or dict(CONSTANTS)[name]
            return cst[:, CCOL[name]:CCOL[name] + n]

        loaded = sem("loaded")
        landed = [sem("landed_0"), sem("landed_1")]
        hi_split = sem("hi_split")
        lo_split = sem("lo_split")
        squared = sem("squared")
        summed = sem("summed")
        inverted = sem("inverted")
        rooted = sem("rooted")
        scaled = sem("scaled")
        x_hi_ready = sem("x_hi_ready")
        x_lo_ready = sem("x_lo_ready")
        act_step = sem("act_step")
        dve_step = sem("dve_step")
        h_ready = {n: sem(f"h_ready_{n}") for n in ("mix_0", "ffn_0", "mix_1", "ffn_1", "oute", "down_0",
                                                   "outo", "down_1")}
        product = {n: sem(f"{n}_product") for n, _ in STREAM}
        drained = {n: sem(f"{n}_drained") for n, _ in STREAM if n not in h_ready}
        u_product = [sem(f"u_{i}_product") for i in range(2)]
        u_drained = [sem(f"u_{i}_drained") for i in range(2)]
        for n in ("oute", "outo", "down_0", "down_1"):
            drained[n] = h_ready[n]
        out_written = sem("out_written")
        stored = sem("stored")
        pads_zero = sem("pads_zero")
        glu = sem("glu")
        conv_ready = sem("conv_ready")
        ln_mean = sem("ln_mean")
        ln_centred = sem("ln_centred")
        ln_squared = sem("ln_squared")
        ln_var = sem("ln_var")
        ln_inverted = sem("ln_inverted")
        ln_rooted = sem("ln_rooted")
        ln_scaled = sem("ln_scaled")
        f_squared = [sem(f"f_squared_{i}") for i in range(2)]
        f_hi_ready = [sem(f"f_hi_ready_{i}") for i in range(2)]
        f_lo_ready = [sem(f"f_lo_ready_{i}") for i in range(2)]
        g_padded = [sem(f"g_padded_{i}") for i in range(2)]
        g_tap = [sem(f"g_tap_{i}") for i in range(2)]
        g_conv = [sem(f"g_conv_{i}") for i in range(2)]
        g_silu = [sem(f"g_silu_{i}") for i in range(2)]
        p_hi_ready = [sem(f"p_hi_ready_{i}") for i in range(2)]
        p_lo_ready = [sem(f"p_lo_ready_{i}") for i in range(2)]
        swapped = sem("swapped")
        turned = sem("turned")
        tables = sem("tables")
        sines = sem("sines")
        ckv_turned = sem("ckv_turned")
        ckv_rows = sem("ckv_rows")
        forget_exp = sem("forget_exp")
        forget_sum = sem("forget_sum")
        forget_log = sem("forget_log")
        fox_logf = sem("fox_logf")
        fox_cum = sem("fox_cum")
        fox_cum_ready = sem("fox_cum_ready")
        q_lat = sem("q_lat")
        q_lat_ready = sem("q_lat_ready")
        dots = sem("dots")
        dots_relu = sem("dots_relu")
        dots_added = sem("dots_added")
        selected = sem("selected")
        A = {n: {s: sem(f"{n}_{s}") for s in ("scores", "peak", "exp", "norm", "turn", "probsT", "out", "o_hi", "o_lo")}
             for n in ("mla", "fox", "dsa", "moba")}
        q_in = sem("q_in")
        q_in_hi = sem("q_in_hi")
        q_in_lo = sem("q_in_lo")
        o_lat = sem("o_lat")
        o_up = sem("o_up")

        qlatT = m

        def at64(b, c, head, t0, n):
            r = 64 * (head % 2)
            return b[r:r + 64, c, t0:t0 + n]

        def mla_terms(hd, t):
            n = P * (t + 1)
            return [(qT[:, hd, P * t:P * t + P], kT[:, hd, 0:n]),
                    (at64(qT, 8 + hd // 2, hd, P * t, P), at64(kT, 8, hd, 0, n))]

        def fox_terms(hd, t):
            n = P * (t + 1)
            mine = cst[0:HEADS, CCOL["pick"] + hd:CCOL["pick"] + hd + 1]
            return [(at64(qT, hd // 2, hd, P * t, P), at64(kT, hd // 2, hd, 0, n)),
                    (mine.to_broadcast([HEADS, P]), negT[:, 0:n]),
                    (cumT[:, P * t:P * t + P], mine.to_broadcast([HEADS, n]))]

        def dsa_terms(hd, t):
            n = P * (t + 1)
            return [(qlatT[:, hd, P * t:P * t + P], kT[:, 5, 0:n]),
                    (at64(qT, 4 + hd // 2, hd, P * t, P), at64(qT, 11, hd, 0, n))]

        def moba_terms(hd, t):
            n = P * (t + 1)
            return [(at64(qT, hd // 2, hd, P * t, P), at64(kT, hd // 2, hd, 0, n))]

        negT = sb("negT", [HEADS, T])
        KINDS = {
            "mla": dict(heads=HEADS, terms=mla_terms, mask=k("mla_mask"), scale=float(NOPE + ROPE) ** -0.5,
                        v=lambda hd, t: val[:, t, P * hd:P * hd + P], pair=False, chunk0=0),
            "fox": dict(heads=HEADS, terms=fox_terms, mask=k("causal"), scale=HD ** -0.5,
                        v=lambda hd, t: val[:, t, HD * hd:HD * hd + HD], pair=True, chunk0=0),
            "dsa": dict(heads=HEADS, terms=dsa_terms, mask=sel[:], scale=HD ** -0.5,
                        v=lambda hd, t: ckvt[:, t, :], pair=True, chunk0=4),
            "moba": dict(heads=MOBA_HEADS, terms=moba_terms, mask=k("causal"), scale=HD ** -0.5,
                         v=lambda hd, t: val[:, t, HD * hd:HD * hd + HD], pair=True, chunk0=0),
        }

        def out_of(kind, hd):
            if KINDS[kind]["pair"]:
                return KINDS[kind]["chunk0"] + hd // 2, hd % 2 == 1
            return KINDS[kind]["chunk0"] + hd, True

        ROPES = {"mla": [(kT, 8), (qT, 8), (qT, 9), (qT, 10), (qT, 11)],
                 "even": [(qT, c) for c in range(4, 12)],
                 "odd": [(b, c) for c in range(8) for b in (qT, kT)]}
        ROPE_AT = {"mla": 0, "even": 5, "odd": 13}

        block = ctx.enter_context(nc.Block())

        @block.sync
        def _(sp):
            sp.dma_start(h[:], x_dram).then_inc(loaded, 16)
            sp.dma_start(vec[:], vec_dram).then_inc(loaded, 16)
            sp.dma_start(cst[:], const_dram).then_inc(loaded, 16)
            sp.dma_start(posi[:], pos_dram).then_inc(loaded, 16)

            def load(u, s):
                sp.dma_start(staged[:, s:s + 1, :], w_stream[bass.ds(u, 1)].rearrange("u p n -> p u n")).then_inc(
                    landed[s], 16)

            load(0, 0)
            load(1, 1)
            with sp.Fori(0, UNITS // 2 - 1) as i:
                for s in range(2):
                    sp.wait_ge(lo_split, i * 4 + 2 * s + 2)
                    load(i * 2 + 2 + s, s)
            for u in range(UNITS // 2 * 2, UNITS):
                sp.wait_ge(lo_split, 2 * (u - 2) + 2)
                load(u, u % 2)
            for c in range(DC):
                sp.wait_ge(out_written, c + 1)
                sp.dma_start(out_dram[:, c, :], xn[:, c, :]).then_inc(stored, 16)
            sp.wait_ge(stored, 16 * DC)

        @block.tensor
        def _(pe):
            def weights(s, o, n):
                return w_hi[:, s, o:o + n], w_lo[:, s, o:o + n]

            def features(out, s, o, kc, xh, xl, fresh=None):
                for c in range(kc):
                    if fresh:
                        fresh(c)
                    wh, wl = weights(s, o + P * c, P)
                    pe.matmul(out, wh, xh[:, c, :], start=(c == 0), stop=False)
                    pe.matmul(out, wh, xl[:, c, :], start=False, stop=False)
                    last = pe.matmul(out, wl, xh[:, c, :], start=False, stop=(c == kc - 1))
                return last

            def rows(out, s, o, n, kc, xh, xl, t):
                for c in range(kc):
                    wh, wl = weights(s, o + n * c, n)
                    tok = slice(P * t, P * t + P)
                    pe.matmul(out, xh[:, c, tok], wh, start=(c == 0), stop=False)
                    pe.matmul(out, xh[:, c, tok], wl, start=False, stop=False)
                    last = pe.matmul(out, xl[:, c, tok], wh, start=False, stop=(c == kc - 1))
                return last

            def bank(name, n):
                if n >= RING:
                    pe.wait_ge(drained[name], n - RING + 1)
                return n % RING

            def arrived(g):
                pe.wait_ge(lo_split, g + 1)

            def normed(name):
                def fresh(c):
                    pe.wait_ge(x_lo_ready, SPLIT_AT[name] + c + 1)
                return fresh

            def sums(name):
                i, base = NORM_AT[name]
                n = NORM_CHUNKS[name]
                if i:
                    pe.wait_ge(inverted, i)
                for c in range(n):
                    pe.wait_ge(squared, base + c + 1)
                    last = pe.matmul(STAT, k("ones"), sq[:, c, :], start=(c == 0), stop=(c == n - 1))
                last.then_inc(summed, 1)

            def linear(name, per_unit, kc, xh, xl, fresh, chunks=None):
                u0 = FIRST[name]
                units = dict(STREAM)[name]
                n = 0
                for u in range(u0, u0 + units):
                    for j in range(per_unit):
                        if j in (0, (per_unit + 1) // 2):
                            arrived(2 * u + (j > 0))
                        b = bank(name, n)
                        features(ps[:, b, 0:T], u % 2, j * kc * P, kc, xh, xl, fresh if n == 0 else None).then_inc(
                            product[name], 1)
                        n += 1

            def ropes(name, ready):
                for i, (b, c) in enumerate(ROPES[name]):
                    ready(b, c)
                    at = ROPE_AT[name] + i
                    if at >= 2:
                        pe.wait_ge(turned, at - 1)
                    pe.matmul(ps[:, 4 + at % 2, 0:T], k("swap" if name == "mla" else "swap2"), b[:, c, :], start=True,
                              stop=True).then_inc(swapped, 1)

            def attention(kind):
                spec, s = KINDS[kind], A[kind]
                H = spec["heads"]
                latent = kind == "dsa"
                for i in range(H + 3 + latent):
                    if i < H:
                        if i >= 2:
                            pe.wait_ge(s["peak"], i - 1)
                        o = ps[:, 4 + i % 2, :]
                        for t in range(TT):
                            terms = spec["terms"](i, t)
                            for n, (a, b) in enumerate(terms):
                                last = pe.matmul(o[:, P * t:P * t + P * (t + 1)], a, b, start=(n == 0),
                                                 stop=(n == len(terms) - 1))
                        last.then_inc(s["scores"], 1)
                    hd = i - 1
                    if 0 <= hd < H:
                        pe.wait_ge(s["norm"], hd + 1)
                        if hd >= 2:
                            pe.wait_ge(s["probsT"], hd - 1)
                        o = ps[:, (6, 2)[hd % 2], :]
                        for n in range(3):
                            last = pe.transpose(o[:, P * n:P * n + P], probs[:, hd % 2, P * (0, 1, 2)[n]:P * n + P],
                                                k("ident"))
                        last.then_inc(s["turn"], 1)
                    hd = i - 2
                    if 0 <= hd < H:
                        pe.wait_ge(s["probsT"], hd + 1)
                        if latent:
                            o = ps[:, (7, 3)[hd % 2], 0:T]
                            if hd >= 2:
                                pe.wait_ge(o_lat, hd - 1)
                        else:
                            c, whole = out_of(kind, hd)
                            c -= spec["chunk0"]
                            r = 64 * (hd % 2) if spec["pair"] else 0
                            rn = 64 if spec["pair"] else P
                            if c >= 2:
                                pe.wait_ge(s["o_lo"], c - 1)
                            o = ps[r:r + rn, (7, 3)[c % 2], 0:T]
                        pT = probsT[:, hd % 2, :]
                        pe.matmul(o, spec["v"](hd, 0), pT[:, 0:T], start=True, stop=False)
                        pe.matmul(o[:, P:T], spec["v"](hd, 1), pT[:, T:SPAN], start=False, stop=True).then_inc(s["out"], 1)
                    hd = i - 3
                    if latent and 0 <= hd < H:
                        pe.wait_ge(o_lat, hd + 1)
                        c = hd // 2
                        if c >= 2:
                            pe.wait_ge(s["o_lo"], c - 1)
                        r = 64 * (hd % 2)
                        pe.matmul(ps[r:r + 64, c % 2, 0:T], v("w_uv2", HD * hd, HD), tmp[:, hd % 2, :], start=True,
                                  stop=True).then_inc(o_up, 1)

            pe.wait_ge(loaded, 64)
            sums("mix_pre_0")
            linear("pw1", 4, DC, x_hi, x_lo, normed("mix_pre_0"))
            for c in range(DC):
                pe.wait_ge(conv_ready, c + 1)
                last = pe.matmul(STAT, k("ones"), conv[:, c, :], start=(c == 0), stop=(c == DC - 1))
            last.then_inc(ln_mean, 1)
            for c in range(DC):
                pe.wait_ge(ln_squared, c + 1)
                last = pe.matmul(STAT, k("ones"), sq[:, c, :], start=(c == 0), stop=(c == DC - 1))
            last.then_inc(ln_var, 1)
            linear("pw2", 4, DC, x_hi, x_lo, normed("layer_norm"))
            sums("mix_post_0")

            def mlp(layer):
                sums(f"ffn_pre_{layer}")
                one, two = f"ff1_{layer}", f"ff2_{layer}"
                pe.wait_ge(x_lo_ready, SPLIT_AT[f"ffn_pre_{layer}"] + DC)
                pe.sem_inc(drained[one], RING)
                u0 = FIRST[one]
                with pe.Fori(0, dict(STREAM)[one] // 2) as i:
                    for s in range(2):
                        for j in range(4):
                            if j % 2 == 0:
                                pe.wait_ge(lo_split, i * 4 + (2 * (u0 + s) + j // 2 + 1))
                            n = 4 * s + j
                            pe.wait_ge(drained[one], i * 8 + (n + 1))
                            features(ps[:, n % RING, 0:T], (u0 + s) % 2, j * DC * P, DC, x_hi, x_lo).then_inc(
                                product[one], 1)
                pe.wait_ge(f_lo_ready[layer], FC)
                pe.sem_inc(drained[two], 2)
                u0 = FIRST[two]
                with pe.Fori(0, dict(STREAM)[two] // 2) as i:
                    for s in range(2):
                        pe.wait_ge(lo_split, i * 4 + (2 * (u0 + s) + 2))
                        pe.wait_ge(drained[two], i * 2 + (s + 1))
                        features(ps[:, s, 0:T], (u0 + s) % 2, 0, FC, f_hi, f_lo).then_inc(product[two], 1)
                sums(f"ffn_post_{layer}")

            mlp(0)

            sums("mix_pre_1")
            linear("kv", 3, DC, f_hi, f_lo, normed("mix_pre_1"))
            pe.wait_ge(drained["kv"], 3)
            linear("dq", 3, DC, x_hi, x_lo, lambda c: pe.wait_ge(q_in_lo, c + 1))
            sums("kv_norm")
            sums("q_norm")
            u = FIRST["ukv"]
            arrived(2 * u)
            pe.wait_ge(x_lo_ready, SPLIT_AT["kv_norm"] + KV_RANK // P)
            pe.wait_ge(drained["dq"], 3)
            n = 0
            for j in range(HEADS):
                b = bank("ukv", n)
                features(ps[:, b, 0:T], u % 2, 2 * P * j, 2, f_hi[:, 8:10], f_lo[:, 8:10]).then_inc(product["ukv"], 1)
                n += 1
            arrived(2 * u + 1)
            for half in range(2):
                for t in range(TT):
                    b = bank("ukv", n)
                    for c in range(2):
                        o = HALF + D * c + 512 * half
                        wh, wl = weights(u % 2, o, 512)
                        xh, xl = (y[:, 8 + c, P * t:P * t + P] for y in (f_hi, f_lo))
                        pe.matmul(ps[:, b, :], xh, wh, start=(c == 0), stop=False)
                        pe.matmul(ps[:, b, :], xh, wl, start=False, stop=False)
                        last = pe.matmul(ps[:, b, :], xl, wh, start=False, stop=(c == 1))
                    last.then_inc(product["ukv"], 1)
                    n += 1
            u = FIRST["uq"]
            pe.wait_ge(x_lo_ready, SPLIT_AT["q_norm"] + Q_RANK // P)
            pe.wait_ge(drained["ukv"], 12)
            for j in range(12):
                if j in (0, 5, 10):
                    arrived(2 * u + (0, 1, 2)[(0, 5, 10).index(j)])
                b = bank("uq", j)
                s, o = ((u % 2, 384 * j) if j < 5 else (u % 2, HALF + 384 * (j - 5)) if j < 10 else
                        ((u + 1) % 2, 384 * (j - 10)))
                features(ps[:, b, 0:T], s, o, 3, f_hi[:, 10:13], f_lo[:, 10:13]).then_inc(product["uq"], 1)
            ropes("mla", lambda b, c: (pe.wait_ge(drained["kv"], 3) if b is kT else
                                       pe.wait_ge(drained["uq"], c + 1)))
            pe.wait_ge(turned, 5)
            attention("mla")
            fresh_o = lambda c: pe.wait_ge(A["mla"]["o_lo"], c + 1)
            linear("wo", 4, DC, x_hi, x_lo, fresh_o)
            sums("mix_post_1")
            mlp(1)

            sums("attn_0")
            u0 = FIRST["even"]
            fresh = normed("attn_0")
            for n in range(16):
                if n % 2 == 0:
                    arrived(2 * u0 + n // 2)
                u = u0 + n // 4
                features(ps[:, bank("even", n), 0:T], u % 2, n % 4 * DC * P, DC, x_hi, x_lo,
                         fresh if n == 0 else None).then_inc(product["even"], 1)
            u = u0 + 4
            arrived(2 * u + 1)
            for t in range(TT):
                rows(ps[:, bank("even", 16 + t), :], u % 2, 0, 512, DC, x_hi, x_lo, t).then_inc(product["even"], 1)
            u = u0 + 5
            arrived(2 * u)
            features(ps[:, bank("even", 18), 0:T], u % 2, 0, DC, x_hi, x_lo).then_inc(product["even"], 1)
            for t in range(TT):
                rows(ps[:, bank("even", 19 + t), 0:12], u % 2, DC * P, 12, DC, x_hi, x_lo, t).then_inc(
                    product["even"], 1)
            ropes("even", lambda b, c: pe.wait_ge(drained["even"], 21))
            sums("g_ckv")
            pe.wait_ge(fox_logf, 1)
            for t in range(TT):
                last = pe.matmul(ps[0:HEADS, 3, 0:T], logf[:, 4, HEADS * t:HEADS * t + HEADS],
                                 k("upto")[:, T * t:T * t + T], start=(t == 0), stop=(t == TT - 1))
            last.then_inc(fox_cum, 1)
            for i in range(IDX_HEADS):
                if i == 0:
                    pe.wait_ge(turned, ROPE_AT["odd"])
                if i >= 2:
                    pe.wait_ge(dots_relu, i - 1)
                o = ps[:, 4 + i % 2, :]
                for t in range(TT):
                    last = pe.matmul(o[:, P * t:P * t + P * (t + 1)], at64(qT, 8 + i // 2, i, P * t, P),
                                     at64(qT, 10, i, 0, P * (t + 1)), start=True, stop=True)
                last.then_inc(dots, 1)
            for hd in range(HEADS):
                if hd >= 2:
                    pe.wait_ge(q_lat_ready, hd - 1)
                r = 64 * (hd % 2)
                pe.matmul(ps[:, hd % 2, 0:T], vec[r:r + 64, VCOL["w_uk2"] + P * (hd // 2):VCOL["w_uk2"] + P * (hd // 2) + P],
                          qT[r:r + 64, 4 + hd // 2, :], start=True, stop=True).then_inc(q_lat, 1)
            pe.wait_ge(scaled, SCALE_AT["g_ckv"] + 1)
            for t in range(TT):
                last = pe.transpose(ps[:, 2, P * t:P * t + P], kT[:, 5, P * t:P * t + P], k("ident"))
            last.then_inc(ckv_turned, 1)
            pe.wait_ge(fox_cum_ready, 1)
            pe.wait_ge(dots_relu, IDX_HEADS)
            pe.wait_ge(ckv_rows, 1)
            attention("fox")
            pe.wait_ge(A["fox"]["o_lo"], 4)
            attention("dsa")
            fresh_o = lambda c: pe.wait_ge(A["dsa"]["o_lo"], 4)
            linear("oute", 4, DC, x_hi, x_lo, fresh_o)

            def glu_mlp(layer):
                sums(f"ffn2_{layer}")
                up, down = f"up_{layer}", f"down_{layer}"
                pe.wait_ge(x_lo_ready, SPLIT_AT[f"ffn2_{layer}"] + DC)
                pe.sem_inc(drained[up], 2)
                pe.sem_inc(u_drained[layer], 2)
                u0, units = FIRST[up], dict(STREAM)[up]

                def unit(i, s):
                    for j in range(2):
                        pe.wait_ge(lo_split, i * 4 + (2 * (u0 + s) + j + 1))
                        n = 2 * s + j
                        sl = (u0 + s) % 2
                        pe.wait_ge(drained[up], i * 4 + (n + 1))
                        features(ps[:, j, 0:T], sl, 2 * j * DC * P, DC, x_hi, x_lo).then_inc(product[up], 1)
                        pe.wait_ge(u_drained[layer], i * 4 + (n + 1))
                        features(ps[:, 2 + j, 0:T], sl, (2 * j + 1) * DC * P, DC, x_hi, x_lo).then_inc(
                            u_product[layer], 1)

                with pe.Fori(0, units // 2) as i:
                    unit(i, 0)
                    unit(i, 1)
                unit(units // 2, 0)
                pe.wait_ge(p_lo_ready[layer], GC)
                pe.sem_inc(drained[down], 2)
                u0 = FIRST[down]
                with pe.Fori(0, dict(STREAM)[down] // 2) as i:
                    for s in range(2):
                        pe.wait_ge(lo_split, i * 4 + (2 * (u0 + s) + 2))
                        pe.wait_ge(drained[down], i * 2 + (s + 1))
                        features(ps[:, s, 0:T], (u0 + s) % 2, 0, GC, f_hi, f_lo).then_inc(product[down], 1)

            glu_mlp(0)
            sums("attn_1")
            u0 = FIRST["odd"]
            fresh = normed("attn_1")
            for n in range(16):
                if n % 2 == 0:
                    arrived(2 * u0 + n // 2)
                features(ps[:, bank("odd", n), 0:T], (u0 + n // 4) % 2, n % 4 * DC * P, DC, x_hi, x_lo,
                         fresh if n == 0 else None).then_inc(product["odd"], 1)
            for half in range(2):
                u = u0 + 4 + half
                arrived(2 * u + 1)
                for t in range(TT):
                    rows(ps[:, bank("odd", 16 + 2 * half + t), :], u % 2, 0, 512, DC, x_hi, x_lo, t).then_inc(
                        product["odd"], 1)
            ropes("odd", lambda b, c: pe.wait_ge(drained["odd"], 16))
            pe.wait_ge(turned, ROPE_AT["odd"] + 16)
            pe.wait_ge(drained["odd"], 20)
            attention("moba")
            fresh_o = lambda c: pe.wait_ge(A["moba"]["o_lo"], c + 1)
            linear("outo", 4, DC, x_hi, x_lo, fresh_o)
            glu_mlp(1)
            sums("final")

        @block.scalar
        def _(act):
            steps = [0]

            def chain(ins):
                steps[0] += 1
                ins.then_inc(act_step, 1)
                act.wait_ge(act_step, steps[0])

            def hi(g, s, at):
                o = HALF * (g % 2)
                act.wait_ge(landed[s], at)
                act.activation(w_hi[:, s, o:o + HALF], staged[:, s, o:o + HALF], ACT.Copy, scale=SW).then_inc(hi_split, 1)

            def split(g):
                if g < HALVES:
                    hi(g, g // 2 % 2, 16 * (g // 4 + 1))

            def squares(name, src, ready):
                for c in range(NORM_CHUNKS[name]):
                    ready(c)
                    act.activation(sq[:, c, :], src[:, c, :], ACT.Square).then_inc(squared, 1)

            def root(name):
                i = NORM_AT[name][0]
                act.wait_ge(inverted, i + 1)
                act.activation(stat[:, 2, :], stat[:, 1, :], ACT.Sqrt).then_inc(rooted, 1)

            def his(name, dst):
                base = SCALE_AT[name]
                for c in range(NORM_CHUNKS[name]):
                    act.wait_ge(scaled, base + c + 1)
                    act.activation(dst[:, c, :], xn[:, c, :], ACT.Copy, scale=SX).then_inc(x_hi_ready, 1)

            def evac(name, n, dst, scale=INV, cols=T):
                act.wait_ge(product[name], n + 1)
                act.activation(dst, ps[:, n % RING, 0:cols], ACT.Copy, scale=scale).then_inc(drained[name], 1)

            def behind(name, per_unit, each=None):
                u0, units = FIRST[name], dict(STREAM)[name]
                for n in range(units * per_unit):
                    if each:
                        each(n)
                    if (n + 1) * 2 % per_unit == 0:
                        act.wait_ge(product[name], n + 1)
                        split(2 * u0 + (n + 1) * 2 // per_unit - 1 + 4)

            def attention(kind):
                spec, s = KINDS[kind], A[kind]
                H = spec["heads"]
                latent = kind == "dsa"
                for i in range(H + 3 + latent):
                    if i < H:
                        act.wait_ge(s["peak"], i + 1)
                        if i >= 2:
                            act.wait_ge(s["turn"], i - 1)
                        b = i % 2
                        for t in range(TT):
                            sl = slice(P * t, P * t + P * (t + 1))
                            last = act.activation(probs[:, b, sl], scores[:, b, sl], ACT.Exp, bias=peak[:, b, 2 + t:3 + t],
                                                  accum_out=peak[:, b, 4 + t:5 + t])
                        last.then_inc(s["exp"], 1)
                    hd = i - 1
                    if 0 <= hd < H:
                        act.wait_ge(s["turn"], hd + 1)
                        if hd >= 2:
                            act.wait_ge(s["out"], hd - 1)
                        act.activation(probsT[:, hd % 2, :], ps[:, (6, 2)[hd % 2], 0:SPAN], ACT.Copy).then_inc(
                            s["probsT"], 1)
                    hd = i - 2
                    if 0 <= hd < H and latent:
                        act.wait_ge(s["out"], hd + 1)
                        if hd >= 2:
                            act.wait_ge(o_up, hd - 1)
                        act.activation(tmp[:, hd % 2, :], ps[:, (7, 3)[hd % 2], 0:T], ACT.Copy).then_inc(o_lat, 1)
                    hd = i - 2 - latent
                    if 0 <= hd < H:
                        c, whole = out_of(kind, hd)
                        if whole:
                            act.wait_ge(o_up if latent else s["out"], hd + 1)
                            n = c - spec["chunk0"]
                            b = n % 2 if latent else (7, 3)[n % 2]
                            act.activation(x_hi[:, c, :], ps[:, b, 0:T], ACT.Copy, scale=SX).then_inc(s["o_hi"], 1)

            for g in range(4):
                split(g)
            act.wait_ge(loaded, 64)
            act.wait_ge(tables, 1)
            act.activation(tmp[:, 2, :], tmp[:, 0, :], ACT.Sin).then_inc(sines, 1)
            act.activation(tmp[:, 3, :], tmp[:, 0, :], ACT.Sin, scale=0.5).then_inc(sines, 1)

            squares("mix_pre_0", h, lambda c: None)
            root("mix_pre_0")
            his("mix_pre_0", x_hi)
            u0 = FIRST["pw1"]
            for j in range(DC):
                act.wait_ge(product["pw1"], 2 * j + 1)
                if j >= 2:
                    act.wait_ge(glu, j - 1)
                act.activation(m[:, 2 * (j % 2), :], ps[:, 2 * j % RING, 0:T], ACT.Sigmoid, bias=v("b_pw1", DC + j),
                               scale=INV).then_inc(drained["pw1"], 1)
                act.wait_ge(product["pw1"], 2 * j + 2)
                act.activation(m[:, 2 * (j % 2) + 1, :], ps[:, (2 * j + 1) % RING, 0:T], ACT.Identity,
                               bias=v("b_pw1", j), scale=INV).then_inc(drained["pw1"], 1)
                split(2 * u0 + j + 4)
            for c in range(DC):
                act.wait_ge(ln_centred, c + 1)
                act.activation(sq[:, c, :], conv[:, c, :], ACT.Square).then_inc(ln_squared, 1)
            act.wait_ge(ln_inverted, 1)
            act.activation(stat[:, 2, :], stat[:, 1, :], ACT.Sqrt).then_inc(ln_rooted, 1)
            for c in range(DC):
                act.wait_ge(ln_scaled, c + 1)
                chain(act.activation(xn[:, c, :], xn[:, c, :], ACT.Silu, bias=v("ln_b", c), scale=v("ln_g", c)))
                act.activation(x_hi[:, c, :], xn[:, c, :], ACT.Copy, scale=SX).then_inc(x_hi_ready, 1)
            behind("pw2", 4)
            squares("mix_post_0", m, lambda c: act.wait_ge(drained["pw2"], c + 1))
            root("mix_post_0")

            def mlp(layer):
                one, two = f"ff1_{layer}", f"ff2_{layer}"
                squares(f"ffn_pre_{layer}", h, lambda c: act.wait_ge(h_ready[f"mix_{layer}"], c + 1))
                root(f"ffn_pre_{layer}")
                his(f"ffn_pre_{layer}", x_hi)
                u0 = FIRST[one]
                with act.Fori(0, dict(STREAM)[one] // 2) as i:
                    for n in range(8):
                        act.wait_ge(product[one], i * 8 + (n + 1))
                        act.wait_ge(f_squared[layer], i * 8 + (n + 1))
                        act.activation(tmp[:, n % 2, :], ps[:, n % RING, 0:T], ACT.Relu, scale=INV).then_inc(drained[one], 1)
                        act.wait_ge(drained[one], i * 8 + (n + 1 + RING))
                        act.activation(f_hi[:, bass.ds(i * 8 + n, 1), :], tmp[:, n % 2:n % 2 + 1, :], ACT.Square,
                                       scale=SF ** 0.5).then_inc(f_hi_ready[layer], 1)
                        if n % 2 == 1:
                            g = 2 * u0 + n // 2 + 4
                            hi(g, g // 2 % 2, i * 16 + 16 * (g // 4 + 1))
                u0 = FIRST[two]
                with act.Fori(0, dict(STREAM)[two] // 2) as i:
                    for s in range(2):
                        act.wait_ge(product[two], i * 2 + (s + 1))
                        for e in range(2):
                            g = 2 * (u0 + s) + e + 4
                            hi(g, g // 2 % 2, i * 16 + 16 * (g // 4 + 1))
                squares(f"ffn_post_{layer}", m, lambda c: act.wait_ge(drained[two], 2 + c + 1))
                root(f"ffn_post_{layer}")

            mlp(0)
            squares("mix_pre_1", h, lambda c: act.wait_ge(h_ready["ffn_0"], c + 1))
            root("mix_pre_1")
            for c in range(DC):
                act.wait_ge(scaled, SCALE_AT["mix_pre_1"] + c + 1)
                act.activation(f_hi[:, c, :], xn[:, c, :], ACT.Copy, scale=SX).then_inc(x_hi_ready, 1)
            for c in range(DC):
                act.wait_ge(q_in, c + 1)
                act.activation(x_hi[:, c, :], m[:, c, :], ACT.Copy, scale=SX).then_inc(q_in_hi, 1)
            u0 = FIRST["kv"]
            act.wait_ge(product["kv"], 2)
            split(2 * u0 + 4)
            act.wait_ge(product["kv"], 3)
            split(2 * u0 + 5)
            squares("kv_norm", kT, lambda c: act.wait_ge(drained["kv"], c + 1))
            u0 = FIRST["dq"]
            act.wait_ge(product["dq"], 2)
            split(2 * u0 + 4)
            act.wait_ge(product["dq"], 3)
            split(2 * u0 + 5)
            root("kv_norm")
            his("kv_norm", f_hi[:, 8:10])
            squares("q_norm", qT, lambda c: act.wait_ge(drained["dq"], c + 1))
            root("q_norm")
            his("q_norm", f_hi[:, 10:13])
            u0 = FIRST["ukv"]
            for n in range(8):
                evac("ukv", n, kT[:, n, :])
            split(2 * u0 + 4)
            for n in range(8, 12):
                half, t = (n - 8) // 2, (n - 8) % 2
                evac("ukv", n, val[:, t, 512 * half:512 * half + 512], cols=512)
            split(2 * u0 + 5)
            u0 = FIRST["uq"]
            for n in range(12):
                evac("uq", n, qT[:, n, :])
                if n in (4, 9, 11):
                    split(2 * u0 + 4 + (4, 9, 11).index(n))
            split(2 * u0 + 7)
            attention("mla")
            behind("wo", 4)
            squares("mix_post_1", m, lambda c: act.wait_ge(drained["wo"], c + 1))
            root("mix_post_1")
            mlp(1)

            squares("attn_0", h, lambda c: act.wait_ge(h_ready["ffn_1"], c + 1))
            root("attn_0")
            his("attn_0", x_hi)
            u0 = FIRST["even"]
            place = [(qT, 0), (qT, 1), (qT, 2), (qT, 3), (kT, 0), (kT, 1), (kT, 2), (kT, 3), (qT, 4), (qT, 5), (qT, 6),
                     (qT, 7), (qT, 8), (qT, 9), (kT, 4), (qT, 10)]
            for n, (b, c) in enumerate(place):
                evac("even", n, b[:, c, :])
                if n % 2:
                    split(2 * u0 + n // 2 + 4)
            for t in range(TT):
                evac("even", 16 + t, val[:, t, 0:512], cols=512)
            split(2 * u0 + 8 + 4)
            split(2 * u0 + 9 + 4)
            evac("even", 18, qT[:, 11, :])
            for t in range(TT):
                evac("even", 19 + t, gates[:, t, :], cols=12)
            split(2 * u0 + 10 + 4)
            split(2 * u0 + 11 + 4)
            squares("g_ckv", kT[:, 4:5], lambda c: act.wait_ge(drained["even"], 15))
            root("g_ckv")
            act.wait_ge(forget_sum, 1)
            act.activation(logf[:, 2, :], logf[:, 1, :], ACT.Exp, scale=-1.0).then_inc(forget_exp, 1)
            act.wait_ge(forget_sum, 2)
            act.activation(logf[:, 1, :], logf[:, 3, :], ACT.Ln).then_inc(forget_log, 1)
            for i in range(IDX_HEADS):
                act.wait_ge(dots, i + 1)
                if i >= 2:
                    act.wait_ge(dots_added, i - 1)
                act.activation(scores[:, i % 2, :], ps[:, 4 + i % 2, 0:SPAN], ACT.Relu,
                               scale=float(HD) ** -0.5 * float(IDX_HEADS) ** -0.5).then_inc(dots_relu, 1)
            for hd in range(HEADS):
                act.wait_ge(q_lat, hd + 1)
                act.activation(qlatT[:, hd, :], ps[:, hd % 2, 0:T], ACT.Copy).then_inc(q_lat_ready, 1)
            act.wait_ge(ckv_turned, 1)
            act.activation(ckvt[:].rearrange("p t r -> p (t r)"), ps[:, 2, 0:T], ACT.Copy).then_inc(ckv_rows, 1)
            attention("fox")
            attention("dsa")
            behind("oute", 4)

            def glu_mlp(layer, name, last_stage):
                up, down = f"up_{layer}", f"down_{layer}"
                squares(f"ffn2_{layer}", h, lambda c: act.wait_ge(h_ready[name], c + 1))
                root(f"ffn2_{layer}")
                his(f"ffn2_{layer}", x_hi)
                u0, units = FIRST[up], dict(STREAM)[up]

                def unit(i, s):
                    for j in range(2):
                        n = 2 * s + j
                        act.wait_ge(product[up], i * 4 + (n + 1))
                        act.wait_ge(g_conv[layer], i * 4 + (n + 1))
                        act.activation(pad[:, j, TAPS2 - 1:TAPS2 - 1 + T], ps[:, j, 0:T], ACT.Copy, scale=INV).then_inc(
                            drained[up], 1)
                        act.wait_ge(g_conv[layer], i * 4 + (n + 3))
                        act.activation(tmp[:, j, :], tmp[:, j, :], ACT.Silu).then_inc(g_silu[layer], 1)
                        act.wait_ge(u_drained[layer], i * 4 + (n + 3))
                        act.activation(f_hi[:, bass.ds(i * 4 + n, 1), :], tmp[:, 2 + j:3 + j, :], ACT.Copy,
                                       scale=SF).then_inc(p_hi_ready[layer], 1)
                        g = 2 * (u0 + s) + j + 4
                        hi(g, g // 2 % 2, i * 16 + 16 * (g // 4 + 1))

                with act.Fori(0, units // 2) as i:
                    unit(i, 0)
                    unit(i, 1)
                unit(units // 2, 0)
                u0, units = FIRST[down], dict(STREAM)[down]

                def pair(i, splits):
                    for s in range(2):
                        act.wait_ge(product[down], i * 2 + (s + 1))
                        for e in range(2):
                            g = 2 * (u0 + s) + e + 4
                            if splits:
                                hi(g, g // 2 % 2, i * 16 + 16 * (g // 4 + 1))

                with act.Fori(0, units // 2 - last_stage) as i:
                    pair(i, True)

            glu_mlp(0, "oute", 0)
            squares("attn_1", h, lambda c: act.wait_ge(h_ready["down_0"], 2 + c + 1))
            root("attn_1")
            his("attn_1", x_hi)
            u0 = FIRST["odd"]
            for n in range(16):
                evac("odd", n, (qT, kT)[n // 8][:, n % 8, :])
                if n % 2:
                    split(2 * u0 + n // 2 + 4)
            for n in range(16, 20):
                half, t = (n - 16) // 2, n % 2
                evac("odd", n, val[:, t, 512 * half:512 * half + 512], cols=512)
                if t:
                    split(2 * u0 + 8 + 2 * half + 4)
                    split(2 * u0 + 8 + 2 * half + 5)
            attention("moba")
            behind("outo", 4)
            glu_mlp(1, "outo", 1)
            squares("final", h, lambda c: act.wait_ge(h_ready["down_1"], 2 + c + 1))
            root("final")

        @block.vector
        def _(dve):
            steps = [0]

            def step(ins):
                steps[0] += 1
                ins.then_inc(dve_step, 1)
                return steps[0]

            def chain(ins):
                dve.wait_ge(dve_step, step(ins))

            def lo(s, e, at):
                o = HALF * e
                dve.wait_ge(hi_split, at)
                dve.scalar_tensor_tensor(w_lo[:, s, o:o + HALF], staged[:, s, o:o + HALF], SW, w_hi[:, s, o:o + HALF],
                                         ALU.mult, ALU.subtract).then_inc(lo_split, 1)

            def split(g):
                if g < HALVES:
                    lo(g // 2 % 2, g % 2, g + 1)

            def invert(name):
                i = NORM_AT[name][0]
                dve.wait_ge(summed, i + 1)
                chain(dve.tensor_scalar(stat[:, 0, :], STAT, 1.0 / (P * NORM_CHUNKS[name]), RMS_EPS, ALU.mult, ALU.add))
                dve.reciprocal(stat[:, 1, :], stat[:, 0, :]).then_inc(inverted, 1)

            def x_lows(name, c, dst):
                dve.wait_ge(x_hi_ready, SPLIT_AT[name] + c + 1)
                dve.scalar_tensor_tensor(dst[1][:, c, :], xn[:, c, :], SX, dst[0][:, c, :], ALU.mult,
                                         ALU.subtract).then_inc(x_lo_ready, 1)

            def scale(name, src, gain, dst):
                n = NORM_CHUNKS[name]
                dve.wait_ge(rooted, NORM_AT[name][0] + 1)
                for c in range(n + 1):
                    if c < n:
                        dve.scalar_tensor_tensor(xn[:, c, :], src[:, c, :], v(gain, c), stat[:, 2, :], ALU.mult,
                                                 ALU.mult).then_inc(scaled, 1)
                    if c:
                        x_lows(name, c - 1, dst)

            def post(name, ready):
                dve.wait_ge(rooted, NORM_AT[name][0] + 1)
                done = []
                for c in range(DC + 1):
                    if c < DC:
                        done.append(step(dve.scalar_tensor_tensor(m[:, c, :], m[:, c, :], v(name, c), stat[:, 2, :],
                                                                  ALU.mult, ALU.mult)))
                    if c:
                        dve.wait_ge(dve_step, done[c - 1])
                        dve.tensor_tensor(h[:, c - 1, :], h[:, c - 1, :], m[:, c - 1, :], ALU.add).then_inc(
                            h_ready[ready], 1)

            def evac(name, n, dst, scale=INV):
                dve.wait_ge(product[name], n + 1)
                dve.tensor_scalar(dst, ps[:, n % RING, 0:T], scale, None, ALU.mult).then_inc(drained[name], 1)

            def into_m(name):
                u0 = FIRST[name]
                for n in range(DC):
                    if name == "pw2":
                        dve.wait_ge(product[name], n + 1)
                        dve.tensor_scalar(m[:, n, :], ps[:, n % RING, 0:T], INV, v("b_pw2", n), ALU.mult,
                                          ALU.add).then_inc(drained[name], 1)
                    else:
                        evac(name, n, m[:, n, :])
                    if n % 2:
                        split(2 * u0 + n // 2 + 4)

            def into_h(name):
                u0 = FIRST[name]
                for n in range(DC):
                    dve.wait_ge(product[name], n + 1)
                    dve.scalar_tensor_tensor(h[:, n, :], ps[:, n % RING, 0:T], INV, h[:, n, :], ALU.mult,
                                             ALU.add).then_inc(h_ready[name], 1)
                    if n % 2:
                        split(2 * u0 + n // 2 + 4)

            def ropes(name):
                c_tab, s_tab = (k("cos"), k("sin")) if name == "mla" else (cos2[:], sin2[:])
                for i, (b, c) in enumerate(ROPES[name]):
                    at = ROPE_AT[name] + i
                    dve.wait_ge(swapped, at + 1)
                    t = tmp[:, 2 + at % 2, :]
                    step(dve.tensor_tensor(t, ps[:, 4 + at % 2, 0:T], s_tab, ALU.mult))
                    chain(dve.tensor_tensor(b[:, c, :], b[:, c, :], c_tab, ALU.mult))
                    dve.tensor_tensor(b[:, c, :], b[:, c, :], t, ALU.add).then_inc(turned, 1)

            def attention(kind):
                spec, s = KINDS[kind], A[kind]
                H = spec["heads"]
                latent = kind == "dsa"
                for i in range(H + 3 + latent):
                    if i < H:
                        b = i % 2
                        dve.wait_ge(s["scores"], i + 1)
                        if i >= 2:
                            dve.wait_ge(s["exp"], i - 1)
                        for t in range(TT):
                            sl = slice(P * t, P * t + P * (t + 1))
                            last = step(dve.tensor_tensor_reduce(scores[:, b, sl], ps[:, 4 + b, sl], spec["mask"][:, sl],
                                                                 spec["scale"], TAKEN, ALU.add, ALU.max,
                                                                 peak[:, b, t:t + 1]))
                        dve.wait_ge(dve_step, last)
                        dve.tensor_scalar(peak[:, b, 2:4], peak[:, b, 0:2], -1.0, None, ALU.mult).then_inc(s["peak"], 1)
                    hd = i - 1
                    if 0 <= hd < H:
                        b = hd % 2
                        dve.wait_ge(s["exp"], hd + 1)
                        chain(dve.reciprocal(peak[:, b, 6:8], peak[:, b, 4:6]))
                        for t in range(TT):
                            sl = slice(P * t, P * t + P * (t + 1))
                            last = dve.tensor_scalar(probs[:, b, sl], probs[:, b, sl], peak[:, b, 6 + t:7 + t], None,
                                                     ALU.mult)
                        last.then_inc(s["norm"], 1)
                    hd = i - 2 - latent
                    if 0 <= hd < H:
                        c, whole = out_of(kind, hd)
                        if whole:
                            n = c - spec["chunk0"]
                            b = n % 2 if latent else (7, 3)[n % 2]
                            dve.wait_ge(s["o_hi"], n + 1)
                            dve.scalar_tensor_tensor(x_lo[:, c, :], ps[:, b, 0:T], SX, x_hi[:, c, :], ALU.mult,
                                                     ALU.subtract).then_inc(s["o_lo"], 1)

            for g in range(4):
                split(g)
            dve.wait_ge(loaded, 64)
            dve.memset(pad[:], 0.0)
            chain(dve.memset(u_pad, 0.0))
            turn1 = 6.28125
            turn2 = float((np.array([2 * np.pi - 6.28125], np.float32).view(np.uint32) & np.uint32(0xFFFFF000)).view(
                np.float32)[0])
            turn3 = float(np.float32(2 * np.pi - 6.28125 - turn2))
            whole = 1.5 * 2.0 ** 23
            chain(dve.tensor_copy(sq[:, 0, :], posi[:]))
            chain(dve.tensor_scalar(sq[:, 1, :], sq[:, 0, :], k("freq2"), None, ALU.mult))
            chain(dve.tensor_scalar(sq[:, 2, :], sq[:, 1, :], float(1.0 / (2 * np.pi)), whole, ALU.mult, ALU.add))
            chain(dve.tensor_scalar(sq[:, 3, :], sq[:, 2, :], whole, None, ALU.subtract))
            chain(dve.scalar_tensor_tensor(sq[:, 1, :], sq[:, 3, :], -turn1, sq[:, 1, :], ALU.mult, ALU.add))
            chain(dve.scalar_tensor_tensor(sq[:, 1, :], sq[:, 3, :], -turn2, sq[:, 1, :], ALU.mult, ALU.add))
            chain(dve.scalar_tensor_tensor(sq[:, 1, :], sq[:, 3, :], -turn3, sq[:, 1, :], ALU.mult, ALU.add))
            dve.tensor_scalar(tmp[:, 0, :], sq[:, 1, :], 3.1415925, -3.1415925, ALU.min, ALU.max).then_inc(tables, 1)
            dve.wait_ge(sines, 2)
            step(dve.tensor_scalar(sin2[:], tmp[:, 2, :], k("sign2"), None, ALU.mult))
            chain(dve.tensor_tensor(cos2[:], tmp[:, 3, :], tmp[:, 3, :], ALU.mult))
            chain(dve.tensor_scalar(cos2[:], cos2[:], -2.0, 1.0, ALU.mult, ALU.add))

            invert("mix_pre_0")
            scale("mix_pre_0", h, "mix_pre_0", (x_hi, x_lo))
            u0 = FIRST["pw1"]
            for j in range(DC):
                dve.wait_ge(drained["pw1"], 2 * j + 2)
                dve.tensor_tensor(u_pad[:, j, TAPS - 1:TAPS - 1 + T], m[:, 2 * (j % 2), :], m[:, 2 * (j % 2) + 1, :],
                                  ALU.mult).then_inc(glu, 1)
                split(2 * u0 + j + 4)
            dve.wait_ge(glu, DC)
            for c in range(DC):
                chain(dve.tensor_scalar(conv[:, c, :], u_pad[:, c, 0:T], v("taps", c), v("b_dw", c), ALU.mult, ALU.add))
                for tap in range(1, TAPS):
                    ins = dve.scalar_tensor_tensor(conv[:, c, :], u_pad[:, c, tap:tap + T], v("taps", DC * tap + c),
                                                   conv[:, c, :], ALU.mult, ALU.add)
                    if tap < TAPS - 1:
                        chain(ins)
                ins.then_inc(conv_ready, 1)
            dve.wait_ge(ln_mean, 1)
            chain(dve.tensor_scalar(stat[:, 0, :], STAT, 1.0 / D, None, ALU.mult))
            for c in range(DC):
                dve.tensor_tensor(conv[:, c, :], conv[:, c, :], stat[:, 0, :], ALU.subtract).then_inc(ln_centred, 1)
            dve.wait_ge(ln_var, 1)
            chain(dve.tensor_scalar(stat[:, 0, :], STAT, 1.0 / D, LN_EPS, ALU.mult, ALU.add))
            dve.reciprocal(stat[:, 1, :], stat[:, 0, :]).then_inc(ln_inverted, 1)
            dve.wait_ge(ln_rooted, 1)
            dve.wait_ge(ln_centred, DC)
            for c in range(DC + 1):
                if c < DC:
                    dve.tensor_tensor(conv[:, c, :], conv[:, c, :], stat[:, 2, :], ALU.mult).then_inc(ln_scaled, 1)
                if c:
                    x_lows("layer_norm", c - 1, (x_hi, x_lo))
            into_m("pw2")
            invert("mix_post_0")
            post("mix_post_0", "mix_0")

            def mlp(layer):
                one, two = f"ff1_{layer}", f"ff2_{layer}"
                invert(f"ffn_pre_{layer}")
                scale(f"ffn_pre_{layer}", h, f"ffn_pre_{layer}", (x_hi, x_lo))
                dve.sem_inc(f_squared[layer], 2)
                u0 = FIRST[one]
                with dve.Fori(0, dict(STREAM)[one] // 2) as i:
                    for n in range(8):
                        r, f = tmp[:, n % 2, :], tmp[:, 2 + n % 2:3 + n % 2, :]
                        dve.wait_ge(drained[one], i * 8 + (n + 1 + RING))
                        dve.tensor_tensor(tmp[:, 2 + n % 2, :], r, r, ALU.mult).then_inc(f_squared[layer], 1)
                        dve.wait_ge(f_hi_ready[layer], i * 8 + (n + 1))
                        dve.wait_ge(f_squared[layer], i * 8 + (n + 3))
                        dve.scalar_tensor_tensor(f_lo[:, bass.ds(i * 8 + n, 1), :], f, SF,
                                                 f_hi[:, bass.ds(i * 8 + n, 1), :], ALU.mult, ALU.subtract).then_inc(
                            f_lo_ready[layer], 1)
                        if n % 2 == 1:
                            g = 2 * u0 + n // 2 + 4
                            lo(g // 2 % 2, g % 2, i * 4 + (g + 1))
                u0 = FIRST[two]
                with dve.Fori(0, dict(STREAM)[two] // 2) as i:
                    for s in range(2):
                        dve.wait_ge(product[two], i * 2 + (s + 1))
                        dve.tensor_scalar(m[:, bass.ds(i * 2 + s, 1), :], ps[:, s:s + 1, 0:T], INVF, None,
                                          ALU.mult).then_inc(drained[two], 1)
                        for e in range(2):
                            g = 2 * (u0 + s) + e + 4
                            lo(g // 2 % 2, e, i * 4 + (g + 1))
                invert(f"ffn_post_{layer}")
                post(f"ffn_post_{layer}", f"ffn_{layer}")

            mlp(0)
            invert("mix_pre_1")
            scale("mix_pre_1", h, "kv_in", (f_hi, f_lo))
            for c in range(DC + 1):
                if c < DC:
                    dve.scalar_tensor_tensor(m[:, c, :], h[:, c, :], v("mix_pre_1", c), stat[:, 2, :], ALU.mult,
                                             ALU.mult).then_inc(q_in, 1)
                if c:
                    dve.wait_ge(q_in_hi, c)
                    dve.scalar_tensor_tensor(x_lo[:, c - 1, :], m[:, c - 1, :], SX, x_hi[:, c - 1, :], ALU.mult,
                                             ALU.subtract).then_inc(q_in_lo, 1)
            u0 = FIRST["kv"]
            evac("kv", 0, kT[:, 0, :])
            evac("kv", 1, kT[:, 1, :])
            split(2 * u0 + 4)
            evac("kv", 2, kT[:, 8, :])
            split(2 * u0 + 5)
            u0 = FIRST["dq"]
            evac("dq", 0, qT[:, 0, :])
            evac("dq", 1, qT[:, 1, :])
            split(2 * u0 + 4)
            evac("dq", 2, qT[:, 2, :])
            split(2 * u0 + 5)
            invert("kv_norm")
            scale("kv_norm", kT, "kv_norm", (f_hi[:, 8:10], f_lo[:, 8:10]))
            invert("q_norm")
            scale("q_norm", qT, "q_norm", (f_hi[:, 10:13], f_lo[:, 10:13]))
            for g in range(2 * FIRST["ukv"] + 4, 2 * FIRST["uq"] + 8):
                split(g)
            ropes("mla")
            attention("mla")
            into_m("wo")
            invert("mix_post_1")
            post("mix_post_1", "mix_1")
            mlp(1)

            invert("attn_0")
            scale("attn_0", h, "attn_0", (x_hi, x_lo))
            for g in range(2 * FIRST["even"] + 4, 2 * FIRST["oute"] + 4):
                split(g)
            ropes("even")
            invert("g_ckv")
            dve.wait_ge(rooted, NORM_AT["g_ckv"][0] + 1)
            dve.scalar_tensor_tensor(kT[:, 5, :], kT[:, 4, :], v("g_ckv"), stat[:, 2, :], ALU.mult, ALU.mult).then_inc(
                scaled, 1)
            gate = gates[:, :, 0:HEADS]
            bias = v("b_fox", 0, HEADS)
            z = logf[:, 0, :].rearrange("p (t h) -> p t h", t=TT)
            for t in range(TT):
                last = step(dve.tensor_tensor(z[:, t, :], gate[:, t, :], bias, ALU.add))
            dve.wait_ge(dve_step, last)
            dve.scalar_tensor_tensor(logf[:, 1, :], logf[:, 0, :], -1.0, logf[:, 0, :], ALU.mult, ALU.max).then_inc(
                forget_sum, 1)
            dve.wait_ge(forget_exp, 1)
            dve.tensor_scalar(logf[:, 3, :], logf[:, 2, :], 1.0, None, ALU.add).then_inc(forget_sum, 1)
            dve.wait_ge(forget_sum, 2)
            chain(dve.tensor_scalar(logf[:, 4, :], logf[:, 3, :], 1.0, None, ALU.subtract))
            chain(dve.tensor_tensor(logf[:, 2, :], logf[:, 2, :], logf[:, 4, :], ALU.subtract))
            dve.wait_ge(forget_log, 1)
            chain(dve.reciprocal(logf[:, 4, :], logf[:, 3, :]))
            chain(dve.tensor_tensor(logf[:, 2, :], logf[:, 2, :], logf[:, 4, :], ALU.mult))
            chain(dve.tensor_tensor(logf[:, 2, :], logf[:, 2, :], logf[:, 1, :], ALU.add))
            dve.scalar_tensor_tensor(logf[:, 4, :], logf[:, 0, :], 0.0, logf[:, 2, :], ALU.min, ALU.subtract).then_inc(
                fox_logf, 1)
            dve.wait_ge(fox_cum, 1)
            step(dve.tensor_copy(cumT[:], ps[0:HEADS, 3, 0:T]))
            dve.tensor_scalar(negT[:], ps[0:HEADS, 3, 0:T], -1.0, None, ALU.mult).then_inc(fox_cum_ready, 1)
            for i in range(IDX_HEADS):
                dve.wait_ge(dots_relu, i + 1)
                if i:
                    dve.wait_ge(dots_added, i)
                for t in range(TT):
                    sl = slice(P * t, P * t + P * (t + 1))
                    w = gates[:, t, HEADS + i:HEADS + i + 1]
                    if i == 0:
                        last = dve.tensor_scalar(idx[:, 0, sl], scores[:, i % 2, sl], w, None, ALU.mult)
                    else:
                        last = dve.scalar_tensor_tensor(idx[:, 0, sl], scores[:, i % 2, sl], w, idx[:, 0, sl], ALU.mult,
                                                        ALU.add)
                last.then_inc(dots_added, 1)
            dve.wait_ge(dots_added, IDX_HEADS)
            chain(dve.tensor_tensor(idx[:, 0, :], idx[:, 0, :], k("causal"), ALU.add))
            for n in range(TOPK // 8):
                a, b = idx[:, n % 2, :], idx[:, (n + 1) % 2, :]
                for t in range(TT):
                    sl = slice(P * t, P * t + P * (t + 1))
                    last = step(dve.max(top8[:, t, :], a[:, sl]))
                dve.wait_ge(dve_step, last)
                for t in range(TT):
                    sl = slice(P * t, P * t + P * (t + 1))
                    last = step(dve.match_replace(b[:, sl], top8[:, t, :], a[:, sl], TAKEN))
                dve.wait_ge(dve_step, last)
            chain(dve.tensor_scalar(sel[:], idx[:, TOPK // 8 % 2, :], TAKEN / 2, MASKED, ALU.is_gt, ALU.mult))
            chain(dve.tensor_tensor(sel[:], sel[:], k("causal"), ALU.add))
            attention("fox")
            attention("dsa")
            into_h("oute")

            def glu_mlp(layer):
                up, down = f"up_{layer}", f"down_{layer}"
                invert(f"ffn2_{layer}")
                scale(f"ffn2_{layer}", h, f"ffn2_{layer}", (x_hi, x_lo))
                dve.sem_inc(g_conv[layer], 2)
                u0, units = FIRST[up], dict(STREAM)[up]

                def unit(i, s):
                    for j in range(2):
                        n = 2 * s + j
                        y = tmp[:, j, :]
                        dve.wait_ge(drained[up], i * 4 + (n + 3))
                        taps = [vec[:, bass.ds(i * 4 + (VCOL[f"taps2_{layer}"] + GC * q + n), 1)] for q in range(TAPS2)]
                        b = vec[:, bass.ds(i * 4 + (VCOL[f"b_cv_{layer}"] + n), 1)]
                        dve.tensor_scalar(y, pad[:, j, 0:T], taps[0], b, ALU.mult, ALU.add).then_inc(g_tap[layer], 1)
                        dve.wait_ge(g_tap[layer], i * 8 + (2 * n + 1))
                        dve.scalar_tensor_tensor(y, pad[:, j, 1:1 + T], taps[1], y, ALU.mult, ALU.add).then_inc(
                            g_tap[layer], 1)
                        dve.wait_ge(g_tap[layer], i * 8 + (2 * n + 2))
                        dve.scalar_tensor_tensor(y, pad[:, j, 2:2 + T], taps[2], y, ALU.mult, ALU.add).then_inc(
                            g_conv[layer], 1)
                        dve.wait_ge(u_product[layer], i * 4 + (n + 1))
                        dve.wait_ge(g_silu[layer], i * 4 + (n + 1))
                        dve.scalar_tensor_tensor(tmp[:, 2 + j, :], ps[:, 2 + j, 0:T], INV, y, ALU.mult,
                                                 ALU.mult).then_inc(u_drained[layer], 1)
                        dve.wait_ge(p_hi_ready[layer], i * 4 + (n + 1))
                        dve.scalar_tensor_tensor(f_lo[:, bass.ds(i * 4 + n, 1), :], tmp[:, 2 + j:3 + j, :], SF,
                                                 f_hi[:, bass.ds(i * 4 + n, 1), :], ALU.mult, ALU.subtract).then_inc(
                            p_lo_ready[layer], 1)
                        g = 2 * (u0 + s) + j + 4
                        lo(g // 2 % 2, j, i * 4 + (g + 1))

                with dve.Fori(0, units // 2) as i:
                    unit(i, 0)
                    unit(i, 1)
                unit(units // 2, 0)
                u0, units = FIRST[down], dict(STREAM)[down]

                def pair(i, splits):
                    for s in range(2):
                        dve.wait_ge(product[down], i * 2 + (s + 1))
                        hc = h[:, bass.ds(i * 2 + s, 1), :]
                        dve.scalar_tensor_tensor(hc, ps[:, s:s + 1, 0:T], INVF, hc, ALU.mult, ALU.add).then_inc(
                            h_ready[down], 1)
                        for e in range(2):
                            g = 2 * (u0 + s) + e + 4
                            if splits:
                                lo(g // 2 % 2, e, i * 4 + (g + 1))

                ends = layer == 1
                with dve.Fori(0, units // 2 - ends) as i:
                    pair(i, True)
                if ends:
                    pair(units // 2 - 1, False)

            glu_mlp(0)
            invert("attn_1")
            scale("attn_1", h, "attn_1", (x_hi, x_lo))
            for g in range(2 * FIRST["odd"] + 4, 2 * FIRST["outo"] + 4):
                split(g)
            ropes("odd")
            attention("moba")
            into_h("outo")
            glu_mlp(1)
            invert("final")
            dve.wait_ge(rooted, NORM_AT["final"][0] + 1)
            for c in range(DC):
                dve.scalar_tensor_tensor(xn[:, c, :], h[:, c, :], v("final", c), stat[:, 2, :], ALU.mult,
                                         ALU.mult).then_inc(out_written, 1)


def columns(w):
    r, n = w.shape
    return list(np.ascontiguousarray(w.reshape(r // P, P, n // P, P).transpose(2, 1, 0, 3)).reshape(n // P, P, r))


def whole(w):
    r, n = w.shape
    return np.ascontiguousarray(w.reshape(r // P, P, n).transpose(1, 0, 2)).reshape(P, r // P * n)


def stream_of(a):
    out = np.zeros((UNITS, P, UNIT), np.float32)

    def put(name, unit, at, blocks):
        for b in blocks:
            out[FIRST[name] + unit, :, at:at + b.shape[1]] = b
            at += b.shape[1]

    def fill(name, chunks, per_unit, first=0):
        for u in range(0, len(chunks), per_unit):
            put(name, first + u // per_unit, 0, chunks[u:u + per_unit])

    def woven(w):
        c = columns(w)
        n = len(c) // 2
        return c[:n], c[n:]

    first, gate = woven(a["conv_w_pw1"][0])
    fill("pw1", [x for g, y in zip(gate, first) for x in (g, y)], 4)
    fill("pw2", columns(a["conv_w_pw2"][0]), 4)
    for layer in range(2):
        fill(f"ff1_{layer}", columns(a["w_ff1"][layer]), 4)
        fill(f"ff2_{layer}", columns(a["w_ff2"][layer]), 1)
    kr = a["kv_w_kr"]
    put("kv", 0, 0, columns(np.concatenate([a["kv_w_dkv"], kr, kr], axis=1)))
    put("dq", 0, 0, columns(a["mla_w_dq"][0]))
    put("ukv", 0, 0, columns(a["kv_w_uk"]))
    put("ukv", 0, HALF, [whole(a["kv_w_uv"])])
    uq = a["mla_w_uq"][0].reshape(Q_RANK, HEADS, NOPE + ROPE)
    uq = columns(np.concatenate([uq[:, :, :NOPE].reshape(Q_RANK, -1), uq[:, :, NOPE:].reshape(Q_RANK, -1)], axis=1))
    put("uq", 0, 0, uq[0:5])
    put("uq", 0, HALF, uq[5:10])
    put("uq", 1, 0, uq[10:12])
    fill("wo", columns(a["mla_w_o"][0]), 4)
    w = a["w_in_even_2"][0]
    wide = HEADS * HD
    fq, fk, fv = (w[:, wide * i:wide * i + wide] for i in range(3))
    ff, w = w[:, 3 * wide:3 * wide + HEADS], w[:, 3 * wide + HEADS:]
    dq, ckv, dkr, iq, ik, iw = np.split(w, np.cumsum([wide, P, ROPE2, IDX_HEADS * HD, HD]), axis=1)
    fill("even", columns(np.concatenate([fq, fk, dq, iq, ckv, ik, ik], axis=1)), 4)
    put("even", 4, 0, [whole(fv)])
    none = np.zeros((D, HD - ROPE2), np.float32)
    put("even", 5, 0, columns(np.concatenate([dkr, none, dkr, none], axis=1)))
    put("even", 5, D, [whole(np.concatenate([ff, iw], axis=1))])
    fill("oute", columns(a["w_out_even_2"][0]), 4)
    for layer in range(2):
        g, u = woven(a["w_up_2"][layer])
        fill(f"up_{layer}", [x for pair in zip(g, u) for x in pair], 4)
        fill(f"down_{layer}", columns(a["w_down_2"][layer]), 1)
    w = a["w_in_odd_2"][0]
    fill("odd", columns(w[:, :2 * D]), 4)
    for half in range(2):
        put("odd", 4 + half, 0, [whole(w[:, 2 * D + 512 * half:2 * D + 512 * half + 512])])
    fill("outo", columns(a["w_out_odd_2"][0]), 4)
    return out


def vectors_of(a):
    out = np.zeros((P, VCOLS), np.float32)

    def put(name, value):
        x = np.asarray(value, np.float32).reshape(-1, P).T
        out[:, VCOL[name]:VCOL[name] + x.shape[1]] = x

    for layer in range(2):
        for name in ("mix_pre", "mix_post", "ffn_pre", "ffn_post"):
            put(f"{name}_{layer}", a[f"{name}_g"][layer])
        put(f"attn_{layer}", a["attn_norm_2"][layer])
        put(f"ffn2_{layer}", a["ffn_norm_2"][layer])
        put(f"taps2_{layer}", a["conv_w_2"][layer])
        put(f"b_cv_{layer}", a["conv_b_2"][layer])
    for name, value in (("b_pw1", a["conv_b_pw1"]), ("taps", a["conv_w_dw"]), ("b_dw", a["conv_b_dw"]),
                        ("ln_g", a["conv_ln_g"]), ("ln_b", a["conv_ln_b"]), ("b_pw2", a["conv_b_pw2"]),
                        ("q_norm", a["mla_q_norm_g"]), ("kv_in", a["kv_in_g"]), ("kv_norm", a["kv_norm_g"]),
                        ("final", a["final_norm_2"]), ("g_ckv", a["g_ckv_2"])):
        put(name, value)
    out[:, VCOL["b_fox"]:VCOL["b_fox"] + HEADS] = a["b_fox_f_2"][0]
    uk = np.zeros((HEADS, HD, P), np.float32)
    uk[:, ROPE2:, :] = a["w_uk_2"][0].transpose(1, 2, 0)
    out[:, VCOL["w_uk2"]:VCOL["w_uk2"] + 4 * P] = uk.reshape(4, P, P).transpose(1, 0, 2).reshape(P, 4 * P)
    out[:, VCOL["w_uv2"]:VCOL["w_uv2"] + HEADS * HD] = a["w_uv_2"][0].reshape(P, HEADS * HD)
    return out


def kernel(**inputs):
    import concourse.bacc as bacc
    from concourse.bass_utils import run_bass_kernel_spmd

    a = {name: np.asarray(value) for name, value in inputs.items()}
    arrays = {
        "weights": stream_of(a),
        "vectors": vectors_of(a),
        "constants": constants(),
        "x_turned": np.ascontiguousarray(a["x"][0].T.reshape(DC, P, T).transpose(1, 0, 2)),
        "positions": np.ascontiguousarray(np.broadcast_to(a["positions_2"].reshape(1, T), (P, T))),
    }
    nc = bacc.Bacc("TRN2", target_bir_lowering=False, num_devices=1)
    args = [nc.dram_tensor(n, x.shape, mybir.dt.from_np(x.dtype), kind="ExternalInput").ap() for n, x in arrays.items()]
    args.append(nc.dram_tensor("out", (P, DC, T), F32, kind="ExternalOutput").ap())
    conformer_mla_fox_dsa_moba_kernel(nc, *args)
    got = run_bass_kernel_spmd(nc, [arrays], core_ids=[0]).results[0]["out"]
    return np.ascontiguousarray(got.transpose(1, 0, 2).reshape(D, T).T)[None]
```

```python
from contextlib import ExitStack

import numpy as np

import concourse.bass as bass
from concourse import mybir

P = 128
D = 1024
T = 256
DC = D // P
TT = T // P
D_FF = 4096
FC = D_FF // P
D_FF2 = 2816
GC = D_FF2 // P
TAPS = 31
TAPS2 = 3
HEADS = 8
NOPE, ROPE = 128, 64
Q_RANK, KV_RANK = 384, 256
MOBA_HEADS = 16
HD = 64
ROPE2 = 16
IDX_HEADS = 4
TOPK = T // 4
CHUNK = 64
UNIT = 4096
HALF = UNIT // 2
SW = 256.0
SX = 4.0
SF = 1.0
INV = 1.0 / (SW * SX)
INVF = 1.0 / (SW * SF)
RMS_EPS = 1e-6
LN_EPS = 1e-5
MASKED = -1e30
TAKEN = -3e38
RING = 4
TURN_LAG, OUT_LAG, UP_LAG = 2, 3, 2
SPAN = P + T

F32 = mybir.dt.float32
F16 = mybir.dt.float16
I32 = mybir.dt.int32
ALU = mybir.AluOpType
ACT = mybir.ActivationFunctionType
AXX = mybir.AxisListType.X

STREAM = [("pw1", 4), ("pw2", 2), ("ff1_0", 8), ("ff2_0", 8), ("kv", 1), ("dq", 1), ("ukv", 1), ("uq", 2),
          ("wo", 2), ("ff1_1", 8), ("ff2_1", 8), ("even", 6), ("oute", 2), ("up_0", 11), ("down_0", 8),
          ("odd", 6), ("outo", 2), ("up_1", 11), ("down_1", 8)]
FIRST = {}
UNITS = 0
for _name, _n in STREAM:
    FIRST[_name] = UNITS
    UNITS += _n
HALVES = 2 * UNITS
QUARTER = HALF // 4
SPREAD = {"mla": (1, 2 * FIRST["uq"] + 6, 2), "even": (0, 2 * FIRST["even"] + 12, 4), "moba": (0, 2 * FIRST["odd"] + 13, 3)}


def spread(kind, step, last):
    first, g, halves = SPREAD[kind]
    n = step - first
    return [(g + q // 4, q % 4) for q in range(max(n, 0), 4 * halves if last else min(n + 1, 4 * halves))]


VECTORS = [("mix_pre_0", DC), ("mix_pre_1", DC), ("mix_post_0", DC), ("mix_post_1", DC), ("ffn_pre_0", DC),
           ("ffn_pre_1", DC), ("ffn_post_0", DC), ("ffn_post_1", DC), ("b_pw1", 2 * DC), ("taps", TAPS * DC),
           ("b_dw", DC), ("ln_g", DC), ("ln_b", DC), ("b_pw2", DC), ("q_norm", Q_RANK // P), ("kv_in", DC),
           ("kv_norm", KV_RANK // P), ("attn_0", DC), ("attn_1", DC), ("ffn2_0", DC), ("ffn2_1", DC),
           ("final", DC), ("g_ckv", 1), ("taps2_0", TAPS2 * GC), ("taps2_1", TAPS2 * GC), ("b_cv_0", GC),
           ("b_cv_1", GC), ("b_fox", HEADS), ("w_uk2", 4 * P), ("w_uv2", HEADS * HD)]
VCOL = {}
VCOLS = 0
for _name, _n in VECTORS:
    VCOL[_name] = VCOLS
    VCOLS += _n

CONSTANTS = [("ident", P), ("ones", P), ("rms_eps", 1), ("ln_eps", 1), ("mla_mask", SPAN), ("causal", SPAN), ("swap", P), ("swap2", P),
             ("cos", T), ("sin", T), ("upto", TT * T), ("pick", HEADS), ("freq2", 1), ("sign2", 1)]
CCOL = {}
CCOLS = 0
for _name, _n in CONSTANTS:
    CCOL[_name] = CCOLS
    CCOLS += _n

NORMS = [("mix_pre_0", DC), ("mix_post_0", DC), ("ffn_pre_0", DC), ("ffn_post_0", DC), ("mix_pre_1", DC),
         ("kv_norm", KV_RANK // P), ("q_norm", Q_RANK // P), ("mix_post_1", DC), ("ffn_pre_1", DC),
         ("ffn_post_1", DC), ("attn_0", DC), ("g_ckv", 1), ("ffn2_0", DC), ("attn_1", DC), ("ffn2_1", DC),
         ("final", DC)]
NORM_AT = {}
NORM_CHUNKS = dict(NORMS)
for _i, (_name, _n) in enumerate(NORMS):
    NORM_AT[_name] = _i


def _starts(names):
    at, found = 0, {}
    for name in names:
        found[name] = at
        at += NORM_CHUNKS.get(name, DC)
    return found


SCALE_AT = _starts(["mix_pre_0", "ffn_pre_0", "mix_pre_1", "kv_norm", "q_norm", "ffn_pre_1", "attn_0", "g_ckv",
                    "ffn2_0", "attn_1", "ffn2_1"])
SQUARE_AT = _starts(["mix_pre_0", "ffn_pre_0", "mix_pre_1", "kv_norm", "q_norm", "ffn_pre_1", "attn_0", "g_ckv"])
ADDED_AT = _starts(["mix_post_0", "ffn_post_0", "mix_post_1", "ffn_post_1", "ffn2_0", "attn_1", "ffn2_1", "final"])
CONV_VECTOR = (0, 2, 4, 6)
CONV_POOL = (1,)
CONV_TENSOR = (3, 5, 7)
SPLIT_AT = _starts(["mix_pre_0", "layer_norm", "ffn_pre_0", "mix_pre_1", "kv_norm", "q_norm", "ffn_pre_1", "attn_0",
                    "ffn2_0", "attn_1", "ffn2_1"])


def constants():
    c = np.zeros((P, CCOLS), np.float32)

    def put(name, value):
        value = np.asarray(value, np.float32)
        c[:value.shape[0], CCOL[name]:CCOL[name] + value.shape[1]] = value

    put("ident", np.eye(P))
    put("ones", np.ones((P, P)))
    q, k = np.arange(T)[:, None], np.arange(T)[None, :]

    def spans(allowed):
        m = np.where(allowed, 0.0, MASKED)
        return np.concatenate([m[:P, :P], m[P:, :]], axis=1)

    put("mla_mask", spans(k // CHUNK <= q // CHUNK))
    put("causal", spans(k <= q))
    d = np.arange(P)
    half = ROPE // 2
    swap = np.zeros((P, P))
    swap[np.where(d % ROPE < half, d + half, d - half), d] = 1.0
    put("swap", swap)
    half2 = ROPE2 // 2
    swap2 = np.zeros((P, P))
    turned = d % HD < ROPE2
    swap2[np.where(d % HD < half2, d + half2, d - half2)[turned], d[turned]] = 1.0
    put("swap2", swap2)
    inv = (1.0 / (10000.0 ** (np.arange(0, ROPE, 2, dtype=np.float32) / np.float32(ROPE)))).astype(np.float32)
    ang = np.arange(T, dtype=np.float32)[None, :] * inv[d % half][:, None]
    put("cos", np.cos(ang))
    put("sin", np.sin(ang) * np.where(d % ROPE < half, -1.0, 1.0)[:, None])
    put("upto", np.concatenate([(np.arange(P)[:, None] + t * P <= k) for t in range(TT)], axis=1))
    pick = np.zeros((P, HEADS))
    pick[0:HEADS] = pick[32:32 + HEADS] = np.eye(HEADS) * HD ** 0.5
    put("pick", pick)
    put("rms_eps", np.full((P, 1), RMS_EPS))
    put("ln_eps", np.full((P, 1), LN_EPS))
    freq = np.float32(500000.0) ** (-np.arange(0, ROPE2, 2, dtype=np.float32) / np.float32(ROPE2))
    put("freq2", np.where(turned, freq[d % half2], 0.0)[:, None])
    put("sign2", np.where(turned, np.where(d % HD < half2, -1.0, 1.0), 0.0)[:, None])
    return c


def conformer_mla_fox_dsa_moba_kernel(nc, w_stream, vec_dram, const_dram, x_dram, pos_dram, out_dram):
    with ExitStack() as ctx:
        def sb(name, shape, dt=F32):
            return ctx.enter_context(nc.sbuf_tensor(name, shape, dt))

        def sem(name):
            return ctx.enter_context(nc.semaphore(name))

        staged = sb("staged", [P, 2, UNIT])
        w_hi = sb("w_hi", [P, 2, UNIT], F16)
        w_lo = sb("w_lo", [P, 2, UNIT], F16)
        vec = sb("vec", [P, VCOLS])
        cst = sb("cst", [P, CCOLS])
        h = sb("h", [P, DC, T])
        m = sb("m", [P, DC, T])
        sq = sb("sq", [P, DC, T])
        xn = sb("xn", [P, DC, T])
        x_hi = sb("x_hi", [P, DC, T], F16)
        x_lo = sb("x_lo", [P, DC, T], F16)
        f_hi = sb("f_hi", [P, FC, T], F16)
        f_lo = sb("f_lo", [P, FC, T], F16)
        qT = sb("qT", [P, 12, T])
        kT = sb("kT", [P, 9, T])
        val = f_lo[:, FC // 2:, :].rearrange("p c t -> p (c t)").bitcast(F32).rearrange("p (t d) -> p t d", t=TT)
        stat = sb("stat", [P, 4, T])
        tmp = sb("tmp", [P, 4, T])
        pad = sb("pad", [P, 2, TAPS2 - 1 + T])
        cos2 = sb("cos2", [P, T])
        sin2 = sb("sin2", [P, T])
        posi = sb("posi", [P, T], I32)
        scores = sb("scores", [P, 2, SPAN])
        probs = sb("probs", [P, 3, SPAN])
        probsT = sb("probsT", [P, 2, SPAN])
        peak = sb("peak", [P, 2, 8])
        idx = sb("idx", [P, 2, SPAN])
        sel = sb("sel", [P, SPAN])
        top8 = sb("top8", [P, 2, 8])
        gates = sb("gates", [P, TT, 12])
        logf = sb("logf", [P, 5, TT * HEADS])
        DECAY = 32 + HEADS
        logf_rows = sb("logf_rows", [P, TT, 32 + HEADS])
        decay_q = xn
        decay_k = sb("decay_k", [P, T])
        ckvt = sb("ckvt", [P, TT, P])
        u_pad = f_hi[:].rearrange("p c t -> p (c t)").bitcast(F32)[:, 0:DC * (TAPS - 1 + T)].rearrange(
            "p (c t) -> p c t", c=DC)
        conv = xn
        diags = [f_lo[:].rearrange("p c t -> p (c t)").bitcast(F32), qT[:].rearrange("p c t -> p (c t)")]
        DIAGS = (FC * T // 2 + 12 * T) // P

        def diagonal(n):
            n %= DIAGS
            first = FC * T // 2 // P
            return diags[0][:, P * n:P * n + P] if n < first else diags[1][:, P * (n - first):P * (n - first) + P]

        ps = ctx.enter_context(nc.psum_tensor("ps", [P, 8, 512], F32))
        STAT = ps[:, 7, 0:T]

        def v(name, i=0, n=1):
            return vec[:, VCOL[name] + i:VCOL[name] + i + n]

        def k(name, n=None):
            n = n or dict(CONSTANTS)[name]
            return cst[:, CCOL[name]:CCOL[name] + n]

        loaded = sem("loaded")
        late_loaded = sem("late_loaded")
        landed_early = sem("landed_early")
        landed = [sem("landed_0"), sem("landed_1")]
        hi_split = sem("hi_split")
        lo_split = sem("lo_split")
        squared = sem("squared")
        m_squared = sem("m_squared")
        m_added = sem("m_added")
        x_loaded = sem("x_loaded")
        pos_loaded = sem("pos_loaded")
        conv_product = sem("conv_product")
        conv_added = sem("conv_added")
        conv_started = sem("conv_started")
        pool_diag = sem("pool_diag")
        act_diag = sem("act_diag")
        diag_used = sem("diag_used")
        conv_drained = sem("conv_drained")
        summed = sem("summed")
        inverted = sem("inverted")
        rooted = sem("rooted")
        scaled = sem("scaled")
        x_hi_ready = sem("x_hi_ready")
        x_lo_ready = sem("x_lo_ready")
        act_step = sem("act_step")
        dve_step = sem("dve_step")
        h_ready = {n: sem(f"h_ready_{n}") for n in ("mix_0", "ffn_0", "mix_1", "ffn_1", "oute", "down_0",
                                                   "outo", "down_1")}
        product = {n: sem(f"{n}_product") for n, _ in STREAM}
        drained = {n: sem(f"{n}_drained") for n, _ in STREAM if n not in h_ready}
        u_product = [sem(f"u_{i}_product") for i in range(2)]
        u_drained = [sem(f"u_{i}_drained") for i in range(2)]
        for n in ("oute", "outo", "down_0", "down_1"):
            drained[n] = h_ready[n]
        out_written = sem("out_written")
        stored = sem("stored")
        pads_zero = sem("pads_zero")
        glu = sem("glu")
        conv_ready = sem("conv_ready")
        ln_mean = sem("ln_mean")
        ln_centred = sem("ln_centred")
        ln_squared = sem("ln_squared")
        ln_var = sem("ln_var")
        ln_inverted = sem("ln_inverted")
        ln_rooted = sem("ln_rooted")
        ln_scaled = sem("ln_scaled")
        f_squared = [sem(f"f_squared_{i}") for i in range(2)]
        f_hi_ready = [sem(f"f_hi_ready_{i}") for i in range(2)]
        f_lo_ready = [sem(f"f_lo_ready_{i}") for i in range(2)]
        g_padded = [sem(f"g_padded_{i}") for i in range(2)]
        g_tap = [sem(f"g_tap_{i}") for i in range(2)]
        g_conv = [sem(f"g_conv_{i}") for i in range(2)]
        g_silu = [sem(f"g_silu_{i}") for i in range(2)]
        p_hi_ready = [sem(f"p_hi_ready_{i}") for i in range(2)]
        p_lo_ready = [sem(f"p_lo_ready_{i}") for i in range(2)]
        swapped = sem("swapped")
        turned = sem("turned")
        tables = sem("tables")
        sines = sem("sines")
        ckv_turned = sem("ckv_turned")
        ckv_rows = sem("ckv_rows")
        forget_exp = sem("forget_exp")
        forget_sum = sem("forget_sum")
        forget_log = sem("forget_log")
        fox_logf = sem("fox_logf")
        fox_cum = sem("fox_cum")
        decay_zero = sem("decay_zero")
        decay_picked = sem("decay_picked")
        fox_cum_ready = sem("fox_cum_ready")
        q_lat = sem("q_lat")
        q_lat_ready = sem("q_lat_ready")
        dots = sem("dots")
        dots_relu = sem("dots_relu")
        dots_added = sem("dots_added")
        selected = sem("selected")
        A = {n: {s: sem(f"{n}_{s}") for s in ("scores", "peak", "exp", "norm", "turn", "probsT", "out", "o_hi", "o_lo")}
             for n in ("mla", "even", "moba")}
        q_in = sem("q_in")
        q_in_hi = sem("q_in_hi")
        q_in_lo = sem("q_in_lo")
        o_lat = sem("o_lat")
        o_up = sem("o_up")

        qlatT = m

        def at64(b, c, head, t0, n):
            r = 64 * (head % 2)
            return b[r:r + 64, c, t0:t0 + n]

        def mla_terms(hd, t):
            n = P * (t + 1)
            return [(qT[:, hd, P * t:P * t + P], kT[:, hd, 0:n]),
                    (at64(qT, 8 + hd // 2, hd, P * t, P), at64(kT, 8, hd, 0, n))]

        def fox_terms(hd, t):
            n = P * (t + 1)
            return [(at64(qT, hd // 2, hd, P * t, P), at64(kT, hd // 2, hd, 0, n)),
                    (decay_q[:, hd, P * t:P * t + P], decay_k[:, 0:n])]

        def dsa_terms(hd, t):
            n = P * (t + 1)
            return [(qlatT[:, hd, P * t:P * t + P], kT[:, 5, 0:n]),
                    (at64(qT, 4 + hd // 2, hd, P * t, P), at64(qT, 11, hd, 0, n))]

        def moba_terms(hd, t):
            n = P * (t + 1)
            return [(at64(qT, hd // 2, hd, P * t, P), at64(kT, hd // 2, hd, 0, n))]

        def even_terms(hd, t):
            return fox_terms(hd, t) if hd < HEADS else dsa_terms(hd - HEADS, t)

        KINDS = {
            "mla": dict(heads=HEADS, latent=HEADS, terms=mla_terms, mask=lambda hd: k("mla_mask"), pair=False,
                        scale=float(NOPE + ROPE) ** -0.5, v=lambda hd, t: val[:, t, P * hd:P * hd + P]),
            "even": dict(heads=2 * HEADS, latent=HEADS, terms=even_terms, pair=True, scale=HD ** -0.5,
                         mask=lambda hd: k("causal") if hd < HEADS else sel[:],
                         v=lambda hd, t: val[:, t, HD * hd:HD * hd + HD] if hd < HEADS else ckvt[:, t, :]),
            "moba": dict(heads=MOBA_HEADS, latent=MOBA_HEADS, terms=moba_terms, mask=lambda hd: k("causal"), pair=True,
                         scale=HD ** -0.5, v=lambda hd, t: val[:, t, HD * hd:HD * hd + HD]),
        }

        def out_of(kind, hd):
            if KINDS[kind]["pair"]:
                return hd // 2, hd % 2 == 1
            return hd, True

        def ended(kind, i):
            H, latent = KINDS[kind]["heads"], KINDS[kind]["latent"]
            found = []
            for hd in (i - OUT_LAG - 1, i - OUT_LAG - 1 - UP_LAG):
                if 0 <= hd < H and (hd >= latent) == (hd == i - OUT_LAG - 1 - UP_LAG):
                    c, whole = out_of(kind, hd)
                    if whole:
                        found.append((c, c % 2 if hd >= latent else (7, 3)[c % 2], hd))
            return found

        def length(kind):
            H, latent = KINDS[kind]["heads"], KINDS[kind]["latent"]
            return H + OUT_LAG + 1 + UP_LAG * (latent < H)

        ROPES = {"mla": [(kT, 8), (qT, 8), (qT, 9), (qT, 10), (qT, 11)],
                 "even": [(qT, c) for c in (8, 9, 10, 11, 4, 5, 6, 7)],
                 "odd": [(b, c) for b in (qT, kT) for c in range(8)]}
        ROPE_AT = {"mla": 0, "even": 5, "odd": 13}

        block = ctx.enter_context(nc.Block())

        @block.sync
        def _(sp):
            sp.dma_start(h[:], x_dram).then_inc(x_loaded, 16)
            early = CCOL["mla_mask"]
            sp.dma_start(cst[:, 0:early], const_dram[:, 0:early]).then_inc(loaded, 16)
            sp.dma_start(vec[:], vec_dram).then_inc(loaded, 16)

            def load(u, s):
                sp.dma_start(staged[:, s:s + 1, :], w_stream[bass.ds(u, 1)].rearrange("u p n -> p u n")).then_inc(
                    landed[s], 16)

            for e in range(2):
                half = slice(HALF * e, HALF * e + HALF)
                sp.dma_start(staged[:, 0, half], w_stream[0, :, half]).then_inc((landed_early, landed[0])[e], 16)
            load(1, 1)
            sp.dma_start(cst[:, early:], const_dram[:, early:]).then_inc(late_loaded, 16)
            sp.dma_start(posi[:], pos_dram).then_inc(pos_loaded, 16)
            with sp.Fori(0, UNITS // 2 - 1) as i:
                for s in range(2):
                    sp.wait_ge(lo_split, i * 4 + 2 * s + 2)
                    load(i * 2 + 2 + s, s)
            for u in range(UNITS // 2 * 2, UNITS):
                sp.wait_ge(lo_split, 2 * (u - 2) + 2)
                load(u, u % 2)
            for c in range(DC):
                sp.wait_ge(out_written, c + 1)
                sp.dma_start(out_dram[:, c, :], xn[:, c, :]).then_inc(stored, 16)
            sp.wait_ge(stored, 16 * DC)

        @block.tensor
        def _(pe):
            def weights(s, o, n):
                return w_hi[:, s, o:o + n], w_lo[:, s, o:o + n]

            def features(out, s, o, kc, xh, xl, fresh=None):
                for c in range(kc):
                    if fresh:
                        fresh(c)
                    wh, wl = weights(s, o + P * c, P)
                    pe.matmul(out, wh, xh[:, c, :], start=(c == 0), stop=False)
                    pe.matmul(out, wh, xl[:, c, :], start=False, stop=False)
                    last = pe.matmul(out, wl, xh[:, c, :], start=False, stop=(c == kc - 1))
                return last

            def rows(out, s, o, n, kc, xh, xl, t):
                for c in range(kc):
                    wh, wl = weights(s, o + n * c, n)
                    tok = slice(P * t, P * t + P)
                    pe.matmul(out, xh[:, c, tok], wh, start=(c == 0), stop=False)
                    pe.matmul(out, xh[:, c, tok], wl, start=False, stop=False)
                    last = pe.matmul(out, xl[:, c, tok], wh, start=False, stop=(c == kc - 1))
                return last

            def bank(name, n):
                if n >= RING:
                    pe.wait_ge(drained[name], n - RING + 1)
                return n % RING

            def arrived(g):
                pe.wait_ge(lo_split, g + 1)

            def normed(name):
                def fresh(c):
                    pe.wait_ge(x_lo_ready, SPLIT_AT[name] + c + 1)
                return fresh

            def sums(name):
                i = NORM_AT[name]
                n = NORM_CHUNKS[name]
                if i:
                    pe.wait_ge(rooted, i)
                if name in ADDED_AT:
                    pe.wait_ge(m_added, ADDED_AT[name] + n)
                    pe.matmul(STAT, k("ones"), stat[:, 3, :], start=True, stop=True).then_inc(summed, 1)
                    return
                for c in range(n):
                    pe.wait_ge(squared, SQUARE_AT[name] + c + 1)
                    last = pe.matmul(STAT, k("ones"), sq[:, c, :], start=(c == 0), stop=(c == n - 1))
                last.then_inc(summed, 1)

            def hidden(ready, n):
                def fresh(c):
                    if c % 8 == 0 or c == n - 2:
                        pe.wait_ge(ready, n if c == n - 2 else min(c + 8, n - 2))
                return fresh

            def linear(name, per_unit, kc, xh, xl, fresh, chunks=None):
                u0 = FIRST[name]
                units = dict(STREAM)[name]
                n = 0
                for u in range(u0, u0 + units):
                    for j in range(per_unit):
                        if j in (0, (per_unit + 1) // 2):
                            arrived(2 * u + (j > 0))
                        b = bank(name, n)
                        features(ps[:, b, 0:T], u % 2, j * kc * P, kc, xh, xl, fresh if n == 0 else None).then_inc(
                            product[name], 1)
                        n += 1

            def swap(name, i):
                b, c = ROPES[name][i]
                at = ROPE_AT[name] + i
                if at >= 2:
                    pe.wait_ge(turned, at - 1)
                pe.matmul(ps[:, 4 + at % 2, 0:T], k("swap" if name == "mla" else "swap2"), b[:, c, :], start=True,
                          stop=True).then_inc(swapped, 1)

            def attention(kind, start=0, stop=None):
                spec, s = KINDS[kind], A[kind]
                H, latent = spec["heads"], spec["latent"]
                for i in range(start, stop or length(kind)):
                    if i < H:
                        if i >= 2:
                            pe.wait_ge(s["peak"], i - 1)
                        o = ps[:, 4 + i % 2, :]
                        for t in range(TT):
                            terms = spec["terms"](i, t)
                            for n, (a, b) in enumerate(terms):
                                last = pe.matmul(o[:, P * t:P * t + P * (t + 1)], a, b, start=(n == 0),
                                                 stop=(n == len(terms) - 1))
                        last.then_inc(s["scores"], 1)
                    hd = i - TURN_LAG
                    if 0 <= hd < H:
                        pe.wait_ge(s["norm"], hd + 1)
                        if hd >= 2:
                            pe.wait_ge(s["probsT"], hd - 1)
                        o = ps[:, (6, 2)[hd % 2], :]
                        for n in range(3):
                            last = pe.transpose(o[:, P * n:P * n + P], probs[:, hd % 3, P * n:P * n + P], k("ident"))
                        last.then_inc(s["turn"], 1)
                    hd = i - OUT_LAG
                    if 0 <= hd < H:
                        pe.wait_ge(s["probsT"], hd + 1)
                        c, whole = out_of(kind, hd)
                        if hd >= latent:
                            o = ps[:, (7, 3)[hd % 2], 0:T]
                            if hd >= latent + 2:
                                pe.wait_ge(o_lat, hd - latent - 1)
                            else:
                                pe.wait_ge(s["o_lo"], out_of(kind, latent)[0] - 1 + hd - latent)
                        else:
                            r = 64 * (hd % 2) if spec["pair"] else 0
                            rn = 64 if spec["pair"] else P
                            if c >= 2:
                                pe.wait_ge(s["o_lo"], c - 1)
                            o = ps[r:r + rn, (7, 3)[c % 2], 0:T]
                        pT = probsT[:, hd % 2, :]
                        pe.matmul(o, spec["v"](hd, 0), pT[:, 0:T], start=True, stop=False)
                        pe.matmul(o[:, P:T], spec["v"](hd, 1), pT[:, T:SPAN], start=False, stop=True).then_inc(s["out"], 1)
                    hd = i - OUT_LAG - UP_LAG
                    if latent <= hd < H:
                        pe.wait_ge(o_lat, hd - latent + 1)
                        c, whole = out_of(kind, hd)
                        if c >= latent // 2 + 2:
                            pe.wait_ge(s["o_lo"], c - 1)
                        r = 64 * (hd % 2)
                        pe.matmul(ps[r:r + 64, c % 2, 0:T], v("w_uv2", HD * (hd - latent), HD), tmp[:, hd % 2, :], start=True,
                                  stop=True).then_inc(o_up, 1)

            pe.wait_ge(loaded, 32)
            sums("mix_pre_0")
            linear("pw1", 4, DC, x_hi, x_lo, normed("mix_pre_0"))
            def mean(chunks, ends=False):
                for n, c in enumerate(chunks):
                    if c in CONV_VECTOR:
                        pe.wait_ge(conv_ready, CONV_VECTOR.index(c) + 1)
                    elif c in CONV_POOL:
                        pe.wait_ge(conv_added, (CONV_POOL.index(c) + 1) * (TAPS - 1))
                    else:
                        pe.wait_ge(conv_drained, CONV_TENSOR.index(c) + 1)
                    last = pe.matmul(STAT, k("ones"), conv[:, c, :], start=(c == 1), stop=(ends and n == len(chunks) - 1))
                if ends:
                    last.then_inc(ln_mean, 1)

            for q, c in enumerate(CONV_TENSOR):
                pe.wait_ge(glu, c + 1)
                for tap in range(TAPS):
                    n = TAPS * q + tap
                    if n < DIAGS:
                        pe.wait_ge(pool_diag, n + 1)
                    else:
                        pe.wait_ge(act_diag, n - DIAGS + 1)
                    pe.matmul(ps[:, 4 + q, 0:T], diagonal(n), u_pad[:, c, tap:tap + T], start=(tap == 0),
                              stop=(tap == TAPS - 1)).then_inc(diag_used, 1)
                if q == 1:
                    mean((1, 3, 0, 2))
            mean((5, 4, 7, 6), True)
            for c in range(DC):
                pe.wait_ge(ln_squared, c + 1)
                last = pe.matmul(STAT, k("ones"), sq[:, c, :], start=(c == 0), stop=(c == DC - 1))
            last.then_inc(ln_var, 1)
            linear("pw2", 4, DC, x_hi, x_lo, normed("layer_norm"))
            sums("mix_post_0")

            def mlp(layer):
                sums(f"ffn_pre_{layer}")
                one, two = f"ff1_{layer}", f"ff2_{layer}"
                pe.sem_inc(drained[one], RING)
                u0 = FIRST[one]
                with pe.Fori(0, dict(STREAM)[one] // 2) as i:
                    for s in range(2):
                        for j in range(4):
                            if j % 2 == 0:
                                pe.wait_ge(lo_split, i * 4 + (2 * (u0 + s) + j // 2 + 1))
                            n = 4 * s + j
                            pe.wait_ge(drained[one], i * 8 + (n + 1))
                            features(ps[:, n % RING, 0:T], (u0 + s) % 2, j * DC * P, DC, x_hi, x_lo,
                                     None if n else normed(f"ffn_pre_{layer}")).then_inc(product[one], 1)
                pe.wait_ge(drained[one], RING + FC - RING + 2)
                pe.sem_inc(drained[two], 2)
                u0 = FIRST[two]
                with pe.Fori(0, dict(STREAM)[two] // 2) as i:
                    for s in range(2):
                        pe.wait_ge(lo_split, i * 4 + (2 * (u0 + s) + 2))
                        pe.wait_ge(drained[two], i * 2 + (s + 1))
                        features(ps[:, s, 0:T], (u0 + s) % 2, 0, FC, f_hi, f_lo,
                                 None if s else hidden(f_lo_ready[layer], FC)).then_inc(product[two], 1)
                sums(f"ffn_post_{layer}")

            mlp(0)

            pe.wait_ge(late_loaded, 16)
            sums("mix_pre_1")
            linear("kv", 3, DC, f_hi, f_lo, normed("mix_pre_1"))
            u = FIRST["dq"]
            for j in range(3):
                if j != 1:
                    arrived(2 * u + j // 2)
                features(ps[:, 4 + j, 0:T], u % 2, j * D, DC, x_hi, x_lo,
                         None if j else lambda c: pe.wait_ge(q_in_lo, c + 1)).then_inc(product["dq"], 1)
                if j == 0:
                    sums("kv_norm")
            u = FIRST["ukv"]
            arrived(2 * u)
            pe.wait_ge(x_lo_ready, SPLIT_AT["kv_norm"] + KV_RANK // P)
            pe.wait_ge(drained["kv"], 3)
            n = 0
            for j in range(HEADS):
                b = bank("ukv", n)
                features(ps[:, b, 0:T], u % 2, 2 * P * j, 2, f_hi[:, 8:10], f_lo[:, 8:10]).then_inc(product["ukv"], 1)
                n += 1
                if j == 2:
                    sums("q_norm")
                if j == 3:
                    pe.wait_ge(drained["dq"], 3)
                    swap("mla", 0)
            arrived(2 * u + 1)
            for half in range(2):
                for t in range(TT):
                    b = bank("ukv", n)
                    for c in range(2):
                        o = HALF + D * c + 512 * half
                        wh, wl = weights(u % 2, o, 512)
                        xh, xl = (y[:, 8 + c, P * t:P * t + P] for y in (f_hi, f_lo))
                        pe.matmul(ps[:, b, :], xh, wh, start=(c == 0), stop=False)
                        pe.matmul(ps[:, b, :], xh, wl, start=False, stop=False)
                        last = pe.matmul(ps[:, b, :], xl, wh, start=False, stop=(c == 1))
                    last.then_inc(product["ukv"], 1)
                    n += 1
            u = FIRST["uq"]
            pe.wait_ge(x_lo_ready, SPLIT_AT["q_norm"] + Q_RANK // P)
            for j in range(12):
                if j in (0, 5, 10):
                    arrived(2 * u + (0, 1, 2)[(0, 5, 10).index(j)])
                if j < RING:
                    pe.wait_ge(drained["ukv"], 12 - RING + j + 1)
                b = bank("uq", j)
                s, o = ((u % 2, 384 * j) if j < 5 else (u % 2, HALF + 384 * (j - 5)) if j < 10 else
                        ((u + 1) % 2, 384 * (j - 10)))
                features(ps[:, b, 0:T], s, o, 3, f_hi[:, 10:13], f_lo[:, 10:13]).then_inc(product["uq"], 1)
                if 2 <= j < 6:
                    pe.wait_ge(drained["uq"], j - 1)
                    swap("mla", j - 1)
                if j == 9:
                    pe.wait_ge(turned, 5)
                    pe.wait_ge(drained["uq"], 6)
                    attention("mla", 0, 2)
            pe.wait_ge(drained["uq"], 12)
            attention("mla", 2)
            fresh_o = lambda c: pe.wait_ge(A["mla"]["o_lo"], c + 1)
            linear("wo", 4, DC, x_hi, x_lo, fresh_o)
            sums("mix_post_1")
            mlp(1)

            sums("attn_0")
            u0 = FIRST["even"]
            fresh = normed("attn_0")

            def chunk(n, j, at):
                u = u0 + j
                features(ps[:, bank("even", n), 0:T], u % 2, at, DC, x_hi, x_lo, fresh if n == 0 else None).then_inc(
                    product["even"], 1)

            def turn_chunk(i, n):
                pe.wait_ge(drained["even"], n + 1)
                swap("even", i)

            def dot(i):
                if i >= 2:
                    pe.wait_ge(dots_relu, i - 1)
                o = ps[:, 4 + i % 2, :]
                for t in range(TT):
                    last = pe.matmul(o[:, P * t:P * t + P * (t + 1)], at64(qT, 8 + i // 2, i, P * t, P),
                                     at64(qT, 10, i, 0, P * (t + 1)), start=True, stop=True)
                last.then_inc(dots, 1)

            def latent_query(hd):
                pe.wait_ge(turned, ROPE_AT["even"] + 5 + hd // 2)
                if hd >= 2:
                    pe.wait_ge(q_lat_ready, hd - 1)
                elif hd == 0:
                    pe.wait_ge(fox_cum_ready, 1)
                else:
                    pe.wait_ge(ckv_rows, 1)
                r = 64 * (hd % 2)
                pe.matmul(ps[:, 6 + hd % 2, 0:T], vec[r:r + 64, VCOL["w_uk2"] + P * (hd // 2):VCOL["w_uk2"] + P * (hd // 2) + P],
                          qT[r:r + 64, 4 + hd // 2, :], start=True, stop=True).then_inc(q_lat, 1)

            for n in range(4):
                if n % 2 == 0:
                    arrived(2 * u0 + n // 2)
                chunk(n, 0, n * D)
                if n >= 2:
                    turn_chunk(n - 2, n - 2)
            arrived(2 * (u0 + 1))
            chunk(4, 1, 0)
            turn_chunk(2, 2)
            for t in range(TT):
                rows(ps[:, bank("even", 5 + t), 0:12], (u0 + 1) % 2, D, 12, DC, x_hi, x_lo, t).then_inc(product["even"], 1)
            turn_chunk(3, 4)
            sums("g_ckv")
            for n in range(7, 11):
                if n % 2:
                    arrived(2 * (u0 + 2) + (n - 7) // 2)
                chunk(n, 2, (n - 7) * D)
                if n == 8:
                    pe.wait_ge(turned, ROPE_AT["even"] + 4)
                    dot(0)
                    dot(1)
                if n == 9:
                    dot(2)
                    dot(3)
            pe.wait_ge(fox_logf, 1)
            for t in range(TT):
                last = pe.matmul(ps[0:DECAY, 6, 0:T], logf_rows[:, t, :], k("upto")[:, T * t:T * t + T], start=(t == 0),
                                 stop=(t == TT - 1))
            last.then_inc(fox_cum, 1)
            pe.wait_ge(dots_relu, IDX_HEADS)
            turn_chunk(4, 7)
            for n in range(11, 15):
                if n % 2:
                    arrived(2 * (u0 + 3) + (n - 11) // 2)
                chunk(n, 3, (n - 11) * D)
                if n < 14:
                    turn_chunk(n - 6, n - 3)
                if n == 12:
                    pe.wait_ge(scaled, SCALE_AT["g_ckv"] + 1)
                    for t in range(TT):
                        last = pe.transpose(ps[:, 7, P * t:P * t + P], kT[:, 5, P * t:P * t + P], k("ident"))
                    last.then_inc(ckv_turned, 1)
            latent_query(0)
            latent_query(1)
            arrived(2 * (u0 + 4) + 1)
            for t in range(TT):
                rows(ps[:, bank("even", 15 + t), :], (u0 + 4) % 2, 0, 512, DC, x_hi, x_lo, t).then_inc(product["even"], 1)
                latent_query(2 + 2 * t)
                latent_query(3 + 2 * t)
            for n in range(17, 21):
                if n % 2:
                    arrived(2 * (u0 + 5) + (n - 17) // 2)
                chunk(n, 5, (n - 17) * D)
                if n == 17:
                    latent_query(6)
                    latent_query(7)
                if n == 19:
                    pe.wait_ge(drained["even"], 18)
                    pe.wait_ge(decay_picked, 1)
                    attention("even", 0, 2)
            pe.wait_ge(drained["even"], 21)
            pe.wait_ge(q_lat_ready, HEADS)
            attention("even", 2)
            fresh_o = lambda c: pe.wait_ge(A["even"]["o_lo"], c + 1)
            pe.wait_ge(A["even"]["o_lo"], DC - 1)
            linear("oute", 4, DC, x_hi, x_lo, fresh_o)

            def glu_mlp(layer):
                sums(f"ffn2_{layer}")
                up, down = f"up_{layer}", f"down_{layer}"
                pe.sem_inc(drained[up], 2)
                pe.sem_inc(u_drained[layer], 2)
                u0, units = FIRST[up], dict(STREAM)[up]

                def unit(i, s):
                    for j in range(2):
                        pe.wait_ge(lo_split, i * 4 + (2 * (u0 + s) + j + 1))
                        n = 2 * s + j
                        sl = (u0 + s) % 2
                        pe.wait_ge(drained[up], i * 4 + (n + 1))
                        features(ps[:, j, 0:T], sl, 2 * j * DC * P, DC, x_hi, x_lo,
                                 None if n else normed(f"ffn2_{layer}")).then_inc(product[up], 1)
                        pe.wait_ge(u_drained[layer], i * 4 + (n + 1))
                        features(ps[:, 2 + j, 0:T], sl, (2 * j + 1) * DC * P, DC, x_hi, x_lo).then_inc(
                            u_product[layer], 1)

                with pe.Fori(0, units // 2) as i:
                    unit(i, 0)
                    unit(i, 1)
                unit(units // 2, 0)
                pe.wait_ge(drained[up], 2 + GC)
                pe.sem_inc(drained[down], 2)
                u0 = FIRST[down]
                with pe.Fori(0, dict(STREAM)[down] // 2) as i:
                    for s in range(2):
                        pe.wait_ge(lo_split, i * 4 + (2 * (u0 + s) + 2))
                        pe.wait_ge(drained[down], i * 2 + (s + 1))
                        features(ps[:, s, 0:T], (u0 + s) % 2, 0, GC, f_hi, f_lo,
                                 None if s else hidden(p_lo_ready[layer], GC)).then_inc(product[down], 1)

            glu_mlp(0)
            sums("attn_1")
            u0 = FIRST["odd"]
            fresh = normed("attn_1")
            for n in range(16):
                if n % 2 == 0:
                    arrived(2 * u0 + n // 2)
                features(ps[:, bank("odd", n), 0:T], (u0 + n // 4) % 2, n % 4 * DC * P, DC, x_hi, x_lo,
                         fresh if n == 0 else None).then_inc(product["odd"], 1)
                if n >= 2:
                    pe.wait_ge(drained["odd"], n - 1)
                    swap("odd", n - 2)
            for half in range(2):
                u = u0 + 4 + half
                arrived(2 * u + 1)
                for t in range(TT):
                    rows(ps[:, bank("odd", 16 + 2 * half + t), :], u % 2, 0, 512, DC, x_hi, x_lo, t).then_inc(
                        product["odd"], 1)
                    if not half:
                        pe.wait_ge(drained["odd"], 15 + t)
                        swap("odd", 14 + t)
                    elif not t:
                        pe.wait_ge(turned, ROPE_AT["odd"] + 16)
                        attention("moba", 0, 2)
            pe.wait_ge(drained["odd"], 20)
            attention("moba", 2)
            fresh_o = lambda c: pe.wait_ge(A["moba"]["o_lo"], c + 1)
            linear("outo", 4, DC, x_hi, x_lo, fresh_o)
            glu_mlp(1)
            sums("final")

        @block.scalar
        def _(act):
            steps = [0]

            def chain(ins):
                steps[0] += 1
                ins.then_inc(act_step, 1)
                act.wait_ge(act_step, steps[0])

            def hi(g, s, at):
                o = HALF * (g % 2)
                if g:
                    act.wait_ge(landed[s], at)
                act.activation(w_hi[:, s, o:o + HALF], staged[:, s, o:o + HALF], ACT.Copy, scale=SW).then_inc(hi_split, 1)

            def split(g):
                if g == 0:
                    act.wait_ge(landed_early, 16)
                if g < HALVES:
                    hi(g, g // 2 % 2, 16 * (g // 4 + (g > 0)))

            def quarter(g, q):
                o = HALF * (g % 2) + QUARTER * q
                act.wait_ge(landed[g // 2 % 2], 16 * (g // 4 + 1))
                ins = act.activation(w_hi[:, g // 2 % 2, o:o + QUARTER], staged[:, g // 2 % 2, o:o + QUARTER], ACT.Copy,
                                     scale=SW)
                if q == 3:
                    ins.then_inc(hi_split, 1)

            def squares(name, src, ready):
                for c in range(NORM_CHUNKS[name]):
                    ready(c)
                    act.activation(sq[:, c, :], src[:, c, :], ACT.Square).then_inc(squared, 1)

            def root(name):
                act.wait_ge(summed, NORM_AT[name] + 1)
                act.activation(stat[:, 0, :], STAT, ACT.Sqrt, bias=k("rms_eps"),
                               scale=1.0 / (P * NORM_CHUNKS[name])).then_inc(rooted, 1)

            def his(name, dst):
                base = SCALE_AT[name]
                for c in range(NORM_CHUNKS[name]):
                    act.wait_ge(scaled, base + c + 1)
                    act.activation(dst[:, c, :], xn[:, c, :], ACT.Copy, scale=SX).then_inc(x_hi_ready, 1)

            def evac(name, n, dst, scale=INV, cols=T):
                act.wait_ge(product[name], n + 1)
                act.activation(dst, ps[:, n % RING, 0:cols], ACT.Copy, scale=scale).then_inc(drained[name], 1)

            def behind(name):
                for n in range(1, DC - 2, 2):
                    act.wait_ge(product[name], n + 1)
                    split(2 * FIRST[name] + n // 2 + 4)

            def last_behind(name):
                act.wait_ge(product[name], DC)
                split(2 * FIRST[name] + 7)

            def attention(kind, start=0, stop=None):
                spec, s = KINDS[kind], A[kind]
                H, latent = spec["heads"], spec["latent"]
                for i in range(start, stop or length(kind)):
                    if i < H:
                        act.wait_ge(s["peak"], i + 1)
                        if i >= 3:
                            act.wait_ge(s["turn"], i - 2)
                        b = i % 2
                        for t in range(TT):
                            sl = slice(P * t, P * t + P * (t + 1))
                            last = act.activation(probs[:, i % 3, sl], scores[:, b, sl], ACT.Exp, bias=peak[:, b, 2 + t:3 + t],
                                                  accum_out=peak[:, b, 4 + t:5 + t])
                        last.then_inc(s["exp"], 1)
                    hd = i - TURN_LAG
                    if 0 <= hd < H:
                        act.wait_ge(s["turn"], hd + 1)
                        if hd >= 2:
                            act.wait_ge(s["out"], hd - 1)
                        act.activation(probsT[:, hd % 2, :], ps[:, (6, 2)[hd % 2], 0:SPAN], ACT.Copy).then_inc(
                            s["probsT"], 1)
                    hd = i - OUT_LAG - 1
                    if latent <= hd < H:
                        act.wait_ge(s["out"], hd + 1)
                        if hd >= latent + 2:
                            act.wait_ge(o_up, hd - latent - 1)
                        act.activation(tmp[:, hd % 2, :], ps[:, (7, 3)[hd % 2], 0:T], ACT.Copy).then_inc(o_lat, 1)
                    for c, b, hd in ended(kind, i):
                        if hd >= latent:
                            act.wait_ge(o_up, hd - latent + 1)
                        else:
                            act.wait_ge(s["out"], hd + 1)
                        act.activation(x_hi[:, c, :], ps[:, b, 0:T], ACT.Copy, scale=SX).then_inc(s["o_hi"], 1)
                    for g, q in spread(kind, i, False):
                        quarter(g, q)

            act.wait_ge(x_loaded, 16)
            squares("mix_pre_0", h, lambda c: None)
            split(0)
            root("mix_pre_0")
            his("mix_pre_0", x_hi)
            for g in range(1, 4):
                split(g)
            act.wait_ge(loaded, 32)
            todo = [(c, tap) for c in CONV_POOL for tap in range(TAPS)]

            def taps(count, chunks):
                for _ in range(count):
                    if not todo or todo[0][0] >= chunks:
                        return
                    c, tap = todo.pop(0)
                    if tap == 0:
                        act.wait_ge(glu, c + 1)
                        act.activation(conv[:, c, :], u_pad[:, c, 0:T], ACT.Identity, bias=v("b_dw", c),
                                       scale=v("taps", c)).then_inc(conv_started, 1)
                        continue
                    n = CONV_POOL.index(c) * (TAPS - 1) + tap - 1
                    if n >= 4:
                        act.wait_ge(conv_added, n - 3)
                    act.activation(tmp[:, n % 4, :], u_pad[:, c, tap:tap + T], ACT.Copy,
                                   scale=v("taps", DC * tap + c)).then_inc(conv_product, 1)

            u0 = FIRST["pw1"]
            for j in range(DC):
                act.wait_ge(product["pw1"], 2 * j + 1)
                if j >= 2:
                    act.wait_ge(glu, j - 1)
                act.activation(m[:, 2 * (j % 2), :], ps[:, 2 * j % RING, 0:T], ACT.Sigmoid, bias=v("b_pw1", DC + j),
                               scale=INV).then_inc(drained["pw1"], 1)
                act.wait_ge(product["pw1"], 2 * j + 2)
                act.activation(m[:, 2 * (j % 2) + 1, :], ps[:, (2 * j + 1) % RING, 0:T], ACT.Identity,
                               bias=v("b_pw1", j), scale=INV).then_inc(drained["pw1"], 1)
                split(2 * u0 + j + 4)
                if j:
                    taps(4, j)
            taps(TAPS * len(CONV_POOL), DC)
            made = DIAGS
            for q, c in enumerate(CONV_TENSOR):
                while made < min(TAPS * (q + 2) + DIAGS // 2, TAPS * len(CONV_TENSOR)):
                    act.wait_ge(diag_used, made - DIAGS + 1)
                    act.activation(diagonal(made), k("ident"), ACT.Copy,
                                   scale=v("taps", DC * (made % TAPS) + CONV_TENSOR[made // TAPS])).then_inc(act_diag, 1)
                    made += 1
                act.wait_ge(diag_used, TAPS * (q + 1))
                act.activation(conv[:, c, :], ps[:, 4 + q, 0:T], ACT.Identity, bias=v("b_dw", c)).then_inc(
                    conv_drained, 1)
            for c in range(DC):
                act.wait_ge(ln_centred, c + 1)
                act.activation(sq[:, c, :], conv[:, c, :], ACT.Square).then_inc(ln_squared, 1)
            act.wait_ge(ln_var, 1)
            act.activation(stat[:, 2, :], STAT, ACT.Sqrt, bias=k("ln_eps"), scale=1.0 / D).then_inc(ln_rooted, 1)
            for c in range(DC):
                act.wait_ge(ln_scaled, c + 1)
                chain(act.activation(xn[:, c, :], xn[:, c, :], ACT.Silu, bias=v("ln_b", c), scale=v("ln_g", c)))
                act.activation(x_hi[:, c, :], xn[:, c, :], ACT.Copy, scale=SX).then_inc(x_hi_ready, 1)
            behind("pw2")
            root("mix_post_0")
            last_behind("pw2")

            def mlp(layer):
                one, two = f"ff1_{layer}", f"ff2_{layer}"
                squares(f"ffn_pre_{layer}", h, lambda c: act.wait_ge(h_ready[f"mix_{layer}"], c + 1))
                root(f"ffn_pre_{layer}")
                his(f"ffn_pre_{layer}", x_hi)
                if layer == 0:
                    act.wait_ge(tables, 1)
                    act.activation(tmp[:, 2, :], tmp[:, 0, :], ACT.Sin).then_inc(sines, 1)
                    act.activation(tmp[:, 3, :], tmp[:, 0, :], ACT.Sin, scale=0.5).then_inc(sines, 1)
                u0 = FIRST[one]
                with act.Fori(0, dict(STREAM)[one] // 2) as i:
                    for n in range(8):
                        act.wait_ge(product[one], i * 8 + (n + 1))
                        act.wait_ge(f_squared[layer], i * 8 + (n + 1))
                        act.activation(tmp[:, n % 2, :], ps[:, n % RING, 0:T], ACT.Relu, scale=INV).then_inc(drained[one], 1)
                        act.wait_ge(drained[one], i * 8 + (n + 1 + RING))
                        act.activation(f_hi[:, bass.ds(i * 8 + n, 1), :], tmp[:, n % 2:n % 2 + 1, :], ACT.Square,
                                       scale=SF ** 0.5).then_inc(f_hi_ready[layer], 1)
                        if n % 2 == 1:
                            g = 2 * u0 + n // 2 + 4
                            hi(g, g // 2 % 2, i * 16 + 16 * (g // 4 + 1))
                u0, units = FIRST[two], dict(STREAM)[two]

                def unit(i, s):
                    act.wait_ge(product[two], i * 2 + (s + 1))
                    for e in range(2):
                        g = 2 * (u0 + s) + e + 4
                        hi(g, g // 2 % 2, i * 16 + 16 * (g // 4 + 1))

                with act.Fori(0, units // 2 - 1) as i:
                    unit(i, 0)
                    unit(i, 1)
                unit(units // 2 - 1, 0)
                root(f"ffn_post_{layer}")

            def last_halves(name, e):
                u = FIRST[name] + dict(STREAM)[name] - 1
                act.wait_ge(product[name], dict(STREAM)[name])
                split(2 * u + e + 4)

            mlp(0)
            last_halves("ff2_0", 0)
            squares("mix_pre_1", h, lambda c: act.wait_ge(h_ready["ffn_0"], c + 1))
            root("mix_pre_1")
            for c in range(DC):
                act.wait_ge(scaled, SCALE_AT["mix_pre_1"] + c + 1)
                act.activation(f_hi[:, c, :], xn[:, c, :], ACT.Copy, scale=SX).then_inc(x_hi_ready, 1)
            for c in range(DC):
                act.wait_ge(q_in, c + 1)
                act.activation(x_hi[:, c, :], m[:, c, :], ACT.Copy, scale=SX).then_inc(q_in_hi, 1)
            last_halves("ff2_0", 1)
            u0 = FIRST["kv"]
            act.wait_ge(product["kv"], 2)
            split(2 * u0 + 4)
            squares("kv_norm", kT, lambda c: act.wait_ge(drained["kv"], c + 1))
            act.wait_ge(product["kv"], 3)
            split(2 * u0 + 5)
            u0 = FIRST["dq"]

            def latent(n):
                act.wait_ge(product["dq"], n + 1)
                act.activation(qT[:, n, :], ps[:, 4 + n, 0:T], ACT.Copy, scale=INV).then_inc(drained["dq"], 1)

            def square_latent(n):
                act.wait_ge(drained["dq"], n + 1)
                act.activation(sq[:, n, :], qT[:, n, :], ACT.Square).then_inc(squared, 1)

            latent(0)
            root("kv_norm")
            latent(1)
            square_latent(0)
            square_latent(1)
            his("kv_norm", f_hi[:, 8:10])
            latent(2)
            square_latent(2)
            split(2 * u0 + 4)
            u0 = FIRST["ukv"]
            for n in range(8):
                evac("ukv", n, kT[:, n, :])
                if n == 2:
                    root("q_norm")
                if n == 5:
                    his("q_norm", f_hi[:, 10:13])
                    split(2 * FIRST["dq"] + 5)
            split(2 * u0 + 4)
            for n in range(8, 12):
                half, t = (n - 8) // 2, (n - 8) % 2
                evac("ukv", n, val[:, t, 512 * half:512 * half + 512], cols=512)
            split(2 * u0 + 5)
            u0 = FIRST["uq"]
            for n in range(12):
                evac("uq", n, qT[:, (n + 8) % 12, :])
                if n in (4, 9):
                    split(2 * u0 + 4 + n // 9)
                if n == 10:
                    attention("mla", 0, 1)
            attention("mla", 1)
            behind("wo")
            root("mix_post_1")
            last_behind("wo")
            mlp(1)
            last_halves("ff2_1", 0)
            squares("attn_0", h, lambda c: act.wait_ge(h_ready["ffn_1"], c + 1))
            root("attn_0")
            his("attn_0", x_hi)
            last_halves("ff2_1", 1)
            u0 = FIRST["even"]

            def weighted(i):
                act.wait_ge(dots, i + 1)
                if i >= 2:
                    act.wait_ge(dots_added, i - 1)
                act.activation(scores[:, i % 2, :], ps[:, 4 + i % 2, 0:SPAN], ACT.Relu,
                               scale=float(HD) ** -0.5 * float(IDX_HEADS) ** -0.5).then_inc(dots_relu, 1)

            def latent_query(hd):
                act.wait_ge(q_lat, hd + 1)
                act.activation(qlatT[:, hd, :], ps[:, 6 + hd % 2, 0:T], ACT.Copy).then_inc(q_lat_ready, 1)

            place = ([(qT, 8), (qT, 9), (qT, 10), (kT, 4), (qT, 11), None, None] + [(qT, c) for c in range(4, 8)] +
                     [(kT, c) for c in range(4)] + [None, None] + [(qT, c) for c in range(4)])
            splits = 0
            for n in range(21):
                if n in (5, 6):
                    evac("even", n, gates[:, n - 5, :], cols=12)
                elif n in (15, 16):
                    evac("even", n, val[:, n - 15, 0:512], cols=512)
                else:
                    evac("even", n, place[n][0][:, place[n][1], :])
                if n == 3:
                    squares("g_ckv", kT[:, 4:5], lambda c: act.wait_ge(drained["even"], 4))
                if n == 7:
                    root("g_ckv")
                    act.wait_ge(forget_sum, 1)
                    act.activation(logf[:, 2, :], logf[:, 1, :], ACT.Exp, scale=-1.0).then_inc(forget_exp, 1)
                if n == 8:
                    act.wait_ge(forget_sum, 2)
                    act.activation(logf[:, 1, :], logf[:, 3, :], ACT.Ln).then_inc(forget_log, 1)
                for _ in range({1: 1, 3: 1, 6: 2, 8: 1, 10: 1, 12: 1, 14: 1}.get(n, 0)):
                    split(2 * u0 + splits + 4)
                    splits += 1
                if n in (9, 10):
                    weighted(2 * n - 18)
                    weighted(2 * n - 17)
                if n == 12:
                    act.wait_ge(ckv_turned, 1)
                    act.activation(ckvt[:].rearrange("p t r -> p (t r)"), ps[:, 7, 0:T], ACT.Copy).then_inc(ckv_rows, 1)
                if 14 <= n < 18:
                    latent_query(2 * n - 28)
                    latent_query(2 * n - 27)
                if n == 20:
                    attention("even", 0, 2)
            attention("even", 2)
            behind("oute")

            def glu_mlp(layer, last_stage):
                up, down = f"up_{layer}", f"down_{layer}"
                root(f"ffn2_{layer}")
                his(f"ffn2_{layer}", x_hi)
                last_behind(("oute", "outo")[layer])
                u0, units = FIRST[up], dict(STREAM)[up]

                def pair(i, n, parts=(True, True)):
                    old, new = parts
                    j = n % 2
                    g = 2 * u0 + n + 3
                    if old and new:
                        act.wait_ge(u_product[layer], i * 4 + n)
                        hi(g, g // 2 % 2, i * 16 + 16 * (g // 4 + 1))
                    if new:
                        act.wait_ge(product[up], i * 4 + (n + 1))
                        act.wait_ge(g_conv[layer], i * 4 + (n + 1))
                        act.activation(pad[:, j, TAPS2 - 1:TAPS2 - 1 + T], ps[:, j, 0:T], ACT.Copy, scale=INV).then_inc(
                            drained[up], 1)
                    if old:
                        act.wait_ge(u_drained[layer], i * 4 + (n + 2))
                        act.activation(f_hi[:, bass.ds(i * 4 + (n - 1), 1), :], tmp[:, 3 - j:4 - j, :], ACT.Copy,
                                       scale=SF).then_inc(p_hi_ready[layer], 1)
                    if old and not new:
                        act.wait_ge(u_product[layer], i * 4 + n)
                        hi(g, g // 2 % 2, i * 16 + 16 * (g // 4 + 1))
                    if new:
                        act.wait_ge(g_conv[layer], i * 4 + (n + 3))
                        act.activation(tmp[:, j, :], tmp[:, j, :], ACT.Silu).then_inc(g_silu[layer], 1)

                pair(0, 0, (False, True))
                pair(0, 1)
                with act.Fori(0, (GC - 2) // 4) as i:
                    for n in range(2, 6):
                        pair(i, n)
                pair(0, GC, (True, False))
                u0, units = FIRST[down], dict(STREAM)[down]

                def unit(i, s):
                    act.wait_ge(product[down], i * 2 + (s + 1))
                    for e in range(2):
                        g = 2 * (u0 + s) + e + 4
                        hi(g, g // 2 % 2, i * 16 + 16 * (g // 4 + 1))

                with act.Fori(0, units // 2 - 1) as i:
                    unit(i, 0)
                    unit(i, 1)
                if not last_stage:
                    unit(units // 2 - 1, 0)

            glu_mlp(0, False)
            root("attn_1")
            his("attn_1", x_hi)
            last_halves("down_0", 0)
            last_halves("down_0", 1)
            u0 = FIRST["odd"]
            for n in range(16):
                evac("odd", n, (qT, kT)[n // 8][:, n % 8, :])
                if n % 2:
                    split(2 * u0 + n // 2 + 4)
            for n in range(16, 20):
                half, t = (n - 16) // 2, n % 2
                evac("odd", n, val[:, t, 512 * half:512 * half + 512], cols=512)
                if n == 17:
                    split(2 * u0 + 8 + 4)
                if n == 18:
                    attention("moba", 0, 2)
            attention("moba", 2)
            behind("outo")
            glu_mlp(1, True)
            root("final")

        @block.gpsimd
        def _(pool):
            pool.wait_ge(loaded, 32)
            for n in range(DIAGS):
                pool.tensor_scalar(diagonal(n), k("ident"), v("taps", DC * (n % TAPS) + CONV_TENSOR[n // TAPS]), None,
                                   ALU.mult).then_inc(pool_diag, 1)
            n = 0
            for q, c in enumerate(CONV_POOL):
                pool.wait_ge(conv_started, q + 1)
                for tap in range(1, TAPS):
                    pool.wait_ge(conv_product, n + 1)
                    if tap > 1:
                        pool.wait_ge(conv_added, n)
                    pool.tensor_tensor(conv[:, c, :], conv[:, c, :], tmp[:, n % 4, :], ALU.add).then_inc(conv_added, 1)
                    n += 1
            pool.wait_ge(late_loaded, 16)
            pool.wait_ge(x_lo_ready, SPLIT_AT["attn_0"] + DC)
            pool.memset(decay_q[:], 0.0).then_inc(decay_zero, 1)
            pool.wait_ge(decay_zero, 1)
            pool.tensor_copy(decay_q[0:HEADS, :, :], cst[0:HEADS, CCOL["pick"]:CCOL["pick"] + HEADS].unsqueeze(2).to_broadcast(
                [HEADS, HEADS, T])).then_inc(decay_picked, 1)

        @block.vector
        def _(dve):
            steps = [0]

            def step(ins):
                steps[0] += 1
                ins.then_inc(dve_step, 1)
                return steps[0]

            def chain(ins):
                dve.wait_ge(dve_step, step(ins))

            def lo(s, e, at):
                o = HALF * e
                dve.wait_ge(hi_split, at)
                dve.scalar_tensor_tensor(w_lo[:, s, o:o + HALF], staged[:, s, o:o + HALF], SW, w_hi[:, s, o:o + HALF],
                                         ALU.mult, ALU.subtract).then_inc(lo_split, 1)

            def split(g):
                if g < HALVES:
                    lo(g // 2 % 2, g % 2, g + 1)

            def invert(name):
                dve.wait_ge(rooted, NORM_AT[name] + 1)
                dve.reciprocal(stat[:, 1, :], stat[:, 0, :]).then_inc(inverted, 1)

            def x_lows(name, c, dst):
                dve.wait_ge(x_hi_ready, SPLIT_AT[name] + c + 1)
                dve.scalar_tensor_tensor(dst[1][:, c, :], xn[:, c, :], SX, dst[0][:, c, :], ALU.mult,
                                         ALU.subtract).then_inc(x_lo_ready, 1)

            def scale(name, src, gain, dst):
                n = NORM_CHUNKS[name]
                dve.wait_ge(inverted, NORM_AT[name] + 1)
                for c in range(n + 1):
                    if c < n:
                        dve.scalar_tensor_tensor(xn[:, c, :], src[:, c, :], v(gain, c), stat[:, 1, :], ALU.mult,
                                                 ALU.mult).then_inc(scaled, 1)
                    if c:
                        x_lows(name, c - 1, dst)

            def post(name, ready):
                dve.wait_ge(inverted, NORM_AT[name] + 1)
                done = []
                for c in range(DC + 1):
                    if c < DC:
                        done.append(step(dve.scalar_tensor_tensor(m[:, c, :], m[:, c, :], v(name, c), stat[:, 1, :],
                                                                  ALU.mult, ALU.mult)))
                    if c:
                        dve.wait_ge(dve_step, done[c - 1])
                        dve.tensor_tensor(h[:, c - 1, :], h[:, c - 1, :], m[:, c - 1, :], ALU.add).then_inc(
                            h_ready[ready], 1)

            def evac(name, n, dst, scale=INV):
                dve.wait_ge(product[name], n + 1)
                dve.tensor_scalar(dst, ps[:, n % RING, 0:T], scale, None, ALU.mult).then_inc(drained[name], 1)

            def add_square(src, c, at, loop=None):
                i, per = loop or (0, 0)
                dve.tensor_tensor(sq[:, c:c + 1, :], src, src, ALU.mult).then_inc(m_squared, 1)
                dve.wait_ge(m_squared, i * per + (at + 1))
                if at:
                    dve.wait_ge(m_added, i * per + at)
                dve.tensor_tensor(stat[:, 3:4, :], stat[:, 3:4, :], sq[:, c:c + 1, :], ALU.add).then_inc(m_added, 1)

            def into_m(name, norm):
                u0 = FIRST[name]
                chain(dve.memset(stat[:, 3, :], 0.0))
                for n in range(DC):
                    if name == "pw2":
                        dve.wait_ge(product[name], n + 1)
                        dve.tensor_scalar(m[:, n, :], ps[:, n % RING, 0:T], INV, v("b_pw2", n), ALU.mult,
                                          ALU.add).then_inc(drained[name], 1)
                    else:
                        evac(name, n, m[:, n, :])
                    dve.wait_ge(drained[name], n + 1)
                    add_square(m[:, n:n + 1, :], n % 2, ADDED_AT[norm] + n)
                    if n % 2 and n < DC - 1:
                        split(2 * u0 + n // 2 + 4)

            def into_h(name, norm):
                u0 = FIRST[name]
                chain(dve.memset(stat[:, 3, :], 0.0))
                for n in range(DC):
                    dve.wait_ge(product[name], n + 1)
                    dve.scalar_tensor_tensor(h[:, n, :], ps[:, n % RING, 0:T], INV, h[:, n, :], ALU.mult,
                                             ALU.add).then_inc(h_ready[name], 1)
                    dve.wait_ge(h_ready[name], n + 1)
                    add_square(h[:, n:n + 1, :], n % 2, ADDED_AT[norm] + n)
                    if n % 2 and n < DC - 1:
                        split(2 * u0 + n // 2 + 4)

            def rope(name, i):
                c_tab, s_tab = (k("cos"), k("sin")) if name == "mla" else (cos2[:], sin2[:])
                b, c = ROPES[name][i]
                at = ROPE_AT[name] + i
                dve.wait_ge(swapped, at + 1)
                t = tmp[:, 2 + at % 2, :]
                step(dve.tensor_tensor(t, ps[:, 4 + at % 2, 0:T], s_tab, ALU.mult))
                chain(dve.tensor_tensor(b[:, c, :], b[:, c, :], c_tab, ALU.mult))
                dve.tensor_tensor(b[:, c, :], b[:, c, :], t, ALU.add).then_inc(turned, 1)

            def quarter(g, q):
                o = HALF * (g % 2) + QUARTER * q
                dve.wait_ge(hi_split, g + 1)
                at = (slice(None), g // 2 % 2, slice(o, o + QUARTER))
                ins = dve.scalar_tensor_tensor(w_lo[at], staged[at], SW, w_hi[at], ALU.mult, ALU.subtract)
                if q == 3:
                    ins.then_inc(lo_split, 1)

            def attention(kind):
                spec, s = KINDS[kind], A[kind]
                H = spec["heads"]
                for i in range(length(kind)):
                    if i < H:
                        b = i % 2
                        dve.wait_ge(s["scores"], i + 1)
                        if i >= 2:
                            dve.wait_ge(s["exp"], i - 1)
                        for t in range(TT):
                            sl = slice(P * t, P * t + P * (t + 1))
                            last = step(dve.tensor_tensor_reduce(scores[:, b, sl], ps[:, 4 + b, sl], spec["mask"](i)[:, sl],
                                                                 spec["scale"], TAKEN, ALU.add, ALU.max,
                                                                 peak[:, b, t:t + 1]))
                        dve.wait_ge(dve_step, last)
                        dve.tensor_scalar(peak[:, b, 2:4], peak[:, b, 0:2], -1.0, None, ALU.mult).then_inc(s["peak"], 1)
                    hd = i - 1
                    if 0 <= hd < H:
                        b = hd % 2
                        dve.wait_ge(s["exp"], hd + 1)
                        chain(dve.reciprocal(peak[:, b, 6:8], peak[:, b, 4:6]))
                        for t in range(TT):
                            sl = slice(P * t, P * t + P * (t + 1))
                            last = dve.tensor_scalar(probs[:, hd % 3, sl], probs[:, hd % 3, sl], peak[:, b, 6 + t:7 + t], None,
                                                     ALU.mult)
                        last.then_inc(s["norm"], 1)
                    for c, b, hd in ended(kind, i):
                        dve.wait_ge(s["o_hi"], c + 1)
                        dve.scalar_tensor_tensor(x_lo[:, c, :], ps[:, b, 0:T], SX, x_hi[:, c, :], ALU.mult,
                                                 ALU.subtract).then_inc(s["o_lo"], 1)
                    for g, q in spread(kind, i - 4, i == length(kind) - 1):
                        quarter(g, q)

            def angles():
                turn1 = 6.28125
                turn2 = float((np.array([2 * np.pi - 6.28125], np.float32).view(np.uint32) & np.uint32(0xFFFFF000)).view(
                    np.float32)[0])
                turn3 = float(np.float32(2 * np.pi - 6.28125 - turn2))
                whole = 1.5 * 2.0 ** 23
                dve.wait_ge(pos_loaded, 16)
                dve.wait_ge(late_loaded, 16)
                chain(dve.tensor_copy(sq[:, 0, :], posi[:]))
                chain(dve.tensor_scalar(sq[:, 1, :], sq[:, 0, :], k("freq2"), None, ALU.mult))
                chain(dve.tensor_scalar(sq[:, 2, :], sq[:, 1, :], float(1.0 / (2 * np.pi)), whole, ALU.mult, ALU.add))
                chain(dve.tensor_scalar(sq[:, 3, :], sq[:, 2, :], whole, None, ALU.subtract))
                chain(dve.scalar_tensor_tensor(sq[:, 1, :], sq[:, 3, :], -turn1, sq[:, 1, :], ALU.mult, ALU.add))
                chain(dve.scalar_tensor_tensor(sq[:, 1, :], sq[:, 3, :], -turn2, sq[:, 1, :], ALU.mult, ALU.add))
                chain(dve.scalar_tensor_tensor(sq[:, 1, :], sq[:, 3, :], -turn3, sq[:, 1, :], ALU.mult, ALU.add))
                dve.tensor_scalar(tmp[:, 0, :], sq[:, 1, :], 3.1415925, -3.1415925, ALU.min, ALU.max).then_inc(tables, 1)
                dve.wait_ge(sines, 2)
                step(dve.tensor_scalar(sin2[:], tmp[:, 2, :], k("sign2"), None, ALU.mult))
                chain(dve.tensor_tensor(cos2[:], tmp[:, 3, :], tmp[:, 3, :], ALU.mult))
                chain(dve.tensor_scalar(cos2[:], cos2[:], -2.0, 1.0, ALU.mult, ALU.add))

            dve.memset(pad[:], 0.0)
            dve.memset(logf_rows[:], 0.0)
            chain(dve.memset(decay_k[:], 0.0))
            step(dve.memset(decay_k[32:DECAY, :], 1.0))
            step(dve.memset(u_pad, 0.0))
            dve.wait_ge(loaded, 32)
            split(0)
            invert("mix_pre_0")
            scale("mix_pre_0", h, "mix_pre_0", (x_hi, x_lo))
            for g in range(1, 4):
                split(g)
            lanes, waiting, behind_tap = [], list(CONV_VECTOR), {}

            def taps(count, chunks):
                for _ in range(count):
                    while len(lanes) < 2 and waiting and waiting[0] < chunks:
                        lanes.append([waiting.pop(0), 0])
                    if not lanes:
                        return
                    c, tap = lanes[0]
                    if tap == 0:
                        dve.wait_ge(glu, c + 1)
                        behind_tap[c] = step(dve.tensor_scalar(conv[:, c, :], u_pad[:, c, 0:T], v("taps", c),
                                                               v("b_dw", c), ALU.mult, ALU.add))
                    else:
                        dve.wait_ge(dve_step, behind_tap[c])
                        ins = dve.scalar_tensor_tensor(conv[:, c, :], u_pad[:, c, tap:tap + T], v("taps", DC * tap + c),
                                                       conv[:, c, :], ALU.mult, ALU.add)
                        if tap < TAPS - 1:
                            behind_tap[c] = step(ins)
                        else:
                            ins.then_inc(conv_ready, 1)
                    lanes[0][1] += 1
                    if tap == TAPS - 1:
                        lanes.pop(0)
                    else:
                        lanes.append(lanes.pop(0))

            u0 = FIRST["pw1"]
            for j in range(DC):
                dve.wait_ge(drained["pw1"], 2 * j + 2)
                dve.tensor_tensor(u_pad[:, j, TAPS - 1:TAPS - 1 + T], m[:, 2 * (j % 2), :], m[:, 2 * (j % 2) + 1, :],
                                  ALU.mult).then_inc(glu, 1)
                split(2 * u0 + j + 4)
                if j:
                    taps(7, j)
            taps(TAPS * DC, DC)
            dve.wait_ge(ln_mean, 1)
            dve.wait_ge(conv_ready, len(CONV_VECTOR))
            chain(dve.tensor_scalar(stat[:, 0, :], STAT, 1.0 / D, None, ALU.mult))
            for c in range(DC):
                dve.tensor_tensor(conv[:, c, :], conv[:, c, :], stat[:, 0, :], ALU.subtract).then_inc(ln_centred, 1)
            dve.wait_ge(ln_rooted, 1)
            dve.reciprocal(stat[:, 1, :], stat[:, 2, :]).then_inc(ln_inverted, 1)
            dve.wait_ge(ln_inverted, 1)
            dve.wait_ge(ln_centred, DC)
            for c in range(DC + 1):
                if c < DC:
                    dve.tensor_tensor(conv[:, c, :], conv[:, c, :], stat[:, 1, :], ALU.mult).then_inc(ln_scaled, 1)
                if c:
                    x_lows("layer_norm", c - 1, (x_hi, x_lo))
            into_m("pw2", "mix_post_0")
            invert("mix_post_0")
            post("mix_post_0", "mix_0")
            split(2 * FIRST["pw2"] + 7)

            def mlp(layer):
                one, two = f"ff1_{layer}", f"ff2_{layer}"
                invert(f"ffn_pre_{layer}")
                scale(f"ffn_pre_{layer}", h, f"ffn_pre_{layer}", (x_hi, x_lo))
                if layer == 0:
                    angles()
                dve.sem_inc(f_squared[layer], 2)
                u0 = FIRST[one]
                with dve.Fori(0, dict(STREAM)[one] // 2) as i:
                    for n in range(8):
                        r, f = tmp[:, n % 2, :], tmp[:, 2 + n % 2:3 + n % 2, :]
                        dve.wait_ge(drained[one], i * 8 + (n + 1 + RING))
                        dve.tensor_tensor(tmp[:, 2 + n % 2, :], r, r, ALU.mult).then_inc(f_squared[layer], 1)
                        dve.wait_ge(f_hi_ready[layer], i * 8 + (n + 1))
                        dve.wait_ge(f_squared[layer], i * 8 + (n + 3))
                        dve.scalar_tensor_tensor(f_lo[:, bass.ds(i * 8 + n, 1), :], f, SF,
                                                 f_hi[:, bass.ds(i * 8 + n, 1), :], ALU.mult, ALU.subtract).then_inc(
                            f_lo_ready[layer], 1)
                        if n % 2 == 1:
                            g = 2 * u0 + n // 2 + 4
                            lo(g // 2 % 2, g % 2, i * 4 + (g + 1))
                u0 = FIRST[two]
                chain(dve.memset(stat[:, 3, :], 0.0))

                def unit(i, s, splits=True):
                    dve.wait_ge(product[two], i * 2 + (s + 1))
                    mc = m[:, bass.ds(i * 2 + s, 1), :]
                    dve.tensor_scalar(mc, ps[:, s:s + 1, 0:T], INVF, None, ALU.mult).then_inc(drained[two], 1)
                    dve.wait_ge(drained[two], i * 2 + (s + 3))
                    add_square(mc, s, ADDED_AT[f"ffn_post_{layer}"] + s, (i, 2))
                    for e in range(2 * splits):
                        g = 2 * (u0 + s) + e + 4
                        lo(g // 2 % 2, e, i * 4 + (g + 1))

                last = dict(STREAM)[two] // 2 - 1
                with dve.Fori(0, last) as i:
                    unit(i, 0)
                    unit(i, 1)
                unit(last, 0)
                unit(last, 1, False)
                invert(f"ffn_post_{layer}")
                post(f"ffn_post_{layer}", f"ffn_{layer}")
                split(2 * (u0 + 2 * last + 1) + 4)

            mlp(0)
            invert("mix_pre_1")
            scale("mix_pre_1", h, "kv_in", (f_hi, f_lo))
            for c in range(DC + 1):
                if c < DC:
                    dve.scalar_tensor_tensor(m[:, c, :], h[:, c, :], v("mix_pre_1", c), stat[:, 1, :], ALU.mult,
                                             ALU.mult).then_inc(q_in, 1)
                if c:
                    dve.wait_ge(q_in_hi, c)
                    dve.scalar_tensor_tensor(x_lo[:, c - 1, :], m[:, c - 1, :], SX, x_hi[:, c - 1, :], ALU.mult,
                                             ALU.subtract).then_inc(q_in_lo, 1)
            split(2 * FIRST["kv"] + 3)
            u0 = FIRST["kv"]
            evac("kv", 0, kT[:, 0, :])
            evac("kv", 1, kT[:, 1, :])
            split(2 * u0 + 4)
            evac("kv", 2, kT[:, 8, :])
            split(2 * u0 + 5)
            invert("kv_norm")
            scale("kv_norm", kT, "kv_norm", (f_hi[:, 8:10], f_lo[:, 8:10]))
            split(2 * FIRST["dq"] + 4)
            invert("q_norm")
            scale("q_norm", qT, "q_norm", (f_hi[:, 10:13], f_lo[:, 10:13]))
            rope("mla", 0)
            split(2 * FIRST["dq"] + 5)
            for e in range(2):
                split(2 * FIRST["ukv"] + 4 + e)
            for i in range(1, 5):
                rope("mla", i)
            u0 = FIRST["uq"]
            split(2 * u0 + 4)
            split(2 * u0 + 5)
            attention("mla")
            into_m("wo", "mix_post_1")
            invert("mix_post_1")
            post("mix_post_1", "mix_1")
            split(2 * FIRST["wo"] + 7)
            mlp(1)

            invert("attn_0")
            scale("attn_0", h, "attn_0", (x_hi, x_lo))
            split(2 * FIRST["even"] + 3)
            u0 = FIRST["even"]
            split(2 * u0 + 4)
            rope("even", 0)
            split(2 * u0 + 5)
            rope("even", 1)
            rope("even", 2)
            dve.wait_ge(drained["even"], 7)
            gate = gates[:, :, 0:HEADS]
            bias = v("b_fox", 0, HEADS)
            z = logf[:, 0, :].rearrange("p (t h) -> p t h", t=TT)
            for t in range(TT):
                last = step(dve.tensor_tensor(z[:, t, :], gate[:, t, :], bias, ALU.add))
            dve.wait_ge(dve_step, last)
            dve.scalar_tensor_tensor(logf[:, 1, :], logf[:, 0, :], -1.0, logf[:, 0, :], ALU.mult, ALU.max).then_inc(
                forget_sum, 1)
            rope("even", 3)
            split(2 * u0 + 6)
            split(2 * u0 + 7)
            invert("g_ckv")
            dve.wait_ge(inverted, NORM_AT["g_ckv"] + 1)
            dve.scalar_tensor_tensor(kT[:, 5, :], kT[:, 4, :], v("g_ckv"), stat[:, 1, :], ALU.mult, ALU.mult).then_inc(
                scaled, 1)
            dve.wait_ge(forget_exp, 1)
            dve.tensor_scalar(logf[:, 3, :], logf[:, 2, :], 1.0, None, ALU.add).then_inc(forget_sum, 1)
            dve.wait_ge(forget_sum, 2)
            chain(dve.tensor_scalar(logf[:, 4, :], logf[:, 3, :], 1.0, None, ALU.subtract))
            chain(dve.tensor_tensor(logf[:, 2, :], logf[:, 2, :], logf[:, 4, :], ALU.subtract))
            dve.wait_ge(forget_log, 1)
            chain(dve.reciprocal(logf[:, 4, :], logf[:, 3, :]))
            chain(dve.tensor_tensor(logf[:, 2, :], logf[:, 2, :], logf[:, 4, :], ALU.mult))
            chain(dve.tensor_tensor(logf[:, 2, :], logf[:, 2, :], logf[:, 1, :], ALU.add))
            lost = logf[:, 2, :].rearrange("p (t h) -> p t h", t=TT)
            chain(dve.scalar_tensor_tensor(logf_rows[:, :, 32:DECAY], z, 0.0, lost, ALU.min, ALU.subtract))
            dve.tensor_scalar(logf_rows[:, :, 0:HEADS], logf_rows[:, :, 32:DECAY], -1.0, None, ALU.mult).then_inc(
                fox_logf, 1)
            split(2 * u0 + 8)
            for i in range(IDX_HEADS):
                dve.wait_ge(dots_relu, i + 1)
                if i:
                    dve.wait_ge(dots_added, i)
                for t in range(TT):
                    sl = slice(P * t, P * t + P * (t + 1))
                    w = gates[:, t, HEADS + i:HEADS + i + 1]
                    if i == 0:
                        last = dve.tensor_scalar(idx[:, 0, sl], scores[:, i % 2, sl], w, None, ALU.mult)
                    else:
                        last = dve.scalar_tensor_tensor(idx[:, 0, sl], scores[:, i % 2, sl], w, idx[:, 0, sl], ALU.mult,
                                                        ALU.add)
                last.then_inc(dots_added, 1)
            dve.wait_ge(dots_added, IDX_HEADS)
            chain(dve.tensor_tensor(idx[:, 0, :], idx[:, 0, :], k("causal"), ALU.add))
            split(2 * u0 + 9)
            dve.wait_ge(fox_cum, 1)
            dve.wait_ge(decay_zero, 1)
            step(dve.tensor_copy(decay_k[0:HEADS, :], ps[0:HEADS, 6, 0:T]))
            dve.tensor_tensor(decay_q[32:DECAY, :, :], ps[32:DECAY, 6:7, 0:T].to_broadcast([HEADS, HEADS, T]),
                              cst[32:DECAY, CCOL["pick"]:CCOL["pick"] + HEADS].unsqueeze(2).to_broadcast([HEADS, HEADS, T]),
                              ALU.mult).then_inc(fox_cum_ready, 1)
            rope("even", 4)
            rope("even", 5)
            split(2 * u0 + 10)
            rope("even", 6)
            rope("even", 7)
            for n in range(TOPK // 8):
                a, b = idx[:, n % 2, :], idx[:, (n + 1) % 2, :]
                for t in range(TT):
                    sl = slice(P * t, P * t + P * (t + 1))
                    last = step(dve.max(top8[:, t, :], a[:, sl]))
                dve.wait_ge(dve_step, last)
                for t in range(TT):
                    sl = slice(P * t, P * t + P * (t + 1))
                    last = step(dve.match_replace(b[:, sl], top8[:, t, :], a[:, sl], TAKEN))
                dve.wait_ge(dve_step, last)
                if n == 1:
                    split(2 * u0 + 11)
            chain(dve.tensor_scalar(sel[:], idx[:, TOPK // 8 % 2, :], TAKEN / 2, MASKED, ALU.is_gt, ALU.mult))
            chain(dve.tensor_tensor(sel[:], sel[:], k("causal"), ALU.add))
            attention("even")
            into_h("oute", "ffn2_0")

            def glu_mlp(layer):
                up, down = f"up_{layer}", f"down_{layer}"
                invert(f"ffn2_{layer}")
                scale(f"ffn2_{layer}", h, f"ffn2_{layer}", (x_hi, x_lo))
                split(2 * FIRST[("oute", "outo")[layer]] + 7)
                dve.sem_inc(g_conv[layer], 2)
                u0, units = FIRST[up], dict(STREAM)[up]

                def pair(i, n, parts=(True, True)):
                    old, new = parts
                    j = n % 2
                    y = tmp[:, j, :]
                    if new:
                        dve.wait_ge(drained[up], i * 4 + (n + 3))
                        taps = [vec[:, bass.ds(i * 4 + (VCOL[f"taps2_{layer}"] + GC * q + n), 1)] for q in range(TAPS2)]
                        b = vec[:, bass.ds(i * 4 + (VCOL[f"b_cv_{layer}"] + n), 1)]
                        dve.tensor_scalar(y, pad[:, j, 0:T], taps[0], b, ALU.mult, ALU.add).then_inc(g_tap[layer], 1)
                        dve.wait_ge(g_tap[layer], i * 8 + (2 * n + 1))
                        dve.scalar_tensor_tensor(y, pad[:, j, 1:1 + T], taps[1], y, ALU.mult, ALU.add).then_inc(
                            g_tap[layer], 1)
                        dve.wait_ge(g_tap[layer], i * 8 + (2 * n + 2))
                        dve.scalar_tensor_tensor(y, pad[:, j, 2:2 + T], taps[2], y, ALU.mult, ALU.add).then_inc(
                            g_conv[layer], 1)
                    if old:
                        dve.wait_ge(p_hi_ready[layer], i * 4 + n)
                        at = bass.ds(i * 4 + (n - 1), 1)
                        dve.scalar_tensor_tensor(f_lo[:, at, :], tmp[:, 3 - j:4 - j, :], SF, f_hi[:, at, :], ALU.mult,
                                                 ALU.subtract).then_inc(p_lo_ready[layer], 1)
                        g = 2 * u0 + n + 3
                        lo(g // 2 % 2, g % 2, i * 4 + (g + 1))
                    if new:
                        dve.wait_ge(u_product[layer], i * 4 + (n + 1))
                        dve.wait_ge(g_silu[layer], i * 4 + (n + 1))
                        dve.scalar_tensor_tensor(tmp[:, 2 + j, :], ps[:, 2 + j, 0:T], INV, y, ALU.mult,
                                                 ALU.mult).then_inc(u_drained[layer], 1)

                pair(0, 0, (False, True))
                pair(0, 1)
                with dve.Fori(0, (GC - 2) // 4) as i:
                    for n in range(2, 6):
                        pair(i, n)
                pair(0, GC, (True, False))
                u0, units = FIRST[down], dict(STREAM)[down]
                chain(dve.memset(stat[:, 3, :], 0.0))

                def unit(i, s, splits=True):
                    dve.wait_ge(product[down], i * 2 + (s + 1))
                    hc = h[:, bass.ds(i * 2 + s, 1), :]
                    dve.scalar_tensor_tensor(hc, ps[:, s:s + 1, 0:T], INVF, hc, ALU.mult, ALU.add).then_inc(
                        h_ready[down], 1)
                    dve.wait_ge(h_ready[down], i * 2 + (s + 3))
                    add_square(hc, s, ADDED_AT["final" if layer else "attn_1"] + s, (i, 2))
                    for e in range(2 * splits):
                        g = 2 * (u0 + s) + e + 4
                        lo(g // 2 % 2, e, i * 4 + (g + 1))

                with dve.Fori(0, units // 2 - 1) as i:
                    unit(i, 0)
                    unit(i, 1)
                unit(units // 2 - 1, 0, layer == 0)
                unit(units // 2 - 1, 1, False)

            glu_mlp(0)
            invert("attn_1")
            scale("attn_1", h, "attn_1", (x_hi, x_lo))
            for e in range(2):
                split(2 * FIRST["odd"] + 2 + e)
            for n in range(DC * 2 + 2):
                if n % 2:
                    split(2 * FIRST["odd"] + n // 2 + 4)
                if n >= 2:
                    rope("odd", n - 2)
            attention("moba")
            into_h("outo", "ffn2_1")
            glu_mlp(1)
            invert("final")
            dve.wait_ge(inverted, NORM_AT["final"] + 1)
            for c in range(DC):
                dve.scalar_tensor_tensor(xn[:, c, :], h[:, c, :], v("final", c), stat[:, 1, :], ALU.mult,
                                         ALU.mult).then_inc(out_written, 1)


def columns(w):
    r, n = w.shape
    return list(np.ascontiguousarray(w.reshape(r // P, P, n // P, P).transpose(2, 1, 0, 3)).reshape(n // P, P, r))


def whole(w):
    r, n = w.shape
    return np.ascontiguousarray(w.reshape(r // P, P, n).transpose(1, 0, 2)).reshape(P, r // P * n)


def stream_of(a):
    out = np.zeros((UNITS, P, UNIT), np.float32)

    def put(name, unit, at, blocks):
        for b in blocks:
            out[FIRST[name] + unit, :, at:at + b.shape[1]] = b
            at += b.shape[1]

    def fill(name, chunks, per_unit, first=0):
        for u in range(0, len(chunks), per_unit):
            put(name, first + u // per_unit, 0, chunks[u:u + per_unit])

    def woven(w):
        c = columns(w)
        n = len(c) // 2
        return c[:n], c[n:]

    first, gate = woven(a["conv_w_pw1"][0])
    fill("pw1", [x for g, y in zip(gate, first) for x in (g, y)], 4)
    fill("pw2", columns(a["conv_w_pw2"][0]), 4)
    for layer in range(2):
        fill(f"ff1_{layer}", columns(a["w_ff1"][layer]), 4)
        fill(f"ff2_{layer}", columns(a["w_ff2"][layer]), 1)
    kr = a["kv_w_kr"]
    put("kv", 0, 0, columns(np.concatenate([a["kv_w_dkv"], kr, kr], axis=1)))
    put("dq", 0, 0, columns(a["mla_w_dq"][0]))
    put("ukv", 0, 0, columns(a["kv_w_uk"]))
    put("ukv", 0, HALF, [whole(a["kv_w_uv"])])
    uq = a["mla_w_uq"][0].reshape(Q_RANK, HEADS, NOPE + ROPE)
    uq = columns(np.concatenate([uq[:, :, NOPE:].reshape(Q_RANK, -1), uq[:, :, :NOPE].reshape(Q_RANK, -1)], axis=1))
    put("uq", 0, 0, uq[0:5])
    put("uq", 0, HALF, uq[5:10])
    put("uq", 1, 0, uq[10:12])
    fill("wo", columns(a["mla_w_o"][0]), 4)
    w = a["w_in_even_2"][0]
    wide = HEADS * HD
    fq, fk, fv = (w[:, wide * i:wide * i + wide] for i in range(3))
    ff, w = w[:, 3 * wide:3 * wide + HEADS], w[:, 3 * wide + HEADS:]
    dq, ckv, dkr, iq, ik, iw = np.split(w, np.cumsum([wide, P, ROPE2, IDX_HEADS * HD, HD]), axis=1)
    none = np.zeros((D, HD - ROPE2), np.float32)
    put("even", 0, 0, columns(np.concatenate([iq, ik, ik, ckv], axis=1)))
    put("even", 1, 0, columns(np.concatenate([dkr, none, dkr, none], axis=1)))
    put("even", 1, D, [whole(np.concatenate([ff, iw], axis=1))])
    put("even", 2, 0, columns(dq))
    put("even", 3, 0, columns(fk))
    put("even", 4, 0, [whole(fv)])
    put("even", 5, 0, columns(fq))
    fill("oute", columns(a["w_out_even_2"][0]), 4)
    for layer in range(2):
        g, u = woven(a["w_up_2"][layer])
        fill(f"up_{layer}", [x for pair in zip(g, u) for x in pair], 4)
        fill(f"down_{layer}", columns(a["w_down_2"][layer]), 1)
    w = a["w_in_odd_2"][0]
    fill("odd", columns(w[:, :2 * D]), 4)
    for half in range(2):
        put("odd", 4 + half, 0, [whole(w[:, 2 * D + 512 * half:2 * D + 512 * half + 512])])
    fill("outo", columns(a["w_out_odd_2"][0]), 4)
    return out


def vectors_of(a):
    out = np.zeros((P, VCOLS), np.float32)

    def put(name, value):
        x = np.asarray(value, np.float32).reshape(-1, P).T
        out[:, VCOL[name]:VCOL[name] + x.shape[1]] = x

    for layer in range(2):
        for name in ("mix_pre", "mix_post", "ffn_pre", "ffn_post"):
            put(f"{name}_{layer}", a[f"{name}_g"][layer])
        put(f"attn_{layer}", a["attn_norm_2"][layer])
        put(f"ffn2_{layer}", a["ffn_norm_2"][layer])
        put(f"taps2_{layer}", a["conv_w_2"][layer])
        put(f"b_cv_{layer}", a["conv_b_2"][layer])
    for name, value in (("b_pw1", a["conv_b_pw1"]), ("taps", a["conv_w_dw"]), ("b_dw", a["conv_b_dw"]),
                        ("ln_g", a["conv_ln_g"]), ("ln_b", a["conv_ln_b"]), ("b_pw2", a["conv_b_pw2"]),
                        ("q_norm", a["mla_q_norm_g"]), ("kv_in", a["kv_in_g"]), ("kv_norm", a["kv_norm_g"]),
                        ("final", a["final_norm_2"]), ("g_ckv", a["g_ckv_2"])):
        put(name, value)
    out[:, VCOL["b_fox"]:VCOL["b_fox"] + HEADS] = a["b_fox_f_2"][0]
    uk = np.zeros((HEADS, HD, P), np.float32)
    uk[:, ROPE2:, :] = a["w_uk_2"][0].transpose(1, 2, 0)
    out[:, VCOL["w_uk2"]:VCOL["w_uk2"] + 4 * P] = uk.reshape(4, P, P).transpose(1, 0, 2).reshape(P, 4 * P)
    out[:, VCOL["w_uv2"]:VCOL["w_uv2"] + HEADS * HD] = a["w_uv_2"][0].reshape(P, HEADS * HD)
    return out


def kernel(**inputs):
    import concourse.bacc as bacc
    from concourse.bass_utils import run_bass_kernel_spmd

    a = {name: np.asarray(value) for name, value in inputs.items()}
    arrays = {
        "weights": stream_of(a),
        "vectors": vectors_of(a),
        "constants": constants(),
        "x_turned": np.ascontiguousarray(a["x"][0].T.reshape(DC, P, T).transpose(1, 0, 2)),
        "positions": np.ascontiguousarray(np.broadcast_to(a["positions_2"].reshape(1, T), (P, T))),
    }
    nc = bacc.Bacc("TRN2", target_bir_lowering=False, num_devices=1)
    args = [nc.dram_tensor(n, x.shape, mybir.dt.from_np(x.dtype), kind="ExternalInput").ap() for n, x in arrays.items()]
    args.append(nc.dram_tensor("out", (P, DC, T), F32, kind="ExternalOutput").ap())
    conformer_mla_fox_dsa_moba_kernel(nc, *args)
    got = run_bass_kernel_spmd(nc, [arrays], core_ids=[0]).results[0]["out"]
    return np.ascontiguousarray(got.transpose(1, 0, 2).reshape(D, T).T)[None]
```

```python
from contextlib import ExitStack

import numpy as np

import concourse.bass as bass
from concourse import mybir

P = 128
D = 1024
T = 256
DC = D // P
TT = T // P
D_FF = 4096
FC = D_FF // P
D_FF2 = 2816
GC = D_FF2 // P
TAPS = 31
TAPS2 = 3
HEADS = 8
NOPE, ROPE = 128, 64
Q_RANK, KV_RANK = 384, 256
MOBA_HEADS = 16
HD = 64
ROPE2 = 16
IDX_HEADS = 4
TOPK = T // 4
CHUNK = 64
UNIT = 4096
HALF = UNIT // 2
SW = 256.0
SX = 4.0
SF = 1.0
INV = 1.0 / (SW * SX)
INVF = 1.0 / (SW * SF)
RMS_EPS = 1e-6
LN_EPS = 1e-5
MASKED = -1e30
TAKEN = -3e38
RING = 4
TURN_LAG, OUT_LAG, UP_LAG = 3, 4, 2
BEHIND_LAG = {"mla": 2, "moba": 4}
LOW_LAG = {"mla": 0, "even": 1, "moba": 1}
SPAN = P + T

F32 = mybir.dt.float32
F16 = mybir.dt.float16
I32 = mybir.dt.int32
ALU = mybir.AluOpType
ACT = mybir.ActivationFunctionType

STREAM = [("pw1", 4), ("pw2", 2), ("ff1_0", 8), ("ff2_0", 8), ("kv", 1), ("dq", 1), ("ukv", 1), ("uq", 2),
          ("wo", 2), ("ff1_1", 8), ("ff2_1", 8), ("even", 6), ("oute", 2), ("up_0", 11), ("down_0", 8),
          ("odd", 6), ("outo", 2), ("up_1", 11), ("down_1", 8)]
FIRST = {}
UNITS = 0
for _name, _n in STREAM:
    FIRST[_name] = UNITS
    UNITS += _n
HALVES = 2 * UNITS
USED = {2 * FIRST["kv"] + 1: 3 * D - HALF, 2 * FIRST["dq"] + 1: 3 * D - HALF, 2 * FIRST["uq"]: 5 * Q_RANK,
        2 * FIRST["uq"] + 1: 5 * Q_RANK, 2 * FIRST["uq"] + 2: 2 * Q_RANK, 2 * FIRST["uq"] + 3: 1,
        2 * FIRST["even"] + 2: D + DC * (HEADS + IDX_HEADS), 2 * FIRST["even"] + 3: 1}
QUARTER = HALF // 4
SPREAD = {"mla": (1, 2 * FIRST["uq"] + 5, 2), "even": (0, 2 * FIRST["even"] + 12, 4), "moba": (0, 2 * FIRST["odd"] + 13, 3)}


def spread(kind, step, last):
    first, g, halves = SPREAD[kind]
    n = step - first
    return [(g + q // 4, q % 4) for q in range(max(n, 0), 4 * halves if last else min(n + 1, 4 * halves))]


SCALED_GAINS = ("ffn_pre_0", "mix_pre_1", "kv_in", "ffn_pre_1", "attn_0", "ffn2_0", "attn_1", "ffn2_1")
VECTORS = [*((_name, DC) for _name in SCALED_GAINS), ("mix_pre_0", DC), ("mix_post_0", DC), ("mix_post_1", DC),
           ("ffn_post_0", DC), ("ffn_post_1", DC), ("b_pw1", 2 * DC), ("taps", TAPS * DC),
           ("b_dw", DC), ("ln_g", DC), ("ln_b", DC), ("b_pw2", DC), ("q_norm", Q_RANK // P), ("kv_norm", KV_RANK // P),
           ("final", DC), ("g_ckv", 1), ("taps2_0", TAPS2 * GC), ("taps2_1", TAPS2 * GC), ("b_cv_0", GC),
           ("b_cv_1", GC), ("b_fox", HEADS), ("w_uk2", 4 * P), ("w_uv2", HEADS * HD)]
VCOL = {}
VCOLS = 0
for _name, _n in VECTORS:
    VCOL[_name] = VCOLS
    VCOLS += _n

CONSTANTS = [("ident", P), ("ones", P), ("rms_eps", 1), ("input_eps", 1), ("ln_eps", 1), ("mla_mask", SPAN),
             ("causal", SPAN), ("swap", P), ("swap2", P), ("cos", T), ("sin", T), ("upto", TT * T), ("pick", HEADS), ("freq2", 1), ("sign2", 1)]
CCOL = {}
CCOLS = 0
for _name, _n in CONSTANTS:
    CCOL[_name] = CCOLS
    CCOLS += _n

NORMS = [("mix_pre_0", DC), ("mix_post_0", DC), ("ffn_pre_0", DC), ("ffn_post_0", DC), ("mix_pre_1", DC),
         ("kv_norm", KV_RANK // P), ("q_norm", Q_RANK // P), ("mix_post_1", DC), ("ffn_pre_1", DC),
         ("ffn_post_1", DC), ("attn_0", DC), ("g_ckv", 1), ("ffn2_0", DC), ("attn_1", DC), ("ffn2_1", DC),
         ("final", DC)]
NORM_AT = {}
NORM_CHUNKS = dict(NORMS)
for _i, (_name, _n) in enumerate(NORMS):
    NORM_AT[_name] = _i


def _starts(names):
    at, found = 0, {}
    for name in names:
        found[name] = at
        at += NORM_CHUNKS.get(name, DC)
    return found


LATE = ("ffn_pre_0", "mix_pre_1", "ffn_pre_1", "attn_0", "ffn2_0", "attn_1", "ffn2_1")
LATE_ADDED = ("ffn2_0", "attn_1", "ffn2_1")
POSTS = ("mix_post_0", "ffn_post_0", "mix_post_1", "ffn_post_1")
SCALE_AT = _starts(["mix_pre_0", "kv_norm", "q_norm", "g_ckv"])
SQUARE_AT = _starts(["mix_pre_0", "ffn_pre_0", "mix_pre_1", "kv_norm", "q_norm", "ffn_pre_1", "attn_0", "g_ckv", "ffn2_0",
                     "attn_1", "ffn2_1"])
ADDED_AT = _starts(["mix_post_0", "ffn_post_0", "mix_post_1", "ffn_post_1", "final"])
CONV_VECTOR = (0, 2, 4)
CONV_POOL = (1, 6)
CONV_TENSOR = (3, 5, 7)
SHARED = {CONV_TENSOR[-1]: 9, CONV_POOL[-1]: 5}
TENSOR_TAPS = TAPS * len(CONV_TENSOR) - SHARED[CONV_TENSOR[-1]]
POOL_TAPS = (TAPS - 1) * len(CONV_POOL) - SHARED[CONV_POOL[-1]]
SPLIT_AT = _starts(["mix_pre_0", "layer_norm", "ffn_pre_0", "mix_pre_1", "kv_norm", "q_norm", "ffn_pre_1", "attn_0",
                    "ffn2_0", "attn_1", "ffn2_1"])


def constants():
    c = np.zeros((P, CCOLS), np.float32)

    def put(name, value):
        value = np.asarray(value, np.float32)
        c[:value.shape[0], CCOL[name]:CCOL[name] + value.shape[1]] = value

    put("ident", np.eye(P))
    put("ones", np.ones((P, P)))
    q, k = np.arange(T)[:, None], np.arange(T)[None, :]

    def spans(allowed):
        m = np.where(allowed, 0.0, MASKED)
        return np.concatenate([m[:P, :P], m[P:, :]], axis=1)

    put("mla_mask", spans(k // CHUNK <= q // CHUNK))
    put("causal", spans(k <= q))
    d = np.arange(P)
    half = ROPE // 2
    swap = np.zeros((P, P))
    swap[np.where(d % ROPE < half, d + half, d - half), d] = 1.0
    put("swap", swap)
    half2 = ROPE2 // 2
    swap2 = np.zeros((P, P))
    turned = d % HD < ROPE2
    swap2[np.where(d % HD < half2, d + half2, d - half2)[turned], d[turned]] = 1.0
    put("swap2", swap2)
    inv = (1.0 / (10000.0 ** (np.arange(0, ROPE, 2, dtype=np.float32) / np.float32(ROPE)))).astype(np.float32)
    ang = np.arange(T, dtype=np.float32)[None, :] * inv[d % half][:, None]
    put("cos", np.cos(ang))
    put("sin", np.sin(ang) * np.where(d % ROPE < half, -1.0, 1.0)[:, None])
    put("upto", np.concatenate([(np.arange(P)[:, None] + t * P <= k) for t in range(TT)], axis=1))
    pick = np.zeros((P, HEADS))
    pick[0:HEADS] = pick[32:32 + HEADS] = np.eye(HEADS) * HD ** 0.5
    put("pick", pick)
    put("rms_eps", np.full((P, 1), RMS_EPS))
    put("input_eps", np.full((P, 1), RMS_EPS / INV ** 2))
    put("ln_eps", np.full((P, 1), LN_EPS))
    freq = np.float32(500000.0) ** (-np.arange(0, ROPE2, 2, dtype=np.float32) / np.float32(ROPE2))
    put("freq2", np.where(turned, freq[d % half2], 0.0)[:, None])
    put("sign2", np.where(turned, np.where(d % HD < half2, -1.0, 1.0), 0.0)[:, None])
    return c


def conformer_mla_fox_dsa_moba_kernel(nc, w_stream, vec_dram, const_dram, x_dram, pos_dram, out_dram):
    with ExitStack() as ctx:
        def sb(name, shape, dt=F32):
            return ctx.enter_context(nc.sbuf_tensor(name, shape, dt))

        def sem(name):
            return ctx.enter_context(nc.semaphore(name))

        staged = sb("staged", [P, 2, UNIT])
        w_hi = sb("w_hi", [P, 2, UNIT], F16)
        w_lo = sb("w_lo", [P, 2, UNIT], F16)
        vec = sb("vec", [P, VCOLS])
        cst = sb("cst", [P, CCOLS])
        h = sb("h", [P, DC, T])
        m = sb("m", [P, DC, T])
        sq = sb("sq", [P, DC, T])
        xn = sb("xn", [P, DC, T])
        x_hi = sb("x_hi", [P, DC, T], F16)
        x_lo = sb("x_lo", [P, DC, T], F16)
        f_hi = sb("f_hi", [P, FC, T], F16)
        f_lo = sb("f_lo", [P, FC, T], F16)
        qT = sb("qT", [P, 12, T])
        kT = sb("kT", [P, 9, T])
        val = f_lo[:, FC // 2:, :].rearrange("p c t -> p (c t)").bitcast(F32).rearrange("p (t d) -> p t d", t=TT)
        stat = sb("stat", [P, 5, T])
        tmp = sb("tmp", [P, 4, T])
        pad = sb("pad", [P, 2, TAPS2 - 1 + T])
        cos2 = sb("cos2", [P, T])
        sin2 = sb("sin2", [P, T])
        posi = sb("posi", [P, T], I32)
        scores = sb("scores", [P, 2, SPAN])
        probs = sb("probs", [P, 3, SPAN])
        probsT = sb("probsT", [P, 2, SPAN])
        peak = sb("peak", [P, 2, 8])
        idx = sb("idx", [P, 2, SPAN])
        sel = sb("sel", [P, SPAN])
        top8 = sb("top8", [P, 2, 8])
        gates = sb("gates", [P, TT, 12])
        logf = sb("logf", [P, 5, TT * HEADS])
        DECAY = 32 + HEADS
        logf_rows = sb("logf_rows", [P, TT, 32 + HEADS])
        decay_q = xn
        decay_k = sb("decay_k", [P, T])
        ckvt = sb("ckvt", [P, TT, P])
        late_col = sb("late_col", [P, TT])
        LATE_SCALE = stat[:, 2, :]
        g_in = (f_hi[:, FC - DC:FC], f_lo[:, FC - DC:FC])
        u_pad = f_hi[:].rearrange("p c t -> p (c t)").bitcast(F32)[:, 0:DC * (TAPS - 1 + T)].rearrange(
            "p (c t) -> p c t", c=DC)
        conv = xn
        diags = [f_lo[:].rearrange("p c t -> p (c t)").bitcast(F32), qT[:].rearrange("p c t -> p (c t)")]
        DIAGS = (FC * T // 2 + 12 * T) // P

        def diagonal(n):
            n %= DIAGS
            first = FC * T // 2 // P
            return diags[0][:, P * n:P * n + P] if n < first else diags[1][:, P * (n - first):P * (n - first) + P]

        ps = ctx.enter_context(nc.psum_tensor("ps", [P, 8, 512], F32))
        STAT = ps[:, 7, 0:T]

        def v(name, i=0, n=1):
            return vec[:, VCOL[name] + i:VCOL[name] + i + n]

        def k(name, n=None):
            n = n or dict(CONSTANTS)[name]
            return cst[:, CCOL[name]:CCOL[name] + n]

        loaded = sem("loaded")
        late_loaded = sem("late_loaded")
        landed_early = sem("landed_early")
        landed = [sem("landed_0"), sem("landed_1")]
        hi_split = sem("hi_split")
        lo_split = sem("lo_split")
        squared = sem("squared")
        m_squared = sem("m_squared")
        m_added = sem("m_added")
        x_loaded = sem("x_loaded")
        conv_product = sem("conv_product")
        conv_added = sem("conv_added")
        conv_started = sem("conv_started")
        pool_diag = sem("pool_diag")
        act_diag = sem("act_diag")
        diag_used = sem("diag_used")
        conv_drained = sem("conv_drained")
        summed = sem("summed")
        inverted = sem("inverted")
        rooted = sem("rooted")
        scaled = sem("scaled")
        gains_scaled = sem("gains_scaled")
        pool_added = sem("pool_added")
        col_turned = sem("col_turned")
        col_ready = sem("col_ready")
        normed_rows = sem("normed_rows")
        x_hi_ready = sem("x_hi_ready")
        x_lo_ready = sem("x_lo_ready")
        act_step = sem("act_step")
        dve_step = sem("dve_step")
        h_ready = {n: sem(f"h_ready_{n}") for n in ("mix_0", "ffn_0", "mix_1", "ffn_1", "oute", "down_0",
                                                   "outo", "down_1")}
        product = {n: sem(f"{n}_product") for n, _ in STREAM}
        drained = {n: sem(f"{n}_drained") for n, _ in STREAM if n not in h_ready}
        u_product = [sem(f"u_{i}_product") for i in range(2)]
        u_drained = [sem(f"u_{i}_drained") for i in range(2)]
        for n in ("oute", "outo", "down_0", "down_1"):
            drained[n] = h_ready[n]
        out_written = sem("out_written")
        stored = sem("stored")
        glu = sem("glu")
        conv_ready = sem("conv_ready")
        ln_summed = sem("ln_summed")
        ln_centred = sem("ln_centred")
        ln_squared = sem("ln_squared")
        ln_inverted = sem("ln_inverted")
        ln_rooted = sem("ln_rooted")
        ln_scaled = sem("ln_scaled")
        f_hi_ready = [sem(f"f_hi_ready_{i}") for i in range(2)]
        f_lo_ready = [sem(f"f_lo_ready_{i}") for i in range(2)]
        g_first = [sem(f"g_first_{i}") for i in range(2)]
        g_normed = [sem(f"g_normed_{i}") for i in range(2)]
        g_conv = [sem(f"g_conv_{i}") for i in range(2)]
        g_silu = [sem(f"g_silu_{i}") for i in range(2)]
        p_hi_ready = [sem(f"p_hi_ready_{i}") for i in range(2)]
        p_lo_ready = [sem(f"p_lo_ready_{i}") for i in range(2)]
        swapped = sem("swapped")
        turned = sem("turned")
        tables = sem("tables")
        sines = sem("sines")
        ckv_turned = sem("ckv_turned")
        ckv_rows = sem("ckv_rows")
        m_scaled = sem("m_scaled")
        forget_sum = sem("forget_sum")
        forget_parts = sem("forget_parts")
        fox_logf = sem("fox_logf")
        fox_cum = sem("fox_cum")
        decay_rows = sem("decay_rows")
        fox_cum_ready = sem("fox_cum_ready")
        q_lat = sem("q_lat")
        q_lat_ready = sem("q_lat_ready")
        dots = sem("dots")
        dots_relu = sem("dots_relu")
        dots_added = sem("dots_added")
        A = {n: {s: sem(f"{n}_{s}") for s in ("scores", "peak", "exp", "inv", "norm", "turn", "probsT", "out", "o_hi", "o_lo")}
             for n in ("mla", "even", "moba")}
        q_in_hi = sem("q_in_hi")
        q_in_lo = sem("q_in_lo")
        o_lat = sem("o_lat")
        o_up = sem("o_up")

        qlatT = m

        def at64(b, c, head, t0, n):
            r = 64 * (head % 2)
            return b[r:r + 64, c, t0:t0 + n]

        def mla_terms(hd, t):
            n = P * (t + 1)
            return [(qT[:, hd, P * t:P * t + P], kT[:, hd, 0:n]),
                    (at64(qT, 8 + hd // 2, hd, P * t, P), at64(kT, 8, hd, 0, n))]

        def fox_terms(hd, t):
            n = P * (t + 1)
            return [(at64(qT, hd // 2, hd, P * t, P), at64(kT, hd // 2, hd, 0, n)),
                    (decay_q[:, hd, P * t:P * t + P], decay_k[:, 0:n])]

        def dsa_terms(hd, t):
            n = P * (t + 1)
            return [(qlatT[:, hd, P * t:P * t + P], kT[:, 5, 0:n]),
                    (at64(qT, 4 + hd // 2, hd, P * t, P), at64(qT, 11, hd, 0, n))]

        def moba_terms(hd, t):
            n = P * (t + 1)
            return [(at64(qT, hd // 2, hd, P * t, P), at64(kT, hd // 2, hd, 0, n))]

        def even_terms(hd, t):
            return fox_terms(hd, t) if hd < HEADS else dsa_terms(hd - HEADS, t)

        KINDS = {
            "mla": dict(heads=HEADS, latent=HEADS, terms=mla_terms, mask=lambda hd: k("mla_mask"), pair=False,
                        scale=float(NOPE + ROPE) ** -0.5, v=lambda hd, t: val[:, t, P * hd:P * hd + P]),
            "even": dict(heads=2 * HEADS, latent=HEADS, terms=even_terms, pair=True, scale=HD ** -0.5,
                         mask=lambda hd: k("causal") if hd < HEADS else sel[:],
                         v=lambda hd, t: val[:, t, HD * hd:HD * hd + HD] if hd < HEADS else ckvt[:, t, :]),
            "moba": dict(heads=MOBA_HEADS, latent=MOBA_HEADS, terms=moba_terms, mask=lambda hd: k("causal"), pair=True,
                         scale=HD ** -0.5, v=lambda hd, t: val[:, t, HD * hd:HD * hd + HD]),
        }

        def out_of(kind, hd):
            if KINDS[kind]["pair"]:
                return hd // 2, hd % 2 == 1
            return hd, True

        def ended(kind, i):
            H, latent = KINDS[kind]["heads"], KINDS[kind]["latent"]
            found = []
            for hd in (i - OUT_LAG - 1, i - OUT_LAG - 1 - UP_LAG):
                if 0 <= hd < H and (hd >= latent) == (hd == i - OUT_LAG - 1 - UP_LAG):
                    c, whole = out_of(kind, hd)
                    if whole:
                        found.append((c, c % 2 if hd >= latent else (7, 3)[c % 2], hd))
            return found

        def length(kind):
            H, latent = KINDS[kind]["heads"], KINDS[kind]["latent"]
            return H + OUT_LAG + 1 + UP_LAG * (latent < H)

        ROPES = {"mla": [(kT, 8), (qT, 8), (qT, 9), (qT, 10), (qT, 11)],
                 "even": [(qT, c) for c in (8, 9, 10, 11, 4, 5, 6, 7)],
                 "odd": [(b, c) for b in (qT, kT) for c in range(8)]}
        ROPE_AT = {"mla": 0, "even": 5, "odd": 13}

        def wait_from(engine, semaphore, value):
            if not isinstance(value, int) or value > 0:
                engine.wait_ge(semaphore, value)

        block = ctx.enter_context(nc.Block())

        @block.sync
        def _(sp):
            sp.dma_start(h[:], x_dram).then_inc(x_loaded, 16)
            early = CCOL["mla_mask"]
            sp.dma_start(cst[:, 0:early], const_dram[:, 0:early]).then_inc(loaded, 16)
            sp.dma_start(vec[:], vec_dram).then_inc(loaded, 16)

            def load(u, s):
                sp.dma_start(staged[:, s:s + 1, :], w_stream[bass.ds(u, 1)].rearrange("u p n -> p u n")).then_inc(
                    landed[s], 16)

            for e in range(2):
                half = slice(HALF * e, HALF * e + HALF)
                sp.dma_start(staged[:, 0, half], w_stream[0, :, half]).then_inc((landed_early, landed[0])[e], 16)
            load(1, 1)
            sp.dma_start(cst[:, early:], const_dram[:, early:]).then_inc(late_loaded, 16)
            sp.dma_start(posi[:], pos_dram).then_inc(late_loaded, 16)

            def stream(first, end, columns):
                def unit(i, u):
                    sp.wait_ge(lo_split, i * 4 + (2 * u - 2))
                    sp.dma_start(staged[:, u % 2:u % 2 + 1, 0:columns],
                                 w_stream[bass.ds(i * 2 + u, 1), :, 0:columns].rearrange("u p n -> p u n")).then_inc(
                        landed[u % 2], 16)

                with sp.Fori(0, (end - first) // 2) as i:
                    unit(i, first)
                    unit(i, first + 1)
                if (end - first) % 2:
                    unit(0, end - 1)

            at = 2
            for layer in range(2):
                down = FIRST[f"down_{layer}"]
                stream(at, down, UNIT)
                at = down + dict(STREAM)[f"down_{layer}"]
                stream(down, at, D_FF2)
            for c in range(DC):
                sp.wait_ge(out_written, c + 1)
                sp.dma_start(out_dram[:, c, :], xn[:, c, :]).then_inc(stored, 16)
            sp.wait_ge(stored, 16 * DC)

        @block.tensor
        def _(pe):
            def weights(s, o, n):
                return w_hi[:, s, o:o + n], w_lo[:, s, o:o + n]

            def features(out, s, o, kc, xh, xl, fresh=None):
                for c in range(kc):
                    if fresh:
                        fresh(c)
                    wh, wl = weights(s, o + P * c, P)
                    pe.matmul(out, wh, xh[:, c, :], start=(c == 0), stop=False)
                    pe.matmul(out, wh, xl[:, c, :], start=False, stop=False)
                    last = pe.matmul(out, wl, xh[:, c, :], start=False, stop=(c == kc - 1))
                return last

            def part(name, s, first, end, kc, xh, xl, c):
                for j in range(first, end):
                    out = ps[:, j, 0:T]
                    wh, wl = weights(s, (j * kc + c) * P, P)
                    pe.matmul(out, wh, xh[:, c, :], start=(c == 0), stop=False)
                    pe.matmul(out, wh, xl[:, c, :], start=False, stop=False)
                    last = pe.matmul(out, wl, xh[:, c, :], start=False, stop=(c == kc - 1))
                    if c == kc - 1:
                        last.then_inc(product[name], 1)

            def together(name, n, xh, xl, fresh):
                arrived(2 * FIRST[name] + (n - 1) // 2)
                for c in range(DC):
                    fresh(c)
                    part(name, FIRST[name] % 2, 0, n, DC, xh, xl, c)

            def rows(out, s, o, n, kc, xh, xl, t):
                for c in range(kc):
                    wh, wl = weights(s, o + n * c, n)
                    tok = slice(P * t, P * t + P)
                    pe.matmul(out, xh[:, c, tok], wh, start=(c == 0), stop=False)
                    pe.matmul(out, xh[:, c, tok], wl, start=False, stop=False)
                    last = pe.matmul(out, xl[:, c, tok], wh, start=False, stop=(c == kc - 1))
                return last

            def bank(name, n):
                if n >= RING:
                    pe.wait_ge(drained[name], n - RING + 1)
                return n % RING

            def arrived(g):
                pe.wait_ge(lo_split, g + 1)

            def normed(name):
                def fresh(c):
                    pe.wait_ge(x_lo_ready, SPLIT_AT[name] + c + 1)
                return fresh

            def sums(name):
                i = NORM_AT[name]
                n = NORM_CHUNKS[name]
                if i:
                    pe.wait_ge(rooted, i)
                if name in LATE_ADDED:
                    pe.wait_ge(pool_added, (DC - 1) * (LATE_ADDED.index(name) + 1))
                    pe.matmul(STAT, k("ones"), stat[:, 4, :], start=True, stop=True).then_inc(summed, 1)
                    return
                if name in ADDED_AT:
                    pe.wait_ge(m_added, ADDED_AT[name] + n)
                    pe.matmul(STAT, k("ones"), stat[:, 3, :], start=True, stop=True).then_inc(summed, 1)
                    return
                for c in range(n):
                    pe.wait_ge(squared, SQUARE_AT[name] + c + 1)
                    last = pe.matmul(STAT, k("ones"), sq[:, c, :], start=(c == 0), stop=(c == n - 1))
                last.then_inc(summed, 1)

            def add_square(name, c):
                if c == 0:
                    pe.wait_ge(rooted, NORM_AT[name])
                pe.wait_ge(squared, SQUARE_AT[name] + c + 1)
                last = pe.matmul(STAT, k("ones"), sq[:, c, :], start=(c == 0), stop=(c == DC - 1))
                if c == DC - 1:
                    last.then_inc(summed, 1)

            def begun(name):
                def fresh(c):
                    if c:
                        add_square(name, c - 1)
                    pe.wait_ge(x_lo_ready, SPLIT_AT[name] + c + 1)
                return fresh

            def hidden(ready, n):
                def fresh(c):
                    if c % 8 == 0 or c == n - 2:
                        pe.wait_ge(ready, n if c == n - 2 else min(c + 8, n - 2))
                return fresh

            def keep_warm(n, b=6):
                for _ in range(n):
                    pe.matmul(ps[:, b, 0:T], decay_k[:, 0:P], decay_k[:], start=True, stop=True)

            def columns(name):
                pe.wait_ge(inverted, NORM_AT[name] + 1)
                for t in range(TT):
                    last = pe.transpose(ps[:, 7, P * t:P * t + P], LATE_SCALE[:, P * t:P * t + P], k("ident"))
                last.then_inc(col_turned, 1)

            def linear(name, per_unit, xh, xl, fresh=None, done=0):
                u0 = FIRST[name]
                n = 0
                for u in range(u0, u0 + dict(STREAM)[name]):
                    for j in range(per_unit):
                        if n >= done:
                            if j in (0, (per_unit + 1) // 2) or n == done:
                                arrived(2 * u + (j >= (per_unit + 1) // 2))
                            features(ps[:, bank(name, n), 0:T], u % 2, j * DC * P, DC, xh, xl,
                                     fresh if n == 0 else None).then_inc(product[name], 1)
                        n += 1

            def swap(name, i):
                b, c = ROPES[name][i]
                at = ROPE_AT[name] + i
                if at >= 2:
                    pe.wait_ge(turned, at - 1)
                pe.matmul(ps[:, 4 + at % 2, 0:T], k("swap" if name == "mla" else "swap2"), b[:, c, :], start=True,
                          stop=True).then_inc(swapped, 1)

            def attention(kind, start=0, stop=None, behind=None):
                spec, s = KINDS[kind], A[kind]
                H, latent = spec["heads"], spec["latent"]
                if behind:
                    arrived(2 * FIRST[behind])
                for i in range(start, length(kind) + BEHIND_LAG[kind] if behind else stop or length(kind)):
                    for c, _, _ in ended(kind, i - BEHIND_LAG[kind]) if behind else ():
                        pe.wait_ge(s["o_lo"], c + 1)
                        part(behind, FIRST[behind] % 2, 0, 2, DC, x_hi, x_lo, c)
                    if i < H:
                        if i >= 2:
                            pe.wait_ge(s["peak"], i - 1)
                        o = ps[:, 4 + i % 2, :]
                        for t in range(TT):
                            terms = spec["terms"](i, t)
                            for n, (a, b) in enumerate(terms):
                                last = pe.matmul(o[:, P * t:P * t + P * (t + 1)], a, b, start=(n == 0),
                                                 stop=(n == len(terms) - 1))
                        last.then_inc(s["scores"], 1)
                    hd = i - TURN_LAG
                    if 0 <= hd < H:
                        pe.wait_ge(s["norm"], hd + 1)
                        if hd >= 2:
                            pe.wait_ge(s["probsT"], hd - 1)
                        o = ps[:, (6, 2)[hd % 2], :]
                        for n in range(3):
                            last = pe.transpose(o[:, P * n:P * n + P], probs[:, hd % 3, P * n:P * n + P], k("ident"))
                        last.then_inc(s["turn"], 1)
                    hd = i - OUT_LAG
                    if 0 <= hd < H:
                        pe.wait_ge(s["probsT"], hd + 1)
                        c, whole = out_of(kind, hd)
                        if hd >= latent:
                            o = ps[:, (7, 3)[hd % 2], 0:T]
                            if hd >= latent + 2:
                                pe.wait_ge(o_lat, hd - latent - 1)
                            else:
                                pe.wait_ge(s["o_lo"], out_of(kind, latent)[0] - 1 + hd - latent)
                        else:
                            r = 64 * (hd % 2) if spec["pair"] else 0
                            rn = 64 if spec["pair"] else P
                            if c >= 2:
                                pe.wait_ge(s["o_lo"], c - 1)
                            o = ps[r:r + rn, (7, 3)[c % 2], 0:T]
                        pT = probsT[:, hd % 2, :]
                        pe.matmul(o, spec["v"](hd, 0), pT[:, 0:T], start=True, stop=False)
                        pe.matmul(o[:, P:T], spec["v"](hd, 1), pT[:, T:SPAN], start=False, stop=True).then_inc(s["out"], 1)
                    hd = i - OUT_LAG - UP_LAG
                    if latent <= hd < H:
                        pe.wait_ge(o_lat, hd - latent + 1)
                        c, whole = out_of(kind, hd)
                        if c >= latent // 2 + 2:
                            pe.wait_ge(s["o_lo"], c - 1)
                        r = 64 * (hd % 2)
                        pe.matmul(ps[r:r + 64, c % 2, 0:T], v("w_uv2", HD * (hd - latent), HD), tmp[:, hd % 2, :], start=True,
                                  stop=True).then_inc(o_up, 1)

            pe.wait_ge(dve_step, 2)
            keep_warm(7)
            pe.wait_ge(loaded, 32)
            sums("mix_pre_0")
            keep_warm(8)
            together("pw1", 2, x_hi, x_lo, normed("mix_pre_0"))
            linear("pw1", 4, x_hi, x_lo, done=2)

            def mean(chunks, ends=False):
                for n, c in enumerate(chunks):
                    if c in CONV_VECTOR:
                        pe.wait_ge(conv_ready, CONV_VECTOR.index(c) + 1)
                    elif c in SHARED:
                        pe.wait_ge(conv_ready, len(CONV_VECTOR) + 1 + list(SHARED).index(c))
                    elif c in CONV_POOL:
                        pe.wait_ge(conv_added, (CONV_POOL.index(c) + 1) * (TAPS - 1))
                    else:
                        pe.wait_ge(conv_drained, CONV_TENSOR.index(c) + 1)
                    last = pe.matmul(STAT, k("ones"), conv[:, c, :], start=(c == 1), stop=(ends and n == len(chunks) - 1))
                if ends:
                    last.then_inc(ln_summed, 1)

            for q, c in enumerate(CONV_TENSOR):
                pe.wait_ge(glu, c + 1)
                count = min(TAPS, TENSOR_TAPS - TAPS * q)
                for tap in range(count):
                    n = TAPS * q + tap
                    if n < DIAGS:
                        pe.wait_ge(pool_diag, n + 1)
                    else:
                        pe.wait_ge(act_diag, n - DIAGS + 1)
                    pe.matmul(ps[:, 4 + q, 0:T], diagonal(n), u_pad[:, c, tap:tap + T], start=(tap == 0),
                              stop=(tap == count - 1)).then_inc(diag_used, 1)
                if q == 1:
                    mean((1, 3, 0, 2))
            mean((5, 4, 7, 6), True)
            for c in range(DC):
                pe.wait_ge(ln_squared, c + 1)
                last = pe.matmul(STAT, k("ones"), sq[:, c, :], start=(c == 0), stop=(c == DC - 1))
            last.then_inc(ln_summed, 1)
            keep_warm(9)
            together("pw2", 3, x_hi, x_lo, normed("layer_norm"))
            linear("pw2", 4, x_hi, x_lo, done=3)
            sums("mix_post_0")
            keep_warm(9)

            def mlp(layer):
                one, two = f"ff1_{layer}", f"ff2_{layer}"
                u0 = FIRST[one]

                def hidden_chunk(i, n):
                    s, j = n // 4, n % 4
                    if j % 2 == 0:
                        pe.wait_ge(lo_split, i * 4 + (2 * (u0 + s) + j // 2 + 1))
                    wait_from(pe, drained[one], i * 8 + (n + 1 - RING))
                    features(ps[:, n % RING, 0:T], (u0 + s) % 2, j * DC * P, DC, x_hi, x_lo).then_inc(product[one], 1)

                together(one, 2, x_hi, x_lo, begun(f"ffn_pre_{layer}"))
                add_square(f"ffn_pre_{layer}", DC - 1)
                for n in range(2, 8):
                    hidden_chunk(0, n)
                with pe.Fori(1, dict(STREAM)[one] // 2) as i:
                    for n in range(8):
                        hidden_chunk(i, n)
                pe.wait_ge(drained[one], FC - RING + 2)
                pe.sem_inc(drained[two], 2)
                u0 = FIRST[two]
                with pe.Fori(0, dict(STREAM)[two] // 2) as i:
                    for s in range(2):
                        pe.wait_ge(lo_split, i * 4 + (2 * (u0 + s) + 2))
                        pe.wait_ge(drained[two], i * 2 + (s + 1))
                        features(ps[:, s, 0:T], (u0 + s) % 2, 0, FC, f_hi, f_lo,
                                 None if s else hidden(f_lo_ready[layer], FC)).then_inc(product[two], 1)
                sums(f"ffn_post_{layer}")
                keep_warm(9)

            mlp(0)

            pe.wait_ge(late_loaded, 32)
            together("kv", 2, f_hi, f_lo, begun("mix_pre_1"))
            add_square("mix_pre_1", DC - 1)
            linear("kv", 3, f_hi, f_lo, done=2)
            u = FIRST["dq"]
            for j in range(3):
                if j != 1:
                    arrived(2 * u + j // 2)
                features(ps[:, 4 + j, 0:T], u % 2, j * D, DC, x_hi, x_lo,
                         None if j else lambda c: pe.wait_ge(q_in_lo, c + 1)).then_inc(product["dq"], 1)
                if j == 0:
                    sums("kv_norm")
            u = FIRST["ukv"]
            arrived(2 * u)
            pe.wait_ge(x_lo_ready, SPLIT_AT["kv_norm"] + KV_RANK // P)
            pe.wait_ge(drained["kv"], 3)
            n = 0
            for j in range(HEADS):
                b = bank("ukv", n)
                features(ps[:, b, 0:T], u % 2, 2 * P * j, 2, f_hi[:, 8:10], f_lo[:, 8:10]).then_inc(product["ukv"], 1)
                n += 1
                if j == 2:
                    sums("q_norm")
                if j == 3:
                    pe.wait_ge(drained["dq"], 3)
                    swap("mla", 0)
            arrived(2 * u + 1)
            for half in range(2):
                for t in range(TT):
                    b = bank("ukv", n)
                    for c in range(2):
                        o = HALF + D * c + 512 * half
                        wh, wl = weights(u % 2, o, 512)
                        xh, xl = (y[:, 8 + c, P * t:P * t + P] for y in (f_hi, f_lo))
                        pe.matmul(ps[:, b, :], xh, wh, start=(c == 0), stop=False)
                        pe.matmul(ps[:, b, :], xh, wl, start=False, stop=False)
                        last = pe.matmul(ps[:, b, :], xl, wh, start=False, stop=(c == 1))
                    last.then_inc(product["ukv"], 1)
                    n += 1
            u = FIRST["uq"]
            pe.wait_ge(x_lo_ready, SPLIT_AT["q_norm"] + Q_RANK // P)
            for j in range(12):
                if j in (0, 5, 10):
                    arrived(2 * u + (0, 1, 2)[(0, 5, 10).index(j)])
                if j < RING:
                    pe.wait_ge(drained["ukv"], 12 - RING + j + 1)
                b = bank("uq", j)
                s, o = ((u % 2, 384 * j) if j < 5 else (u % 2, HALF + 384 * (j - 5)) if j < 10 else
                        ((u + 1) % 2, 384 * (j - 10)))
                features(ps[:, b, 0:T], s, o, 3, f_hi[:, 10:13], f_lo[:, 10:13]).then_inc(product["uq"], 1)
                if 2 <= j < 6:
                    pe.wait_ge(drained["uq"], j - 1)
                    swap("mla", j - 1)
                if j == 9:
                    pe.wait_ge(turned, 5)
                    pe.wait_ge(drained["uq"], 6)
                    attention("mla", 0, 2)
            pe.wait_ge(drained["uq"], 12)
            attention("mla", 2, behind="wo")
            linear("wo", 4, x_hi, x_lo, done=2)
            sums("mix_post_1")
            keep_warm(9)
            mlp(1)

            u0 = FIRST["even"]

            def chunk(n, j, at):
                u = u0 + j
                features(ps[:, bank("even", n), 0:T], u % 2, at, DC, x_hi, x_lo).then_inc(product["even"], 1)

            def turn_chunk(i, n):
                pe.wait_ge(drained["even"], n + 1)
                swap("even", i)

            def dot(i):
                if i >= 2:
                    pe.wait_ge(dots_relu, i - 1)
                o = ps[:, 4 + i % 2, :]
                for t in range(TT):
                    last = pe.matmul(o[:, P * t:P * t + P * (t + 1)], at64(qT, 8 + i // 2, i, P * t, P),
                                     at64(qT, 10, i, 0, P * (t + 1)), start=True, stop=True)
                last.then_inc(dots, 1)

            def latent_query(hd):
                pe.wait_ge(turned, ROPE_AT["even"] + 5 + hd // 2)
                if hd >= 2:
                    pe.wait_ge(q_lat_ready, hd - 1)
                elif hd == 0:
                    pe.wait_ge(fox_cum_ready, 1)
                else:
                    pe.wait_ge(ckv_rows, 1)
                r = 64 * (hd % 2)
                pe.matmul(ps[:, 6 + hd % 2, 0:T], vec[r:r + 64, VCOL["w_uk2"] + P * (hd // 2):VCOL["w_uk2"] + P * (hd // 2) + P],
                          qT[r:r + 64, 4 + hd // 2, :], start=True, stop=True).then_inc(q_lat, 1)

            together("even", 2, x_hi, x_lo, begun("attn_0"))
            add_square("attn_0", DC - 1)
            arrived(2 * u0 + 1)
            for n in range(2, 4):
                chunk(n, 0, n * D)
                turn_chunk(n - 2, n - 2)
            arrived(2 * (u0 + 1))
            chunk(4, 1, 0)
            turn_chunk(2, 2)
            columns("attn_0")
            for t in range(TT):
                rows(ps[:, bank("even", 5 + t), 0:12], (u0 + 1) % 2, D, 12, DC, x_hi, x_lo, t).then_inc(product["even"], 1)
            turn_chunk(3, 4)
            pe.wait_ge(col_ready, 1)
            sums("g_ckv")
            for n in range(7, 11):
                if n % 2:
                    arrived(2 * (u0 + 2) + (n - 7) // 2)
                chunk(n, 2, (n - 7) * D)
                if n == 8:
                    pe.wait_ge(turned, ROPE_AT["even"] + 4)
                    dot(0)
                    dot(1)
                if n == 10:
                    dot(2)
                    dot(3)
            for n in range(11, 15):
                if n % 2:
                    arrived(2 * (u0 + 3) + (n - 11) // 2)
                chunk(n, 3, (n - 11) * D)
                if n == 11:
                    pe.wait_ge(fox_logf, 1)
                    for t in range(TT):
                        last = pe.matmul(ps[0:DECAY, 6, 0:T], logf_rows[:, t, :], k("upto")[:, T * t:T * t + T],
                                         start=(t == 0), stop=(t == TT - 1))
                    last.then_inc(fox_cum, 1)
                    pe.wait_ge(scaled, SCALE_AT["g_ckv"] + 1)
                    for t in range(TT):
                        last = pe.transpose(ps[:, 7, P * t:P * t + P], kT[:, 5, P * t:P * t + P], k("ident"))
                    last.then_inc(ckv_turned, 1)
                    pe.wait_ge(dots_relu, IDX_HEADS)
                turn_chunk(n - 7, n - 4)
            arrived(2 * (u0 + 4) + 1)
            for t in range(TT):
                rows(ps[:, bank("even", 15 + t), :], (u0 + 4) % 2, 0, 512, DC, x_hi, x_lo, t).then_inc(product["even"], 1)
                latent_query(2 * t)
                latent_query(2 * t + 1)
            for n in range(17, 21):
                if n % 2:
                    arrived(2 * (u0 + 5) + (n - 17) // 2)
                chunk(n, 5, (n - 17) * D)
                if n < 19:
                    latent_query(2 * n - 30)
                    latent_query(2 * n - 29)
                if n == 19:
                    pe.wait_ge(normed_rows, 6)
                    pe.wait_ge(decay_rows, 2)
                    attention("even", 0, 2)
            pe.wait_ge(drained["even"], 21)
            pe.wait_ge(q_lat_ready, HEADS)
            pe.wait_ge(normed_rows, 9)
            attention("even", 2)
            fresh_o = lambda c: pe.wait_ge(A["even"]["o_lo"], c + 1)
            pe.wait_ge(A["even"]["o_lo"], DC - 1)
            linear("oute", 4, x_hi, x_lo, fresh_o)

            def glu_mlp(layer):
                up, down = f"up_{layer}", f"down_{layer}"
                u0, units = FIRST[up], dict(STREAM)[up]

                def unit(i, s):
                    for j in range(2):
                        pe.wait_ge(lo_split, i * 4 + (2 * (u0 + s) + j + 1))
                        n = 2 * s + j
                        sl = (u0 + s) % 2
                        first = isinstance(i, int) and i == 0 and n == 0
                        wait_from(pe, drained[up], i * 4 + (n - 1))
                        features(ps[:, j, 0:T], sl, 2 * j * DC * P, DC, *g_in,
                                 normed(f"ffn2_{layer}") if first else None).then_inc(product[up], 1)
                        if first:
                            sums(f"ffn2_{layer}")
                        wait_from(pe, u_drained[layer], i * 4 + (n - 1))
                        features(ps[:, 2 + j, 0:T], sl, (2 * j + 1) * DC * P, DC, *g_in).then_inc(u_product[layer], 1)

                pe.wait_ge(h_ready[("oute", "outo")[layer]], DC - RING + 1)
                unit(0, 0)
                unit(0, 1)
                with pe.Fori(1, units // 2) as i:
                    unit(i, 0)
                    unit(i, 1)
                unit(units // 2, 0)
                pe.wait_ge(drained[up], GC)
                pe.sem_inc(drained[down], 2)
                u0 = FIRST[down]
                with pe.Fori(0, dict(STREAM)[down] // 2) as i:
                    for s in range(2):
                        pe.wait_ge(lo_split, i * 4 + (2 * (u0 + s) + 2))
                        pe.wait_ge(drained[down], i * 2 + (s + 1))
                        features(ps[:, s, 0:T], (u0 + s) % 2, 0, GC, f_hi, f_lo,
                                 None if s else hidden(p_lo_ready[layer], GC)).then_inc(product[down], 1)

            glu_mlp(0)
            u0 = FIRST["odd"]
            fresh = normed("attn_1")
            pe.wait_ge(h_ready["down_0"], 2 + DC - 1)
            for n in range(16):
                if n % 2 == 0:
                    arrived(2 * u0 + n // 2)
                features(ps[:, bank("odd", n), 0:T], (u0 + n // 4) % 2, n % 4 * DC * P, DC, x_hi, x_lo,
                         fresh if n == 0 else None).then_inc(product["odd"], 1)
                if n == 1:
                    sums("attn_1")
                if n == 6:
                    columns("attn_1")
                if n >= 2:
                    pe.wait_ge(drained["odd"], n - 1)
                    swap("odd", n - 2)
            for half in range(2):
                u = u0 + 4 + half
                arrived(2 * u + 1)
                for t in range(TT):
                    rows(ps[:, bank("odd", 16 + 2 * half + t), :], u % 2, 0, 512, DC, x_hi, x_lo, t).then_inc(
                        product["odd"], 1)
                    if not half:
                        pe.wait_ge(drained["odd"], 15 + t)
                        swap("odd", 14 + t)
                    elif not t:
                        pe.wait_ge(turned, ROPE_AT["odd"] + 16)
                        attention("moba", 0, 2)
            pe.wait_ge(drained["odd"], 20)
            attention("moba", 2, behind="outo")
            linear("outo", 4, x_hi, x_lo, done=2)
            glu_mlp(1)
            sums("final")

        @block.scalar
        def _(act):
            def hi(g, s, at, n=HALF):
                o = HALF * (g % 2)
                if g:
                    act.wait_ge(landed[s], at)
                act.activation(w_hi[:, s, o:o + n], staged[:, s, o:o + n], ACT.Copy, scale=SW).then_inc(hi_split, 1)

            def split(g):
                if g == 0:
                    act.wait_ge(landed_early, 16)
                if g < HALVES:
                    hi(g, g // 2 % 2, 16 * (g // 4 + (g > 0)), USED.get(g, HALF))

            def quarter(g, q):
                o = HALF * (g % 2) + QUARTER * q
                act.wait_ge(landed[g // 2 % 2], 16 * (g // 4 + 1))
                ins = act.activation(w_hi[:, g // 2 % 2, o:o + QUARTER], staged[:, g // 2 % 2, o:o + QUARTER], ACT.Copy,
                                     scale=SW)
                if q == 3:
                    ins.then_inc(hi_split, 1)

            def squares(name, src, ready):
                for c in range(NORM_CHUNKS[name]):
                    ready(c)
                    act.activation(sq[:, c, :], src[:, c, :], ACT.Square).then_inc(squared, 1)

            def root(name):
                late = name in LATE
                act.wait_ge(summed, NORM_AT[name] + 1)
                act.activation(stat[:, 0, :], STAT, ACT.Sqrt, bias=k("input_eps" if late else "rms_eps"),
                               scale=(INV ** -2 if late else 1.0) / (P * NORM_CHUNKS[name])).then_inc(rooted, 1)

            def begin(name, dst, ready, i, c, ahead=0):
                act.wait_ge(ready, i * 2 + (c + 1 + ahead))
                at = bass.ds(i * 2 + c, 1)
                act.activation(dst[:, at, :], h[:, at, :], ACT.Copy,
                               scale=vec[:, bass.ds(i * 2 + (VCOL["kv_in" if name == "mix_pre_1" else name] + c), 1)]
                               ).then_inc(x_hi_ready, 1)
                if name == "mix_pre_1":
                    act.activation(x_hi[:, at, :], h[:, at, :], ACT.Copy, scale=v(name, c)).then_inc(q_in_hi, 1)
                act.activation(sq[:, at, :], h[:, at, :], ACT.Square).then_inc(squared, 1)

            def columns(n):
                act.wait_ge(col_turned, n)
                act.activation(late_col[:], ps[:, 7, 0:T].rearrange("p (t q) -> p t q", t=TT)[:, :, 0], ACT.Copy).then_inc(
                    col_ready, 1)

            def his(name, dst):
                base = SCALE_AT[name]
                for c in range(NORM_CHUNKS[name]):
                    act.wait_ge(scaled, base + c + 1)
                    act.activation(dst[:, c, :], xn[:, c, :], ACT.Copy, scale=SX).then_inc(x_hi_ready, 1)

            def evac(name, n, dst, scale=INV, cols=T):
                act.wait_ge(product[name], n + 1)
                act.activation(dst, ps[:, n % RING, 0:cols], ACT.Copy, scale=scale).then_inc(drained[name], 1)

            def behind(name, norm=None):
                for n in range(DC):
                    if norm:
                        begin(norm, g_in[0], h_ready[name], 0, n)
                    if n % 2 and n < (DC // 2 if norm else DC - 1):
                        act.wait_ge(product[name], n + 1)
                        split(2 * FIRST[name] + n // 2 + 4)

            def last_behind(name):
                act.wait_ge(product[name], DC)
                split(2 * FIRST[name] + 7)

            def attention(kind, start=0, stop=None):
                spec, s = KINDS[kind], A[kind]
                H, latent = spec["heads"], spec["latent"]
                for i in range(start, stop or length(kind)):
                    if i < H:
                        act.wait_ge(s["peak"], i + 1)
                        if i >= 3:
                            act.wait_ge(s["turn"], i - 2)
                        b = i % 2
                        for t in range(TT):
                            sl = slice(P * t, P * t + P * (t + 1))
                            last = act.activation(probs[:, i % 3, sl], scores[:, b, sl], ACT.Exp, bias=peak[:, b, 2 + t:3 + t],
                                                  accum_out=peak[:, b, 4 + t:5 + t])
                        last.then_inc(s["exp"], 1)
                    hd = i - TURN_LAG
                    if 0 <= hd < H:
                        act.wait_ge(s["turn"], hd + 1)
                        if hd >= 2:
                            act.wait_ge(s["out"], hd - 1)
                        act.activation(probsT[:, hd % 2, :], ps[:, (6, 2)[hd % 2], 0:SPAN], ACT.Copy).then_inc(
                            s["probsT"], 1)
                    hd = i - OUT_LAG - 1
                    if latent <= hd < H:
                        act.wait_ge(s["out"], hd + 1)
                        if hd >= latent + 2:
                            act.wait_ge(o_up, hd - latent - 1)
                        act.activation(tmp[:, hd % 2, :], ps[:, (7, 3)[hd % 2], 0:T], ACT.Copy).then_inc(o_lat, 1)
                    for c, b, hd in ended(kind, i):
                        if hd >= latent:
                            act.wait_ge(o_up, hd - latent + 1)
                        else:
                            act.wait_ge(s["out"], hd + 1)
                        act.activation(x_hi[:, c, :], ps[:, b, 0:T], ACT.Copy, scale=SX).then_inc(s["o_hi"], 1)
                    for g, q in spread(kind, i, False):
                        quarter(g, q)

            act.wait_ge(x_loaded, 16)
            squares("mix_pre_0", h, lambda c: None)
            root("mix_pre_0")
            for g in range(2):
                split(g)
            his("mix_pre_0", x_hi)
            for g in range(2, 4):
                split(g)
            act.wait_ge(loaded, 32)
            todo = [(c, tap) for c in CONV_POOL for tap in range(TAPS - SHARED.get(c, 0))]

            def taps(count, chunks):
                for _ in range(count):
                    if not todo or todo[0][0] >= chunks:
                        return
                    c, tap = todo.pop(0)
                    if tap == 0:
                        act.wait_ge(glu, c + 1)
                        act.activation(conv[:, c, :], u_pad[:, c, 0:T], ACT.Identity, bias=v("b_dw", c),
                                       scale=v("taps", c)).then_inc(conv_started, 1)
                        continue
                    n = CONV_POOL.index(c) * (TAPS - 1) + tap - 1
                    if n >= 4:
                        act.wait_ge(conv_added, n - 3)
                    act.activation(tmp[:, n % 4, :], u_pad[:, c, tap:tap + T], ACT.Copy,
                                   scale=v("taps", DC * tap + c)).then_inc(conv_product, 1)

            u0 = FIRST["pw1"]
            for j in range(DC):
                act.wait_ge(product["pw1"], 2 * j + 1)
                if j >= 2:
                    act.wait_ge(glu, j - 1)
                act.activation(m[:, 2 * (j % 2), :], ps[:, 2 * j % RING, 0:T], ACT.Sigmoid, bias=v("b_pw1", DC + j),
                               scale=INV).then_inc(drained["pw1"], 1)
                act.wait_ge(product["pw1"], 2 * j + 2)
                act.activation(m[:, 2 * (j % 2) + 1, :], ps[:, (2 * j + 1) % RING, 0:T], ACT.Identity,
                               bias=v("b_pw1", j), scale=INV).then_inc(drained["pw1"], 1)
                split(2 * u0 + j + 4)
                if j:
                    taps(4, j)
            made = DIAGS
            for q, c in enumerate(CONV_TENSOR):
                while made < min(TAPS * (q + 2) + DIAGS // 2, TENSOR_TAPS):
                    act.wait_ge(diag_used, made - DIAGS + 1)
                    act.activation(diagonal(made), k("ident"), ACT.Copy,
                                   scale=v("taps", DC * (made % TAPS) + CONV_TENSOR[made // TAPS])).then_inc(act_diag, 1)
                    made += 1
                    if made % 2:
                        taps(1, DC)
                if q == len(CONV_TENSOR) - 1:
                    taps(TAPS * len(CONV_POOL), DC)
                    break
                if q:
                    taps(6, DC)
                act.wait_ge(diag_used, TAPS * (q + 1))
                act.activation(conv[:, c, :], ps[:, 4 + q, 0:T], ACT.Identity, bias=v("b_dw", c)).then_inc(
                    conv_drained, 1)
            for c in range(DC):
                act.wait_ge(ln_centred, c + 1)
                act.activation(sq[:, c, :], conv[:, c, :], ACT.Square).then_inc(ln_squared, 1)
            act.wait_ge(ln_summed, 2)
            act.activation(stat[:, 2, :], STAT, ACT.Sqrt, bias=k("ln_eps"), scale=1.0 / D).then_inc(ln_rooted, 1)
            for c in range(DC + 1):
                if c < DC:
                    act.wait_ge(ln_scaled, c + 1)
                    act.activation(xn[:, c, :], xn[:, c, :], ACT.Silu, bias=v("ln_b", c), scale=v("ln_g", c)).then_inc(
                        act_step, 1)
                if c:
                    act.wait_ge(act_step, c)
                    act.activation(x_hi[:, c - 1, :], xn[:, c - 1, :], ACT.Copy, scale=SX).then_inc(x_hi_ready, 1)
            behind("pw2")
            root("mix_post_0")
            last_behind("pw2")

            def mlp(layer):
                one, two = f"ff1_{layer}", f"ff2_{layer}"
                for c in range(DC):
                    begin(f"ffn_pre_{layer}", x_hi, h_ready[f"mix_{layer}"], 0, c)
                root(f"ffn_pre_{layer}")
                u0 = FIRST[one]

                def hidden_chunk(i, n):
                    r = tmp[:, n % 2:n % 2 + 1, :]
                    if n % 2 == 1:
                        act.wait_ge(product[one], i * 8 + (n + 1))
                        g = 2 * u0 + n // 2 + 4
                        hi(g, g // 2 % 2, i * 16 + 16 * (g // 4 + 1))
                    act.wait_ge(drained[one], i * 8 + (n + 1))
                    wait_from(act, f_lo_ready[layer], i * 8 + (n - 1))
                    act.activation(tmp[:, 2 + n % 2:3 + n % 2, :], r, ACT.Square)
                    act.activation(f_hi[:, bass.ds(i * 8 + n, 1), :], r, ACT.Square, scale=SF ** 0.5).then_inc(
                        f_hi_ready[layer], 1)

                for n in range(8):
                    hidden_chunk(0, n)
                with act.Fori(1, dict(STREAM)[one] // 2) as i:
                    for n in range(8):
                        hidden_chunk(i, n)
                if layer == 0:
                    act.wait_ge(tables, 1)
                    act.activation(tmp[:, 2, :], tmp[:, 0, :], ACT.Sin).then_inc(sines, 1)
                    act.activation(tmp[:, 3, :], tmp[:, 0, :], ACT.Sin, scale=0.5).then_inc(sines, 1)
                u0, units = FIRST[two], dict(STREAM)[two]

                def unit(i, s):
                    act.wait_ge(product[two], i * 2 + (s + 1))
                    for e in range(2):
                        g = 2 * (u0 + s) + e + 4
                        hi(g, g // 2 % 2, i * 16 + 16 * (g // 4 + 1))

                with act.Fori(0, units // 2 - 1) as i:
                    unit(i, 0)
                    unit(i, 1)
                unit(units // 2 - 1, 0)
                root(f"ffn_post_{layer}")

            def last_halves(name, e):
                u = FIRST[name] + dict(STREAM)[name] - 1
                act.wait_ge(product[name], dict(STREAM)[name])
                split(2 * u + e + 4)

            act.wait_ge(gains_scaled, 1)
            mlp(0)
            last_halves("ff2_0", 0)
            for c in range(DC):
                begin("mix_pre_1", f_hi, h_ready["ffn_0"], 0, c)
            last_halves("ff2_0", 1)
            root("mix_pre_1")
            u0 = FIRST["kv"]
            act.wait_ge(product["kv"], 2)
            split(2 * u0 + 4)
            squares("kv_norm", kT, lambda c: act.wait_ge(drained["kv"], c + 1))
            act.wait_ge(product["kv"], 3)
            split(2 * u0 + 5)
            u0 = FIRST["dq"]

            def square_latent(n):
                act.wait_ge(drained["dq"], n + 1)
                act.activation(sq[:, n, :], qT[:, n, :], ACT.Square).then_inc(squared, 1)

            root("kv_norm")
            square_latent(0)
            square_latent(1)
            his("kv_norm", f_hi[:, 8:10])
            square_latent(2)
            act.wait_ge(product["dq"], 3)
            split(2 * u0 + 4)
            u0 = FIRST["ukv"]
            for n in range(8):
                evac("ukv", n, kT[:, n, :])
                if n == 2:
                    root("q_norm")
                if n == 5:
                    his("q_norm", f_hi[:, 10:13])
            split(2 * FIRST["dq"] + 5)
            for n in range(8, 12):
                half, t = (n - 8) // 2, (n - 8) % 2
                if n == 10:
                    split(2 * u0 + 4)
                evac("ukv", n, val[:, t, 512 * half:512 * half + 512], cols=512)
            split(2 * u0 + 5)
            u0 = FIRST["uq"]
            for n in range(12):
                evac("uq", n, qT[:, (n + 8) % 12, :])
                if n == 4:
                    split(2 * u0 + 4)
                if n == 10:
                    attention("mla", 0, 1)
            attention("mla", 1)
            split(2 * FIRST["wo"] + 3)
            behind("wo")
            root("mix_post_1")
            last_behind("wo")
            mlp(1)
            last_halves("ff2_1", 0)
            for c in range(DC):
                begin("attn_0", x_hi, h_ready["ffn_1"], 0, c)
            last_halves("ff2_1", 1)
            root("attn_0")
            u0 = FIRST["even"]

            def weighted(i):
                act.wait_ge(dots, i + 1)
                if i >= 2:
                    act.wait_ge(dots_added, i - 1)
                act.activation(scores[:, i % 2, :], ps[:, 4 + i % 2, 0:SPAN], ACT.Relu,
                               scale=float(HD) ** -0.5 * float(IDX_HEADS) ** -0.5).then_inc(dots_relu, 1)

            def latent_query(hd):
                act.wait_ge(q_lat, hd + 1)
                act.activation(qlatT[:, hd, :], ps[:, 6 + hd % 2, 0:T], ACT.Copy).then_inc(q_lat_ready, 1)

            place = ([(qT, 8), (qT, 9), (qT, 10), (kT, 4), (qT, 11), None, None] + [(qT, c) for c in range(4, 8)] +
                     [(kT, c) for c in range(4)] + [None, None] + [(qT, c) for c in range(4)])
            splits = 0
            for n in range(21):
                if n in (5, 6):
                    evac("even", n, gates[:, n - 5, :], late_col[:, n - 5:n - 4], cols=12)
                elif n in (15, 16):
                    evac("even", n, val[:, n - 15, 0:512], late_col[:, n - 15:n - 14], cols=512)
                else:
                    evac("even", n, place[n][0][:, place[n][1], :], 1.0)
                if n == 4:
                    columns(1)
                    act.wait_ge(col_ready, 1)
                    squares("g_ckv", kT[:, 4:5], lambda c: act.wait_ge(normed_rows, 1))
                if n == 7:
                    root("g_ckv")
                    act.wait_ge(forget_sum, 1)
                    act.activation(logf[:, 2, :], logf[:, 1, :], ACT.Exp, scale=-1.0).then_inc(forget_parts, 1)
                if n == 8:
                    weighted(0)
                    weighted(1)
                    act.wait_ge(forget_sum, 2)
                    act.activation(logf[:, 1, :], logf[:, 3, :], ACT.Ln).then_inc(forget_parts, 1)
                for _ in range({1: 1, 3: 1, 6: 2, 8: 1, 10: 1, 12: 1, 14: 1}.get(n, 0)):
                    split(2 * u0 + splits + 4)
                    splits += 1
                if n == 10:
                    weighted(2)
                    weighted(3)
                if n == 11:
                    act.wait_ge(ckv_turned, 1)
                    act.activation(ckvt[:].rearrange("p t r -> p (t r)"), ps[:, 7, 0:T], ACT.Copy).then_inc(ckv_rows, 1)
                if 15 <= n < 19:
                    latent_query(2 * n - 30)
                    latent_query(2 * n - 29)
                if n == 20:
                    attention("even", 0, 2)
            attention("even", 2)
            behind("oute", "ffn2_0")

            def glu_mlp(layer, last_stage):
                up, down = f"up_{layer}", f"down_{layer}"
                act.wait_ge(product[("oute", "outo")[layer]], DC)
                split(2 * FIRST[("oute", "outo")[layer]] + 6)
                root(f"ffn2_{layer}")
                last_behind(("oute", "outo")[layer])
                u0, units = FIRST[up], dict(STREAM)[up]

                def pair(i, n, parts=(True, True)):
                    old, new = parts
                    j = n % 2
                    g = 2 * u0 + n + 3
                    if old and new:
                        act.wait_ge(u_product[layer], i * 4 + n)
                        hi(g, g // 2 % 2, i * 16 + 16 * (g // 4 + 1))
                    if old:
                        act.wait_ge(u_drained[layer], i * 4 + n)
                        act.activation(f_hi[:, bass.ds(i * 4 + (n - 1), 1), :], tmp[:, 3 - j:4 - j, :], ACT.Copy,
                                       scale=SF).then_inc(p_hi_ready[layer], 1)
                    if old and not new:
                        act.wait_ge(u_product[layer], i * 4 + n)
                        hi(g, g // 2 % 2, i * 16 + 16 * (g // 4 + 1))
                    if new:
                        act.wait_ge(drained[up], i * 4 + (n + 1))
                        wait_from(act, u_drained[layer], i * 4 + (n - 1))
                        act.activation(tmp[:, j, :], pad[:, j, 0:T], ACT.Identity,
                                       bias=vec[:, bass.ds(i * 4 + (VCOL[f"b_cv_{layer}"] + n), 1)],
                                       scale=vec[:, bass.ds(i * 4 + (VCOL[f"taps2_{layer}"] + n), 1)]).then_inc(
                            g_first[layer], 1)
                        act.wait_ge(g_conv[layer], i * 8 + (2 * n + 2))
                        act.activation(tmp[:, j, :], tmp[:, j, :], ACT.Silu).then_inc(g_silu[layer], 1)

                pair(0, 0, (False, True))
                pair(0, 1)
                with act.Fori(0, (GC - 2) // 4) as i:
                    for n in range(2, 6):
                        pair(i, n)
                pair(0, GC, (True, False))
                u0, units = FIRST[down], dict(STREAM)[down]

                def unit(i, s, splits=True):
                    act.wait_ge(product[down], i * 2 + (s + 1))
                    for e in range(2 * splits):
                        g = 2 * (u0 + s) + e + 4
                        hi(g, g // 2 % 2, i * 16 + 16 * (g // 4 + 1))
                    if not last_stage:
                        begin("attn_1", x_hi, h_ready[down], i, s, 2)

                with act.Fori(0, units // 2 - 1) as i:
                    unit(i, 0)
                    unit(i, 1)
                if not last_stage:
                    unit(units // 2 - 1, 0)
                    unit(units // 2 - 1, 1, False)

            glu_mlp(0, False)
            last_halves("down_0", 0)
            last_halves("down_0", 1)
            root("attn_1")
            u0 = FIRST["odd"]
            for n in range(16):
                evac("odd", n, (qT, kT)[n // 8][:, n % 8, :], 1.0)
                if n == 7:
                    columns(2)
                if n % 2:
                    split(2 * u0 + n // 2 + 4)
            for n in range(16, 20):
                half, t = (n - 16) // 2, n % 2
                if n == 16:
                    act.wait_ge(col_ready, 2)
                evac("odd", n, val[:, t, 512 * half:512 * half + 512], late_col[:, t:t + 1], cols=512)
                if n == 17:
                    split(2 * u0 + 8 + 4)
                if n == 18:
                    attention("moba", 0, 2)
            attention("moba", 2)
            behind("outo", "ffn2_1")
            glu_mlp(1, True)
            root("final")

        @block.gpsimd
        def _(pool):
            pool.wait_ge(loaded, 32)
            for n in range(DIAGS):
                pool.tensor_scalar(diagonal(n), k("ident"), v("taps", DC * (n % TAPS) + CONV_TENSOR[n // TAPS]), None,
                                   ALU.mult).then_inc(pool_diag, 1)
            n = 0
            for q, c in enumerate(CONV_POOL):
                pool.wait_ge(conv_started, q + 1)
                for tap in range(1, TAPS - SHARED.get(c, 0)):
                    pool.wait_ge(conv_product, n + 1)
                    if tap > 1:
                        pool.wait_ge(conv_added, n)
                    pool.tensor_tensor(conv[:, c, :], conv[:, c, :], tmp[:, n % 4, :], ALU.add).then_inc(conv_added, 1)
                    n += 1

            def add_squares(name):
                base, at = (DC - 1) * LATE_ADDED.index(name), SQUARE_AT[name]
                for c in range(1, DC):
                    pool.wait_ge(squared, at + c + 1)
                    if c > 1:
                        pool.wait_ge(pool_added, base + c - 1)
                    pool.tensor_tensor(stat[:, 4, :], sq[:, 0, :] if c == 1 else stat[:, 4, :], sq[:, c, :],
                                       ALU.add).then_inc(pool_added, 1)

            def scale_gates(layer):
                pool.wait_ge(inverted, NORM_AT[f"ffn2_{layer}"] + 1)
                with pool.Fori(0, GC // 2) as i:
                    for j in range(2):
                        pool.wait_ge(g_silu[layer], i * 2 + (j + 1))
                        pool.tensor_tensor(tmp[:, j, :], tmp[:, j, :], LATE_SCALE, ALU.mult).then_inc(g_normed[layer], 1)

            def divide(kind):
                s = A[kind]
                for hd in range(KINDS[kind]["heads"]):
                    pool.wait_ge(s["inv"], hd + 1)
                    for t in range(TT):
                        sl = slice(P * t, P * t + P * (t + 1))
                        last = pool.tensor_tensor(probs[:, hd % 3, sl], probs[:, hd % 3, sl],
                                                  peak[:, hd % 2, 6 + t:7 + t].to_broadcast([P, P * (t + 1)]), ALU.mult)
                    last.then_inc(s["norm"], 1)

            def add_to_h(name, ready):
                for c in range(DC):
                    pool.wait_ge(m_scaled, DC * POSTS.index(name) + c + 1)
                    pool.tensor_tensor(h[:, c, :], h[:, c, :], m[:, c, :], ALU.add).then_inc(h_ready[ready], 1)

            add_to_h("mix_post_0", "mix_0")
            add_to_h("ffn_post_0", "ffn_0")
            pool.wait_ge(late_loaded, 32)
            pool.wait_ge(x_lo_ready, SPLIT_AT["q_norm"] + Q_RANK // P)
            pool.memset(decay_q[:], 0.0).then_inc(decay_rows, 1)
            pool.wait_ge(decay_rows, 1)
            pool.tensor_copy(decay_q[0:HEADS, :, :], cst[0:HEADS, CCOL["pick"]:CCOL["pick"] + HEADS].unsqueeze(2).to_broadcast(
                [HEADS, HEADS, T])).then_inc(decay_rows, 1)
            divide("mla")
            add_to_h("mix_post_1", "mix_1")
            add_to_h("ffn_post_1", "ffn_1")
            pool.wait_ge(inverted, NORM_AT["attn_0"] + 1)
            for n, (b, c) in ([(3, (kT, 4))] + [(11 + c, (kT, c)) for c in range(4)] + [(17 + c, (qT, c)) for c in range(4)]):
                pool.wait_ge(drained["even"], n + 1)
                pool.tensor_tensor(b[:, c, :], b[:, c, :], LATE_SCALE, ALU.mult).then_inc(normed_rows, 1)
            divide("even")
            add_squares("ffn2_0")
            scale_gates(0)
            add_squares("attn_1")
            divide("moba")
            add_squares("ffn2_1")
            scale_gates(1)

        @block.vector
        def _(dve):
            steps = [0]

            def step(ins):
                steps[0] += 1
                ins.then_inc(dve_step, 1)
                return steps[0]

            def chain(ins):
                dve.wait_ge(dve_step, step(ins))

            def lo(s, e, at, n=HALF):
                o = HALF * e
                dve.wait_ge(hi_split, at)
                dve.scalar_tensor_tensor(w_lo[:, s, o:o + n], staged[:, s, o:o + n], SW, w_hi[:, s, o:o + n],
                                         ALU.mult, ALU.subtract).then_inc(lo_split, 1)

            def split(g):
                if g < HALVES:
                    lo(g // 2 % 2, g % 2, g + 1, USED.get(g, HALF))

            def invert(name):
                dve.wait_ge(rooted, NORM_AT[name] + 1)
                dve.reciprocal(LATE_SCALE if name in LATE else stat[:, 1, :], stat[:, 0, :]).then_inc(inverted, 1)

            def low(name, c, dst):
                dve.wait_ge(x_hi_ready, SPLIT_AT[name] + c + 1)
                dve.scalar_tensor_tensor(dst[1][:, c, :], h[:, c, :], v("kv_in" if name == "mix_pre_1" else name, c),
                                         dst[0][:, c, :], ALU.mult, ALU.subtract).then_inc(x_lo_ready, 1)
                if name == "mix_pre_1":
                    dve.wait_ge(q_in_hi, c + 1)
                    dve.scalar_tensor_tensor(x_lo[:, c, :], h[:, c, :], v(name, c), x_hi[:, c, :], ALU.mult,
                                             ALU.subtract).then_inc(q_in_lo, 1)

            def x_lows(name, c, dst):
                dve.wait_ge(x_hi_ready, SPLIT_AT[name] + c + 1)
                dve.scalar_tensor_tensor(dst[1][:, c, :], xn[:, c, :], SX, dst[0][:, c, :], ALU.mult,
                                         ALU.subtract).then_inc(x_lo_ready, 1)

            def scale(name, src, gain, dst):
                n = NORM_CHUNKS[name]
                dve.wait_ge(inverted, NORM_AT[name] + 1)
                for c in range(n + 1):
                    if c < n:
                        dve.scalar_tensor_tensor(xn[:, c, :], src[:, c, :], v(gain, c), stat[:, 1, :], ALU.mult,
                                                 ALU.mult).then_inc(scaled, 1)
                    if c:
                        x_lows(name, c - 1, dst)

            def post(name, norm, dst):
                dve.wait_ge(inverted, NORM_AT[name] + 1)
                for c in range(DC + 2):
                    if c < DC:
                        dve.scalar_tensor_tensor(m[:, c, :], m[:, c, :], v(name, c), stat[:, 1, :], ALU.mult,
                                                 ALU.mult).then_inc(m_scaled, 1)
                    if c >= 2:
                        low(norm, c - 2, dst)

            def evac(name, n, dst, scale=INV):
                dve.wait_ge(product[name], n + 1)
                dve.tensor_scalar(dst, ps[:, n % RING, 0:T], scale, None, ALU.mult).then_inc(drained[name], 1)

            def add_square(src, c, at, loop=None):
                i, per = loop or (0, 0)
                dve.tensor_tensor(sq[:, c:c + 1, :], src, src, ALU.mult).then_inc(m_squared, 1)
                dve.wait_ge(m_squared, i * per + (at + 1))
                if at:
                    dve.wait_ge(m_added, i * per + at)
                dve.tensor_tensor(stat[:, 3:4, :], stat[:, 3:4, :], sq[:, c:c + 1, :], ALU.add).then_inc(m_added, 1)

            def into_m(name, norm):
                u0 = FIRST[name]
                chain(dve.memset(stat[:, 3, :], 0.0))
                for n in range(DC):
                    if name == "pw2":
                        dve.wait_ge(product[name], n + 1)
                        dve.tensor_scalar(m[:, n, :], ps[:, n % RING, 0:T], INV, v("b_pw2", n), ALU.mult,
                                          ALU.add).then_inc(drained[name], 1)
                    else:
                        evac(name, n, m[:, n, :])
                    dve.wait_ge(drained[name], n + 1)
                    add_square(m[:, n:n + 1, :], n % 2, ADDED_AT[norm] + n)
                    if n % 2 and n < DC // 2:
                        split(2 * u0 + n // 2 + 4)

            def into_h(name, norm):
                u0 = FIRST[name]
                for n in range(DC):
                    dve.wait_ge(product[name], n + 1)
                    dve.scalar_tensor_tensor(h[:, n, :], ps[:, n % RING, 0:T], INV, h[:, n, :], ALU.mult,
                                             ALU.add).then_inc(h_ready[name], 1)
                    if n:
                        low(norm, n - 1, g_in)
                    if n % 2 and n < DC // 2:
                        split(2 * u0 + n // 2 + 4)
                low(norm, DC - 1, g_in)

            def late_tables():
                step(dve.tensor_tensor(tmp[:, 0, :], cos2[:], LATE_SCALE, ALU.mult))
                chain(dve.tensor_tensor(tmp[:, 1, :], sin2[:], LATE_SCALE, ALU.mult))

            def rope(name, i):
                c_tab, s_tab = (k("cos"), k("sin")) if name == "mla" else (tmp[:, 0, :], tmp[:, 1, :])
                b, c = ROPES[name][i]
                at = ROPE_AT[name] + i
                dve.wait_ge(swapped, at + 1)
                t = tmp[:, 2 + at % 2, :]
                step(dve.tensor_tensor(t, ps[:, 4 + at % 2, 0:T], s_tab, ALU.mult))
                chain(dve.tensor_tensor(b[:, c, :], b[:, c, :], c_tab, ALU.mult))
                dve.tensor_tensor(b[:, c, :], b[:, c, :], t, ALU.add).then_inc(turned, 1)

            def quarter(g, q):
                o = HALF * (g % 2) + QUARTER * q
                dve.wait_ge(hi_split, g + 1)
                at = (slice(None), g // 2 % 2, slice(o, o + QUARTER))
                ins = dve.scalar_tensor_tensor(w_lo[at], staged[at], SW, w_hi[at], ALU.mult, ALU.subtract)
                if q == 3:
                    ins.then_inc(lo_split, 1)

            def attention(kind):
                spec, s = KINDS[kind], A[kind]
                H = spec["heads"]
                for i in range(length(kind) + LOW_LAG[kind]):
                    if i < H:
                        b = i % 2
                        dve.wait_ge(s["scores"], i + 1)
                        if i >= 2:
                            dve.wait_ge(s["exp"], i - 1)
                        for t in range(TT):
                            sl = slice(P * t, P * t + P * (t + 1))
                            last = step(dve.tensor_tensor_reduce(scores[:, b, sl], ps[:, 4 + b, sl], spec["mask"](i)[:, sl],
                                                                 spec["scale"], TAKEN, ALU.add, ALU.max,
                                                                 peak[:, b, t:t + 1]))
                        dve.wait_ge(dve_step, last)
                        dve.tensor_scalar(peak[:, b, 2:4], peak[:, b, 0:2], -1.0, None, ALU.mult).then_inc(s["peak"], 1)
                    hd = i - 1
                    if 0 <= hd < H:
                        b = hd % 2
                        dve.wait_ge(s["exp"], hd + 1)
                        if hd >= 2:
                            dve.wait_ge(s["norm"], hd - 1)
                        dve.reciprocal(peak[:, b, 6:8], peak[:, b, 4:6]).then_inc(s["inv"], 1)
                    for c, b, hd in ended(kind, i - LOW_LAG[kind]):
                        dve.wait_ge(s["o_hi"], c + 1)
                        dve.scalar_tensor_tensor(x_lo[:, c, :], ps[:, b, 0:T], SX, x_hi[:, c, :], ALU.mult,
                                                 ALU.subtract).then_inc(s["o_lo"], 1)
                    for g, q in spread(kind, i - 4, i == length(kind) + LOW_LAG[kind] - 1):
                        quarter(g, q)

            def angles():
                turn1 = 6.28125
                turn2 = float((np.array([2 * np.pi - 6.28125], np.float32).view(np.uint32) & np.uint32(0xFFFFF000)).view(
                    np.float32)[0])
                turn3 = float(np.float32(2 * np.pi - 6.28125 - turn2))
                whole = 1.5 * 2.0 ** 23
                dve.wait_ge(late_loaded, 32)
                chain(dve.tensor_copy(sq[:, 0, :], posi[:]))
                chain(dve.tensor_scalar(sq[:, 1, :], sq[:, 0, :], k("freq2"), None, ALU.mult))
                chain(dve.tensor_scalar(sq[:, 2, :], sq[:, 1, :], float(1.0 / (2 * np.pi)), whole, ALU.mult, ALU.add))
                chain(dve.tensor_scalar(sq[:, 3, :], sq[:, 2, :], whole, None, ALU.subtract))
                chain(dve.scalar_tensor_tensor(sq[:, 1, :], sq[:, 3, :], -turn1, sq[:, 1, :], ALU.mult, ALU.add))
                chain(dve.scalar_tensor_tensor(sq[:, 1, :], sq[:, 3, :], -turn2, sq[:, 1, :], ALU.mult, ALU.add))
                chain(dve.scalar_tensor_tensor(sq[:, 1, :], sq[:, 3, :], -turn3, sq[:, 1, :], ALU.mult, ALU.add))
                dve.tensor_scalar(tmp[:, 0, :], sq[:, 1, :], 3.1415925, -3.1415925, ALU.min, ALU.max).then_inc(tables, 1)
                dve.wait_ge(sines, 2)
                step(dve.tensor_scalar(sin2[:], tmp[:, 2, :], k("sign2"), None, ALU.mult))
                chain(dve.tensor_tensor(cos2[:], tmp[:, 3, :], tmp[:, 3, :], ALU.mult))
                chain(dve.tensor_scalar(cos2[:], cos2[:], -2.0, 1.0, ALU.mult, ALU.add))

            dve.memset(pad[:], 0.0)
            dve.memset(logf_rows[:], 0.0)
            chain(dve.memset(decay_k[:], 0.0))
            step(dve.memset(decay_k[32:DECAY, :], 1.0))
            step(dve.memset(u_pad, 0.0))
            dve.wait_ge(loaded, 32)
            at = slice(VCOL[SCALED_GAINS[0]], VCOL[SCALED_GAINS[-1]] + DC)
            dve.tensor_scalar(vec[:, at], vec[:, at], SX, None, ALU.mult).then_inc(gains_scaled, 1)
            invert("mix_pre_0")
            split(0)
            scale("mix_pre_0", h, "mix_pre_0", (x_hi, x_lo))
            for g in range(1, 4):
                split(g)
            share = m[:, 4, :]
            lanes, waiting, behind_tap = [], [*CONV_VECTOR, *SHARED], {}

            def taps(count, chunks):
                for _ in range(count):
                    while len(lanes) < 2 and waiting and waiting[0] < chunks:
                        c = waiting.pop(0)
                        lanes.append([c, TAPS - SHARED[c] if c in SHARED else 0])
                    if not lanes:
                        return
                    c, tap = lanes[0]
                    at = share if c == CONV_POOL[-1] else conv[:, c, :]
                    if c not in behind_tap:
                        dve.wait_ge(glu, c + 1)
                        taken = u_pad[:, c, tap:tap + T]
                        behind_tap[c] = step(
                            dve.tensor_scalar(at, taken, v("taps", DC * tap + c), None, ALU.mult) if at is share else
                            dve.tensor_scalar(at, taken, v("taps", DC * tap + c), v("b_dw", c), ALU.mult, ALU.add))
                    else:
                        dve.wait_ge(dve_step, behind_tap[c])
                        ins = dve.scalar_tensor_tensor(at, u_pad[:, c, tap:tap + T], v("taps", DC * tap + c), at, ALU.mult,
                                                       ALU.add)
                        if tap < TAPS - 1 or c not in CONV_VECTOR:
                            behind_tap[c] = step(ins)
                        else:
                            ins.then_inc(conv_ready, 1)
                    lanes[0][1] += 1
                    if tap == TAPS - 1:
                        lanes.pop(0)
                    else:
                        lanes.append(lanes.pop(0))

            u0 = FIRST["pw1"]
            for j in range(DC):
                dve.wait_ge(drained["pw1"], 2 * j + 2)
                dve.tensor_tensor(u_pad[:, j, TAPS - 1:TAPS - 1 + T], m[:, 2 * (j % 2), :], m[:, 2 * (j % 2) + 1, :],
                                  ALU.mult).then_inc(glu, 1)
                split(2 * u0 + j + 4)
                if j:
                    taps(7, j)
            taps(TAPS * DC, DC)
            dve.wait_ge(dve_step, max(behind_tap.values()))
            dve.wait_ge(diag_used, TENSOR_TAPS)
            c = CONV_TENSOR[-1]
            dve.tensor_tensor(conv[:, c, :], conv[:, c, :], ps[:, 4 + len(CONV_TENSOR) - 1, 0:T], ALU.add).then_inc(
                conv_ready, 1)
            dve.wait_ge(conv_added, POOL_TAPS)
            c = CONV_POOL[-1]
            dve.tensor_tensor(conv[:, c, :], conv[:, c, :], share, ALU.add).then_inc(conv_ready, 1)
            dve.wait_ge(ln_summed, 1)
            dve.wait_ge(conv_ready, len(CONV_VECTOR) + len(SHARED))
            chain(dve.tensor_scalar(stat[:, 0, :], STAT, 1.0 / D, None, ALU.mult))
            for c in range(DC):
                dve.tensor_tensor(conv[:, c, :], conv[:, c, :], stat[:, 0, :], ALU.subtract).then_inc(ln_centred, 1)
            dve.wait_ge(ln_rooted, 1)
            dve.reciprocal(stat[:, 1, :], stat[:, 2, :]).then_inc(ln_inverted, 1)
            dve.wait_ge(ln_inverted, 1)
            dve.wait_ge(ln_centred, DC)
            for c in range(DC + 3):
                if c < DC:
                    dve.tensor_tensor(conv[:, c, :], conv[:, c, :], stat[:, 1, :], ALU.mult).then_inc(ln_scaled, 1)
                if c >= 3:
                    x_lows("layer_norm", c - 3, (x_hi, x_lo))
            into_m("pw2", "mix_post_0")
            invert("mix_post_0")
            dve.wait_ge(gains_scaled, 1)
            post("mix_post_0", "ffn_pre_0", (x_hi, x_lo))

            def mlp(layer):
                one, two = f"ff1_{layer}", f"ff2_{layer}"
                u0 = FIRST[one]
                split(2 * u0 + 2)
                invert(f"ffn_pre_{layer}")
                dve.wait_ge(inverted, NORM_AT[f"ffn_pre_{layer}"] + 1)

                def hidden_low(i, n):
                    f = tmp[:, 2 + n % 2:3 + n % 2, :]
                    dve.wait_ge(f_hi_ready[layer], i * 8 + (n + 1))
                    at = bass.ds(i * 8 + n, 1)
                    dve.scalar_tensor_tensor(f_lo[:, at, :], f, SF, f_hi[:, at, :], ALU.mult, ALU.subtract).then_inc(
                        f_lo_ready[layer], 1)

                def hidden_chunk(i, n):
                    dve.wait_ge(product[one], i * 8 + (n + 1))
                    wait_from(dve, f_hi_ready[layer], i * 8 + (n - 1))
                    dve.scalar_tensor_tensor(tmp[:, n % 2, :], ps[:, n % RING, 0:T], 0.0, LATE_SCALE, ALU.max,
                                             ALU.mult).then_inc(drained[one], 1)
                    if n or not isinstance(i, int):
                        hidden_low(i, n - 1)
                    if n % 2 == 0:
                        g = 2 * u0 + n // 2 + 3
                        lo(g // 2 % 2, g % 2, i * 4 + (g + 1))

                for n in range(8):
                    hidden_chunk(0, n)
                with dve.Fori(1, dict(STREAM)[one] // 2) as i:
                    for n in range(8):
                        hidden_chunk(i, n)
                hidden_low(0, FC - 1)
                split(2 * FIRST[two] + 3)
                if layer == 0:
                    angles()
                u0 = FIRST[two]
                chain(dve.memset(stat[:, 3, :], 0.0))

                def unit(i, s, splits=True):
                    dve.wait_ge(product[two], i * 2 + (s + 1))
                    mc = m[:, bass.ds(i * 2 + s, 1), :]
                    dve.tensor_scalar(mc, ps[:, s:s + 1, 0:T], INVF, None, ALU.mult).then_inc(drained[two], 1)
                    dve.wait_ge(drained[two], i * 2 + (s + 3))
                    add_square(mc, s, ADDED_AT[f"ffn_post_{layer}"] + s, (i, 2))
                    for e in range(2 * splits):
                        g = 2 * (u0 + s) + e + 4
                        lo(g // 2 % 2, e, i * 4 + (g + 1))

                last = dict(STREAM)[two] // 2 - 1
                with dve.Fori(0, last) as i:
                    unit(i, 0)
                    unit(i, 1)
                unit(last, 0)
                unit(last, 1, False)
                invert(f"ffn_post_{layer}")
                post(f"ffn_post_{layer}", *(("mix_pre_1", (f_hi, f_lo)), ("attn_0", (x_hi, x_lo)))[layer])
                split(2 * (u0 + 2 * last + 1) + 4)

            mlp(0)
            invert("mix_pre_1")
            dve.wait_ge(inverted, NORM_AT["mix_pre_1"] + 1)
            u0 = FIRST["kv"]

            def latent(name, n, dst, bank):
                dve.wait_ge(product[name], n + 1)
                dve.tensor_tensor(dst, ps[:, bank, 0:T], LATE_SCALE, ALU.mult).then_inc(drained[name], 1)

            latent("kv", 0, kT[:, 0, :], 0)
            split(2 * u0 + 3)
            latent("kv", 1, kT[:, 1, :], 1)
            split(2 * u0 + 4)
            latent("kv", 2, kT[:, 8, :], 2)
            latent("dq", 0, qT[:, 0, :], 4)
            invert("kv_norm")
            latent("dq", 1, qT[:, 1, :], 5)
            scale("kv_norm", kT, "kv_norm", (f_hi[:, 8:10], f_lo[:, 8:10]))
            latent("dq", 2, qT[:, 2, :], 6)
            split(2 * u0 + 5)
            split(2 * FIRST["dq"] + 4)
            invert("q_norm")
            scale("q_norm", qT, "q_norm", (f_hi[:, 10:13], f_lo[:, 10:13]))
            rope("mla", 0)
            split(2 * FIRST["dq"] + 5)
            for e in range(2):
                split(2 * FIRST["ukv"] + 4 + e)
            for i in range(1, 5):
                rope("mla", i)
            u0 = FIRST["uq"]
            split(2 * u0 + 4)
            attention("mla")
            split(2 * FIRST["wo"] + 3)
            into_m("wo", "mix_post_1")
            invert("mix_post_1")
            post("mix_post_1", "ffn_pre_1", (x_hi, x_lo))
            mlp(1)

            invert("attn_0")
            dve.wait_ge(inverted, NORM_AT["attn_0"] + 1)
            late_tables()
            u0 = FIRST["even"]
            split(2 * u0 + 3)
            rope("even", 0)
            split(2 * u0 + 4)
            rope("even", 1)
            split(2 * u0 + 5)
            rope("even", 2)
            dve.wait_ge(drained["even"], 7)
            gate = gates[:, :, 0:HEADS]
            bias = v("b_fox", 0, HEADS)
            z = logf[:, 0, :].rearrange("p (t h) -> p t h", t=TT)
            for t in range(TT):
                last = step(dve.tensor_tensor(z[:, t, :], gate[:, t, :], bias, ALU.add))
            dve.wait_ge(dve_step, last)
            dve.scalar_tensor_tensor(logf[:, 1, :], logf[:, 0, :], -1.0, logf[:, 0, :], ALU.mult, ALU.max).then_inc(
                forget_sum, 1)
            rope("even", 3)
            split(2 * u0 + 6)
            split(2 * u0 + 7)
            invert("g_ckv")
            dve.wait_ge(inverted, NORM_AT["g_ckv"] + 1)
            dve.scalar_tensor_tensor(kT[:, 5, :], kT[:, 4, :], v("g_ckv"), stat[:, 1, :], ALU.mult, ALU.mult).then_inc(
                scaled, 1)
            dve.wait_ge(forget_parts, 1)
            dve.tensor_scalar(logf[:, 3, :], logf[:, 2, :], 1.0, None, ALU.add).then_inc(forget_sum, 1)
            dve.wait_ge(forget_sum, 2)
            chain(dve.tensor_scalar(logf[:, 4, :], logf[:, 3, :], 1.0, None, ALU.subtract))
            chain(dve.tensor_tensor(logf[:, 2, :], logf[:, 2, :], logf[:, 4, :], ALU.subtract))
            dve.wait_ge(forget_parts, 2)
            chain(dve.reciprocal(logf[:, 4, :], logf[:, 3, :]))
            chain(dve.tensor_tensor(logf[:, 2, :], logf[:, 2, :], logf[:, 4, :], ALU.mult))
            chain(dve.tensor_tensor(logf[:, 2, :], logf[:, 2, :], logf[:, 1, :], ALU.add))
            lost = logf[:, 2, :].rearrange("p (t h) -> p t h", t=TT)
            chain(dve.scalar_tensor_tensor(logf_rows[:, :, 32:DECAY], z, 0.0, lost, ALU.min, ALU.subtract))
            dve.tensor_scalar(logf_rows[:, :, 0:HEADS], logf_rows[:, :, 32:DECAY], -1.0, None, ALU.mult).then_inc(
                fox_logf, 1)
            split(2 * u0 + 8)
            for i in range(IDX_HEADS):
                dve.wait_ge(dots_relu, i + 1)
                if i:
                    dve.wait_ge(dots_added, i)
                for t in range(TT):
                    sl = slice(P * t, P * t + P * (t + 1))
                    w = gates[:, t, HEADS + i:HEADS + i + 1]
                    if i == 0:
                        last = dve.tensor_scalar(idx[:, 0, sl], scores[:, i % 2, sl], w, None, ALU.mult)
                    else:
                        last = dve.scalar_tensor_tensor(idx[:, 0, sl], scores[:, i % 2, sl], w, idx[:, 0, sl], ALU.mult,
                                                        ALU.add)
                last.then_inc(dots_added, 1)
            dve.wait_ge(dots_added, IDX_HEADS)
            chain(dve.tensor_tensor(idx[:, 0, :], idx[:, 0, :], k("causal"), ALU.add))
            split(2 * u0 + 9)
            dve.wait_ge(fox_cum, 1)
            dve.wait_ge(decay_rows, 1)
            step(dve.tensor_copy(decay_k[0:HEADS, :], ps[0:HEADS, 6, 0:T]))
            dve.tensor_tensor(decay_q[32:DECAY, :, :], ps[32:DECAY, 6:7, 0:T].to_broadcast([HEADS, HEADS, T]),
                              cst[32:DECAY, CCOL["pick"]:CCOL["pick"] + HEADS].unsqueeze(2).to_broadcast([HEADS, HEADS, T]),
                              ALU.mult).then_inc(fox_cum_ready, 1)
            rope("even", 4)
            rope("even", 5)
            split(2 * u0 + 10)
            rope("even", 6)
            rope("even", 7)
            for n in range(TOPK // 8):
                a, b = idx[:, n % 2, :], idx[:, (n + 1) % 2, :]
                for t in range(TT):
                    sl = slice(P * t, P * t + P * (t + 1))
                    last = step(dve.max(top8[:, t, :], a[:, sl]))
                dve.wait_ge(dve_step, last)
                for t in range(TT):
                    sl = slice(P * t, P * t + P * (t + 1))
                    last = step(dve.match_replace(b[:, sl], top8[:, t, :], a[:, sl], TAKEN))
                dve.wait_ge(dve_step, last)
                if n == 1:
                    split(2 * u0 + 11)
            chain(dve.tensor_scalar(sel[:], idx[:, TOPK // 8 % 2, :], TAKEN / 2, MASKED, ALU.is_gt, ALU.mult))
            chain(dve.tensor_tensor(sel[:], sel[:], k("causal"), ALU.add))
            attention("even")
            into_h("oute", "ffn2_0")

            def glu_mlp(layer):
                up, down = f"up_{layer}", f"down_{layer}"
                split(2 * FIRST[("oute", "outo")[layer]] + 6)
                invert(f"ffn2_{layer}")
                split(2 * FIRST[("oute", "outo")[layer]] + 7)
                dve.wait_ge(inverted, NORM_AT[f"ffn2_{layer}"] + 1)
                u0, units = FIRST[up], dict(STREAM)[up]

                def pair(i, n, parts=(True, True)):
                    old, new = parts
                    j = n % 2
                    y = tmp[:, j, :]
                    if new:
                        dve.wait_ge(product[up], i * 4 + (n + 1))
                        dve.tensor_tensor(pad[:, j, TAPS2 - 1:TAPS2 - 1 + T], ps[:, j, 0:T], LATE_SCALE, ALU.mult).then_inc(
                            drained[up], 1)
                    if old:
                        dve.wait_ge(p_hi_ready[layer], i * 4 + n)
                        at = bass.ds(i * 4 + (n - 1), 1)
                        dve.scalar_tensor_tensor(f_lo[:, at, :], tmp[:, 3 - j:4 - j, :], SF, f_hi[:, at, :], ALU.mult,
                                                 ALU.subtract).then_inc(p_lo_ready[layer], 1)
                    if new:
                        taps = [vec[:, bass.ds(i * 4 + (VCOL[f"taps2_{layer}"] + GC * q + n), 1)] for q in range(TAPS2)]
                        dve.wait_ge(g_first[layer], i * 4 + (n + 1))
                        dve.wait_ge(drained[up], i * 4 + (n + 1))
                        dve.scalar_tensor_tensor(y, pad[:, j, 1:1 + T], taps[1], y, ALU.mult, ALU.add).then_inc(
                            g_conv[layer], 1)
                        dve.wait_ge(g_conv[layer], i * 8 + (2 * n + 1))
                        dve.scalar_tensor_tensor(y, pad[:, j, 2:2 + T], taps[2], y, ALU.mult, ALU.add).then_inc(
                            g_conv[layer], 1)
                    if old:
                        g = 2 * u0 + n + 3
                        lo(g // 2 % 2, g % 2, i * 4 + (g + 1))
                    if new:
                        dve.wait_ge(u_product[layer], i * 4 + (n + 1))
                        dve.wait_ge(g_normed[layer], i * 4 + (n + 1))
                        dve.scalar_tensor_tensor(tmp[:, 2 + j, :], ps[:, 2 + j, 0:T], 1.0, y, ALU.mult,
                                                 ALU.mult).then_inc(u_drained[layer], 1)

                pair(0, 0, (False, True))
                pair(0, 1)
                with dve.Fori(0, (GC - 2) // 4) as i:
                    for n in range(2, 6):
                        pair(i, n)
                pair(0, GC, (True, False))
                u0, units = FIRST[down], dict(STREAM)[down]
                if layer:
                    chain(dve.memset(stat[:, 3, :], 0.0))

                def unit(i, s, splits=True):
                    dve.wait_ge(product[down], i * 2 + (s + 1))
                    hc = h[:, bass.ds(i * 2 + s, 1), :]
                    dve.scalar_tensor_tensor(hc, ps[:, s:s + 1, 0:T], INVF, hc, ALU.mult, ALU.add).then_inc(
                        h_ready[down], 1)
                    if layer:
                        dve.wait_ge(h_ready[down], i * 2 + (s + 3))
                        add_square(hc, s, ADDED_AT["final"] + s, (i, 2))
                    for e in range(2 * splits):
                        g = 2 * (u0 + s) + e + 4
                        lo(g // 2 % 2, e, i * 4 + (g + 1))
                    if not layer:
                        at = bass.ds(i * 2 + s, 1)
                        dve.wait_ge(x_hi_ready, i * 2 + (SPLIT_AT["attn_1"] + s + 1))
                        dve.scalar_tensor_tensor(x_lo[:, at, :], hc, vec[:, bass.ds(i * 2 + (VCOL["attn_1"] + s), 1)],
                                                 x_hi[:, at, :], ALU.mult, ALU.subtract).then_inc(x_lo_ready, 1)

                with dve.Fori(0, units // 2 - 1) as i:
                    unit(i, 0)
                    unit(i, 1)
                unit(units // 2 - 1, 0, layer == 0)
                unit(units // 2 - 1, 1, False)

            glu_mlp(0)
            split(2 * FIRST["odd"] + 2)
            invert("attn_1")
            dve.wait_ge(inverted, NORM_AT["attn_1"] + 1)
            late_tables()
            split(2 * FIRST["odd"] + 3)
            for n in range(DC * 2 + 2):
                if n % 2:
                    split(2 * FIRST["odd"] + n // 2 + 4)
                if n >= 2:
                    rope("odd", n - 2)
            attention("moba")
            into_h("outo", "ffn2_1")
            glu_mlp(1)
            invert("final")
            dve.wait_ge(inverted, NORM_AT["final"] + 1)
            for c in range(DC):
                dve.scalar_tensor_tensor(xn[:, c, :], h[:, c, :], v("final", c), stat[:, 1, :], ALU.mult,
                                         ALU.mult).then_inc(out_written, 1)


def columns(w):
    r, n = w.shape
    return list(np.ascontiguousarray(w.reshape(r // P, P, n // P, P).transpose(2, 1, 0, 3)).reshape(n // P, P, r))


def whole(w):
    r, n = w.shape
    return np.ascontiguousarray(w.reshape(r // P, P, n).transpose(1, 0, 2)).reshape(P, r // P * n)


def stream_of(a):
    out = np.zeros((UNITS, P, UNIT), np.float32)

    def put(name, unit, at, blocks):
        for b in blocks:
            out[FIRST[name] + unit, :, at:at + b.shape[1]] = b
            at += b.shape[1]

    def fill(name, chunks, per_unit, first=0):
        for u in range(0, len(chunks), per_unit):
            put(name, first + u // per_unit, 0, chunks[u:u + per_unit])

    def woven(w):
        c = columns(w)
        n = len(c) // 2
        return c[:n], c[n:]

    first, gate = woven(a["conv_w_pw1"][0])
    fill("pw1", [x for g, y in zip(gate, first) for x in (g, y)], 4)
    fill("pw2", columns(a["conv_w_pw2"][0]), 4)
    for layer in range(2):
        fill(f"ff1_{layer}", columns(a["w_ff1"][layer]), 4)
        fill(f"ff2_{layer}", columns(a["w_ff2"][layer]), 1)
    kr = a["kv_w_kr"]
    put("kv", 0, 0, columns(np.concatenate([a["kv_w_dkv"], kr, kr], axis=1)))
    put("dq", 0, 0, columns(a["mla_w_dq"][0]))
    put("ukv", 0, 0, columns(a["kv_w_uk"]))
    put("ukv", 0, HALF, [whole(a["kv_w_uv"])])
    uq = a["mla_w_uq"][0].reshape(Q_RANK, HEADS, NOPE + ROPE)
    uq = columns(np.concatenate([uq[:, :, NOPE:].reshape(Q_RANK, -1), uq[:, :, :NOPE].reshape(Q_RANK, -1)], axis=1))
    put("uq", 0, 0, uq[0:5])
    put("uq", 0, HALF, uq[5:10])
    put("uq", 1, 0, uq[10:12])
    fill("wo", columns(a["mla_w_o"][0]), 4)
    w = a["w_in_even_2"][0]
    wide = HEADS * HD
    fq, fk, fv = (w[:, wide * i:wide * i + wide] for i in range(3))
    ff, w = w[:, 3 * wide:3 * wide + HEADS], w[:, 3 * wide + HEADS:]
    dq, ckv, dkr, iq, ik, iw = np.split(w, np.cumsum([wide, P, ROPE2, IDX_HEADS * HD, HD]), axis=1)
    none = np.zeros((D, HD - ROPE2), np.float32)
    put("even", 0, 0, columns(np.concatenate([iq, ik, ik, ckv], axis=1)))
    put("even", 1, 0, columns(np.concatenate([dkr, none, dkr, none], axis=1)))
    put("even", 1, D, [whole(np.concatenate([ff, iw], axis=1))])
    put("even", 2, 0, columns(dq))
    put("even", 3, 0, columns(fk))
    put("even", 4, 0, [whole(fv)])
    put("even", 5, 0, columns(fq))
    fill("oute", columns(a["w_out_even_2"][0]), 4)
    for layer in range(2):
        g, u = woven(a["w_up_2"][layer])
        fill(f"up_{layer}", [x for pair in zip(g, u) for x in pair], 4)
        fill(f"down_{layer}", columns(a["w_down_2"][layer]), 1)
    w = a["w_in_odd_2"][0]
    fill("odd", columns(w[:, :2 * D]), 4)
    for half in range(2):
        put("odd", 4 + half, 0, [whole(w[:, 2 * D + 512 * half:2 * D + 512 * half + 512])])
    fill("outo", columns(a["w_out_odd_2"][0]), 4)
    return out


def vectors_of(a):
    out = np.zeros((P, VCOLS), np.float32)

    def put(name, value):
        x = np.asarray(value, np.float32).reshape(-1, P).T
        out[:, VCOL[name]:VCOL[name] + x.shape[1]] = x

    for layer in range(2):
        for name in ("mix_pre", "mix_post", "ffn_pre", "ffn_post"):
            put(f"{name}_{layer}", a[f"{name}_g"][layer])
        put(f"attn_{layer}", a["attn_norm_2"][layer])
        put(f"ffn2_{layer}", a["ffn_norm_2"][layer])
        put(f"taps2_{layer}", a["conv_w_2"][layer])
        put(f"b_cv_{layer}", a["conv_b_2"][layer])
    for name, value in (("b_pw1", a["conv_b_pw1"]), ("taps", a["conv_w_dw"]), ("b_dw", a["conv_b_dw"]),
                        ("ln_g", a["conv_ln_g"]), ("ln_b", a["conv_ln_b"]), ("b_pw2", a["conv_b_pw2"]),
                        ("q_norm", a["mla_q_norm_g"]), ("kv_in", a["kv_in_g"]), ("kv_norm", a["kv_norm_g"]),
                        ("final", a["final_norm_2"]), ("g_ckv", a["g_ckv_2"])):
        put(name, value)
    out[:, VCOL["b_fox"]:VCOL["b_fox"] + HEADS] = a["b_fox_f_2"][0]
    uk = np.zeros((HEADS, HD, P), np.float32)
    uk[:, ROPE2:, :] = a["w_uk_2"][0].transpose(1, 2, 0)
    out[:, VCOL["w_uk2"]:VCOL["w_uk2"] + 4 * P] = uk.reshape(4, P, P).transpose(1, 0, 2).reshape(P, 4 * P)
    out[:, VCOL["w_uv2"]:VCOL["w_uv2"] + HEADS * HD] = a["w_uv_2"][0].reshape(P, HEADS * HD)
    return out


def kernel(**inputs):
    import concourse.bacc as bacc
    from concourse.bass_utils import run_bass_kernel_spmd

    a = {name: np.asarray(value) for name, value in inputs.items()}
    arrays = {
        "weights": stream_of(a),
        "vectors": vectors_of(a),
        "constants": constants(),
        "x_turned": np.ascontiguousarray(a["x"][0].T.reshape(DC, P, T).transpose(1, 0, 2)),
        "positions": np.ascontiguousarray(np.broadcast_to(a["positions_2"].reshape(1, T), (P, T))),
    }
    nc = bacc.Bacc("TRN2", target_bir_lowering=False, num_devices=1)
    args = [nc.dram_tensor(n, x.shape, mybir.dt.from_np(x.dtype), kind="ExternalInput").ap() for n, x in arrays.items()]
    args.append(nc.dram_tensor("out", (P, DC, T), F32, kind="ExternalOutput").ap())
    conformer_mla_fox_dsa_moba_kernel(nc, *args)
    got = run_bass_kernel_spmd(nc, [arrays], core_ids=[0]).results[0]["out"]
    return np.ascontiguousarray(got.transpose(1, 0, 2).reshape(D, T).T)[None]
```
